# Optimizing a Trainium2 kernel written in Bass

```python
import math
import jax, jax.numpy as jnp
from jax import lax
import numpy as np

D_MODEL = 2048
BATCH = 1
SEQ = 256
DEPTH = 1

CHUNK = 64
Q_BLOCK = 128
HEAD_DIM = 128
SB_HEADS = 8
DN_HEADS = 8
SB_WIDTH = SB_HEADS * HEAD_DIM
DN_WIDTH = DN_HEADS * HEAD_DIM
MIX_WIDTH = SB_WIDTH + DN_WIDTH
SHORT_CONV = 4
FFN_CONV = 3
D_FF = 5632
IN_COLS = 3 * SB_WIDTH + 4 * DN_WIDTH + 2 * DN_HEADS
EPS = 1e-6

kernel_name = "sb_gdn_hybrid_convffn_block"

def rmsnorm(x, gain):
    xf = x.astype(jnp.float32)
    y = xf * lax.rsqrt(jnp.mean(xf * xf, axis=-1, keepdims=True) + EPS)
    return (y * gain.astype(jnp.float32)).astype(x.dtype)

def l2norm(x):
    xf = x.astype(jnp.float32)
    return xf * lax.rsqrt(jnp.sum(xf * xf, axis=-1, keepdims=True) + EPS)

def causal_dwconv(x, w):
    K = w.shape[0]
    T = x.shape[1]
    xp = jnp.pad(x, ((0, 0), (K - 1, 0), (0, 0)))
    out = xp[:, 0:T] * w[0]
    for j in range(1, K):
        out = out + xp[:, j:j + T] * w[j]
    return out

def _heads(t, n):
    B, T, _ = t.shape
    return t.reshape(B, T, n, HEAD_DIM).transpose(0, 2, 1, 3)

def stick_breaking_attention(q, k, v):
    B, H, T, Dh = q.shape
    scale = Dh ** -0.5
    outs = []
    for blk in range(T // Q_BLOCK):
        q0 = blk * Q_BLOCK
        kend = q0 + Q_BLOCK
        z = jnp.einsum('bhqd,bhkd->bhqk', q[:, :, q0:kend], k[:, :, :kend]).astype(jnp.float32) * scale
        t_idx = q0 + jnp.arange(Q_BLOCK)[:, None]
        s_idx = jnp.arange(kend)[None, :]
        valid = s_idx < t_idx
        log_beta = jax.nn.log_sigmoid(z)
        log_1m = jnp.where(valid, jax.nn.log_sigmoid(-z), 0.0)
        later = lax.cumsum(log_1m, axis=3, reverse=True) - log_1m
        att = jnp.where(valid, jnp.exp(log_beta + later), 0.0)
        outs.append(jnp.einsum('bhqk,bhkd->bhqd', att.astype(v.dtype), v[:, :, :kend]))
    return jnp.concatenate(outs, axis=2)

def gated_delta_rule(q, k, v, g, beta):
    out_dtype = v.dtype
    B, H, T, Dk = q.shape
    Dv = v.shape[-1]
    C = CHUNK
    N = T // C
    q = q.astype(jnp.float32) * (Dk ** -0.5)
    k = k.astype(jnp.float32)
    v = v.astype(jnp.float32)
    beta = beta.astype(jnp.float32)
    q = q.reshape(B, H, N, C, Dk)
    k = k.reshape(B, H, N, C, Dk)
    v = v.reshape(B, H, N, C, Dv)
    beta = beta.reshape(B, H, N, C)
    g = jnp.cumsum(g.astype(jnp.float32).reshape(B, H, N, C), axis=-1)

    causal = jnp.tril(jnp.ones((C, C), dtype=bool))
    strict = jnp.tril(jnp.ones((C, C), dtype=bool), k=-1)
    diff = g[..., :, None] - g[..., None, :]
    decay = jnp.where(causal, jnp.exp(jnp.where(causal, diff, 0.0)), 0.0)

    k_beta = k * beta[..., None]
    v_beta = v * beta[..., None]
    L = jnp.where(strict, jnp.einsum('bhncd,bhnmd->bhncm', k_beta, k) * decay, 0.0)
    eye = jnp.eye(C, dtype=jnp.float32)
    T_mat = lax.linalg.triangular_solve(eye + L, jnp.broadcast_to(eye, L.shape),
                                        left_side=True, lower=True, unit_diagonal=True)
    u = jnp.einsum('bhncm,bhnmd->bhncd', T_mat, v_beta)
    w = jnp.einsum('bhncm,bhnmd->bhncd', T_mat, k_beta * jnp.exp(g)[..., None])
    qk_intra = jnp.where(causal, jnp.einsum('bhncd,bhnmd->bhncm', q, k) * decay, 0.0)
    g_last = g[..., -1]
    k_to_end = k * jnp.exp(g_last[..., None] - g)[..., None]
    q_decay = q * jnp.exp(g)[..., None]

    def step(S, xs):
        u_i, w_i, qa_i, qd_i, kt_i, gl_i = xs
        v_new = u_i - jnp.einsum('bhcd,bhde->bhce', w_i, S)
        o = jnp.einsum('bhcd,bhde->bhce', qd_i, S) + jnp.einsum('bhcm,bhme->bhce', qa_i, v_new)
        S = S * jnp.exp(gl_i)[..., None, None] + jnp.einsum('bhcd,bhce->bhde', kt_i, v_new)
        return S, o

    to_scan = lambda t: jnp.moveaxis(t, 2, 0)
    xs = (to_scan(u), to_scan(w), to_scan(qk_intra), to_scan(q_decay), to_scan(k_to_end),
          jnp.moveaxis(g_last, 2, 0))
    S0 = jnp.zeros((B, H, Dk, Dv), dtype=jnp.float32)
    _, o = lax.scan(step, S0, xs)
    o = jnp.moveaxis(o, 0, 2).reshape(B, H, T, Dv)
    return o.astype(out_dtype)

def token_mixer(xn, w_in, sb_out_gain, dn_conv_w, dn_a_log, dn_dt_bias, dn_out_gain, w_out):
    B, T, _ = xn.shape
    proj = jnp.einsum('btd,dc->btc', xn, w_in)
    sizes = (SB_WIDTH, SB_WIDTH, SB_WIDTH, 3 * DN_WIDTH, DN_WIDTH, DN_HEADS, DN_HEADS)
    offs = np.cumsum(sizes)[:-1].tolist()
    sb_q, sb_k, sb_v, dn_qkv, dn_z, dn_b, dn_a = jnp.split(proj, offs, axis=-1)

    o_sb = stick_breaking_attention(_heads(sb_q, SB_HEADS), _heads(sb_k, SB_HEADS), _heads(sb_v, SB_HEADS))
    o_sb = rmsnorm(o_sb.transpose(0, 2, 1, 3), sb_out_gain).reshape(B, T, SB_WIDTH)

    dn_qkv = jax.nn.silu(causal_dwconv(dn_qkv, dn_conv_w))
    dq, dk, dv = jnp.split(dn_qkv, 3, axis=-1)
    q = l2norm(_heads(dq, DN_HEADS))
    k = l2norm(_heads(dk, DN_HEADS))
    v = _heads(dv, DN_HEADS)
    beta = jax.nn.sigmoid(dn_b.astype(jnp.float32)).transpose(0, 2, 1)
    g = -(jnp.exp(dn_a_log.astype(jnp.float32)) *
          jax.nn.softplus(dn_a.astype(jnp.float32) + dn_dt_bias.astype(jnp.float32))).transpose(0, 2, 1)
    o_dn = gated_delta_rule(q, k, v, g, beta).transpose(0, 2, 1, 3)
    o_dn = rmsnorm(o_dn, dn_out_gain) * jax.nn.silu(dn_z.reshape(B, T, DN_HEADS, HEAD_DIM))
    o_dn = o_dn.reshape(B, T, DN_WIDTH).astype(xn.dtype)

    mix = jnp.concatenate([o_sb.astype(xn.dtype), o_dn], axis=-1)
    return jnp.einsum('btc,cd->btd', mix, w_out)

def conv_ffn(xn, w_up, ffn_conv_w, ffn_conv_b, w_down):
    h = jnp.einsum('btd,df->btf', xn, w_up)
    h = causal_dwconv(h, ffn_conv_w) + ffn_conv_b
    gate, val = jnp.split(h, 2, axis=-1)
    return jnp.einsum('btf,fd->btd', jax.nn.gelu(gate, approximate=True) * val, w_down)

def setup_inputs(seed: int = 0) -> dict:
    key = jax.random.key(seed)
    ks = jax.random.split(key, 20)
    f32 = jnp.float32
    nrm = lambda k, shape, s: jax.random.normal(k, shape, f32) * s
    gain = lambda k, shape: 1.0 + 0.05 * jax.random.normal(k, shape, f32)
    dt = jnp.exp(jax.random.uniform(ks[5], (DEPTH, DN_HEADS), f32, math.log(1e-3), math.log(1e-1)))
    return {
        "x": jax.random.normal(ks[0], (BATCH, SEQ, D_MODEL), f32),
        "w_in": nrm(ks[1], (DEPTH, D_MODEL, IN_COLS), D_MODEL ** -0.5),
        "sb_out_gain": gain(ks[2], (DEPTH, HEAD_DIM)),
        "dn_conv_w": nrm(ks[3], (DEPTH, SHORT_CONV, 3 * DN_WIDTH), SHORT_CONV ** -0.5),
        "dn_a_log": jnp.log(jax.random.uniform(ks[4], (DEPTH, DN_HEADS), f32, 1.0, 16.0)),
        "dn_dt_bias": dt + jnp.log(-jnp.expm1(-dt)),
        "dn_out_gain": gain(ks[6], (DEPTH, HEAD_DIM)),
        "w_out": nrm(ks[7], (DEPTH, MIX_WIDTH, D_MODEL), MIX_WIDTH ** -0.5),
        "ln_mix_pre": gain(ks[8], (DEPTH, D_MODEL)),
        "ln_mix_post": gain(ks[9], (DEPTH, D_MODEL)),
        "w_up": nrm(ks[10], (DEPTH, D_MODEL, 2 * D_FF), D_MODEL ** -0.5),
        "ffn_conv_w": nrm(ks[11], (DEPTH, FFN_CONV, 2 * D_FF), FFN_CONV ** -0.5),
        "ffn_conv_b": nrm(ks[12], (DEPTH, 2 * D_FF), 0.01),
        "w_down": nrm(ks[13], (DEPTH, D_FF, D_MODEL), D_FF ** -0.5),
        "ln_ffn_pre": gain(ks[14], (DEPTH, D_MODEL)),
        "ln_ffn_post": gain(ks[15], (DEPTH, D_MODEL)),
    }

def reference(x, w_in, sb_out_gain, dn_conv_w, dn_a_log, dn_dt_bias, dn_out_gain, w_out,
              ln_mix_pre, ln_mix_post, w_up, ffn_conv_w, ffn_conv_b, w_down, ln_ffn_pre, ln_ffn_post):
    h = x
    for l in range(DEPTH):
        m = token_mixer(rmsnorm(h, ln_mix_pre[l]), w_in[l], sb_out_gain[l], dn_conv_w[l],
                        dn_a_log[l], dn_dt_bias[l], dn_out_gain[l], w_out[l])
        h = h + rmsnorm(m, ln_mix_post[l])
        f = conv_ffn(rmsnorm(h, ln_ffn_pre[l]), w_up[l], ffn_conv_w[l], ffn_conv_b[l], w_down[l])
        h = h + rmsnorm(f, ln_ffn_post[l])
    return h


_drawn_inputs = setup_inputs


def setup_inputs(seed=0):
    import zlib

    import numpy as np

    out = dict(_drawn_inputs(seed))
    spreads = {}
    factors = {'dn_out_gain': 2.669, 'ffn_conv_b': 7.09}
    for name, (base, spread) in spreads.items():
        noise = np.random.default_rng([zlib.crc32(name.encode()), seed]).standard_normal(out[name].shape)
        drawn = base * np.exp(spread * noise) if base else spread * noise
        out[name] = __import__('jax').numpy.asarray(drawn.astype(out[name].dtype))
    for name, factor in factors.items():
        out[name] = (out[name] * factor).astype(out[name].dtype)
    return out
```

```python
from contextlib import ExitStack

import numpy as np
import concourse.bass as bass
from concourse import mybir

P = 128
T = 256
D = 2048
KT = D // P
DFF = 5632
FT = DFF // P
HEADS = 8
NJ = T // P
EPS = 1e-6
QSCALE = float(P) ** -0.5
GROUP = 4
CHUNK_K = 4
CHUNK = 2048
RAW = 4
DN_GROUPS = 6
IN_GROUPS = 14
OUT_GROUPS = 4
UP_STEPS = FT // GROUP
IN_CHUNKS = IN_GROUPS * 4
OUT_CHUNKS = OUT_GROUPS * 4
UP_CHUNKS = UP_STEPS * 8
DOWN_K = 2
DOWN_TILES = 8
HALF_CHUNKS = FT // DOWN_K
DOWN_CHUNKS = 2 * HALF_CHUNKS
CHUNKS = IN_CHUNKS + OUT_CHUNKS + UP_CHUNKS + DOWN_CHUNKS
LEVELS = 7
UNITS = HEADS * NJ


def hybrid_block_kernel(nc, x, wts, w_ba, norm_gains, head_gains, dn_conv, dn_gate, ffn_cw, ffn_cb, out):
    f32 = mybir.dt.float32
    f32r = mybir.dt.float32r
    ALU = mybir.AluOpType
    ACT = mybir.ActivationFunctionType
    ctx = ExitStack()
    with ctx:
        def sb(name, shape, dt=f32):
            return ctx.enter_context(nc.sbuf_tensor(name, shape, dt))

        def sem(name):
            return ctx.enter_context(nc.semaphore(name))

        res = sb("residual", [P, KT, T])
        raw = sb("raw", [P, RAW, CHUNK])
        w_hi = sb("w_hi", [P, 2, CHUNK], f32r)
        w_lo = sb("w_lo", [P, 2, CHUNK], f32r)
        half = sb("half", [P, 2, T])
        ident = sb("ident", [P, P])
        ones = sb("ones", [P, P])
        gains = sb("gains", [P, 4, KT])
        hgains = sb("hgains", [P, 2])
        dcw = sb("dcw", [P, 4, 24])
        fcw = sb("fcw", [P, 3, 2 * FT])
        fcb = sb("fcb", [P, 2 * FT])
        rstd = sb("rstd", [P, T])
        vrow = sb("vrow", [P, T])
        gate_mark = sb("gate_mark", [P, 8])
        gate, mark = gate_mark[0:8, 0:4], gate_mark[:, 4:8]
        cols = sb("cols", [P, 6, HEADS])
        ssum = sb("ssum", [P, T])
        halfs = [half[:, 0, :], half[:, 1, :], rstd[:, :], vrow[:, :]]
        base = (nc.sbuf_base + 63) // 64 * 64
        xhl = nc.alloc_sbuf_tensor_at("xhl", [P, KT, 2, T], f32r, offset=base)
        down = nc.alloc_sbuf_tensor_at("down", [P, KT, T], f32, offset=base)
        dsq = nc.alloc_sbuf_tensor_at("dsq", [P, 2, T], f32, offset=base + KT * T * 4)
        base += KT * 2 * T * 4
        room = (nc.sbuf_usable_end - base) // 4
        arena = nc.alloc_sbuf_tensor_at("arena", [P, room], f32, offset=base)
        act = nc.alloc_sbuf_tensor_at("ffn_act", [P, FT, 2, T], f32r, offset=base)
        used = [0]

        def cut(n):
            a = used[0]
            used[0] += n
            assert used[0] <= room, (used[0], room)
            return arena[:, a:a + n]

        proj = cut(56 * T).rearrange("p (n t) -> p n t", t=T)
        tmat = cut(UNITS * P).rearrange("p (u n) -> p u n", n=P)
        tmatT = cut(UNITS * P).rearrange("p (u n) -> p u n", n=P)
        ltri = cut(UNITS * P).rearrange("p (u n) -> p u n", n=P)
        qa = cut(UNITS * P).rearrange("p (u n) -> p u n", n=P)
        kb = cut(2 * T).rearrange("p (b t) -> p b t", t=T)
        dm = cut(2 * T).rearrange("p (b t) -> p b t", t=T)
        lmask = cut(LEVELS * P).rearrange("p (l n) -> p l n", n=P)
        xb = cut(2 * 4 * P).rearrange("p (b u n) -> p b u n", b=2, n=P)
        bb = cut(2 * 4 * P).rearrange("p (b u n) -> p b u n", b=2, n=P)
        a0 = 56 * T
        full = arena[:, a0:a0 + KT * T].rearrange("p (k t) -> p k t", t=T)
        squ = arena[:, a0:a0 + KT * T].rearrange("p (k t) -> p k t", t=T)
        x0 = 56 * T + 4 * UNITS * P + 4 * T + LEVELS * P
        rows = arena[0:8, x0:x0 + 4 * T].rearrange("p (r t) -> p r t", t=T)
        sel = arena[0:8, x0 + 4 * T:x0 + 8 * T].rearrange("p (h m) -> p h m", m=P)
        c0 = a0 + KT * T
        hist = arena[:, c0:c0 + 2 * (T + 3)].rearrange("p (b t) -> p b t", b=2)
        conv = arena[:, c0 + 1024:c0 + 1024 + 2 * T].rearrange("p (b t) -> p b t", b=2)
        mixo = arena[:, 0:KT * T].rearrange("p (n t) -> p n t", t=T)
        f0 = FT * 2 * T
        fhist = arena[:, f0:f0 + 4 * (T + 2)].rearrange("p (b t) -> p b t", b=4)
        f1 = f0 + 4 * (T + 2)
        fconv = arena[:, f1:f1 + 4 * T].rearrange("p (b t) -> p b t", b=4)
        gelu = arena[:, f1 + 4 * T:f1 + 8 * T].rearrange("p (b t) -> p b t", b=4)
        prod = arena[:, f1 + 8 * T:f1 + 10 * T].rearrange("p (b t) -> p b t", b=2)
        assert f1 + 10 * T <= room, (f1 + 10 * T, room)
        wba = arena[:, c0 + 2048:c0 + 2048 + 256].rearrange("p (k n) -> p k n", n=16)
        small = arena[0:8, c0 + 2304:c0 + 2304 + 6 * T].rearrange("p (r t) -> p r t", t=T)

        ps = [ctx.enter_context(nc.psum_tensor(f"bank{i}", [P, 512], f32)) for i in range(8)]

        raw_full = [sem(f"raw_full{i}") for i in range(RAW)]
        hi_ready = sem("hi_ready")
        lo_ready = sem("lo_ready")
        chunk_used = sem("chunk_used")
        bank_full = sem("bank_full")
        half_ready = sem("half_ready")
        bank_free = sem("bank_free")
        small_in = sem("small_in")
        x_in = sem("x_in")
        const_ready = sem("const_ready")
        out_done = sem("out_done")
        T_ = dict()

        def s(name):
            if name not in T_:
                T_[name] = sem(name)
            return T_[name]

        sums = [0]

        def square_sum(pool, step, src, k, buf, slot):
            if k == 0:
                if sums[0]:
                    pool.wait_ge(s("ss_mm"), sums[0])
                ins = pool.tensor_tensor(ssum[:, :], src[:, k, :], src[:, k, :], ALU.mult)
                sums[0] += 1
            else:
                step(pool.tensor_tensor(buf[:, slot, :], src[:, k, :], src[:, k, :], ALU.mult))
                ins = pool.tensor_tensor(ssum[:, :], ssum[:, :], buf[:, slot, :], ALU.add)
            if k == KT - 1:
                ins.then_inc(s("ss_ready"), 1)
            else:
                step(ins)

        spb = arena[:, a0:a0 + 8 * 512].rearrange("p (b n) -> p b n", n=512)
        AB = [spb[:, i, 0:384] for i in (0, 1)]
        SP = [spb[:, i, 0:384] for i in (2, 3)]
        AT = [spb[:, i, 0:384] for i in (4, 5)]
        VT = [spb[:, i, 0:256] for i in (6, 7)]
        osb = arena[:, a0 + 8192:a0 + 8192 + 1024].rearrange("p (b n) -> p b n", n=256)

        def l2b(i):
            return ltri[:, 4 * (i % 2):4 * (i % 2) + 4, :].rearrange("p u n -> p (u n)")

        def eg(h):
            return tmat[:, h, :]

        def neg_w(b):
            return tmat[:, 0:4, :].rearrange("p u n -> p (u n)") if b == 0 else \
                tmat[:, 8:12, :].rearrange("p u n -> p (u n)")

        def state(b):
            return tmat[:, 4:8, :].rearrange("p u n -> p (u n)") if b == 0 else \
                tmat[:, 12:16, :].rearrange("p u n -> p (u n)")

        def v_new(b, j):
            o = 8 * b + 4 * j
            return ltri[:, o:o + 4, :].rearrange("p u n -> p (u n)")

        def l2_apply(dve, i):
            dve.wait_ge(s("l2_rstd"), i + 1)
            nc.vector.tensor_tensor(proj[:, 2 * i:2 * i + 2, :], proj[:, 2 * i:2 * i + 2, :],
                                    l2b(i).rearrange("p (a t) -> p a t", t=T), ALU.mult).then_inc(s("l2_done"), 1)

        def head_norm_inv(dve, h, name, bank):
            dve.wait_ge(s(f"{name}_mm"), h + 1)
            b = osb[:, 2 + h % 2, :]
            nc.vector.tensor_scalar(b, ps[bank + h % 2][:, 0:T] if name == "on" else ps[4 + h % 2][:, 0:T],
                                    1.0 / P, EPS, ALU.mult, ALU.add).then_inc(s(f"{name}_v"), 1)
            dve.wait_ge(s(f"{name}_v"), h + 1)
            nc.vector.reciprocal(b, b).then_inc(s(f"{name}_inv"), 1)

        def dn_gate_out(dve, h):
            V = nc.vector
            dve.wait_ge(s("on_rstd"), h + 1)
            V.scalar_tensor_tensor(proj[:, h, :], proj[:, h, :], hgains[:, 1:2], osb[:, 2 + h % 2, :],
                                   ALU.mult, ALU.mult).then_inc(s("mixd_n"), 1)
            dve.wait_ge(s("mixd_n"), h + 1)
            V.tensor_tensor(proj[:, h, :], proj[:, h, :], proj[:, 24 + h, :], ALU.mult).then_inc(s("mixd_f"), 1)
            dve.wait_ge(s("mixd_hi"), h + 1)
            V.tensor_tensor(xhl[:, HEADS + h, 1, :], proj[:, h, :], xhl[:, HEADS + h, 0, :].bitcast(f32), ALU.subtract
                            ).then_inc(s("mix_lo"), 1)

        def sb_out(dve, h):
            V = nc.vector
            dve.wait_ge(s("son_rstd"), h + 1)
            V.scalar_tensor_tensor(proj[:, 32 + h, :], proj[:, 32 + h, :], hgains[:, 0:1], osb[:, 2 + h % 2, :],
                                   ALU.mult, ALU.mult).then_inc(s("mixs_f"), 1)
            dve.wait_ge(s("mixs_hi"), h + 1)
            V.tensor_tensor(xhl[:, h, 1, :], proj[:, 32 + h, :], xhl[:, h, 0, :].bitcast(f32), ALU.subtract
                            ).then_inc(s("mix_lo"), 1)

        def norm_mm(pe, h):
            pe.wait_ge(s("o_sq"), h + 1)
            if h >= 2:
                pe.wait_ge(s("on_v"), h - 1)
            nc.tensor.matmul(ps[6 + h % 2][:, 0:T], ones[:, :], osb[:, h % 2, :], start=True, stop=True
                             ).then_inc(s("on_mm"), 1)

        block = ctx.enter_context(nc.Block())
        x_v = x
        NX = 4

        @block.sync
        def _(sp):
            for q in range(NX):
                sp.dma_start(res[:, 4 * q:4 * q + 4, :], x_v[:, 4 * q:4 * q + 4, :]).then_inc(s(f"x_in{q}"), 16)
            for slot in range(RAW):
                sp.dma_start(raw[:, slot, :], wts[slot, :, :]).then_inc(raw_full[slot], 16)
            with sp.Fori(1, CHUNKS // RAW) as i:
                for slot in range(RAW):
                    sp.wait_ge(lo_ready, i * RAW + (slot + 1 - RAW))
                    sp.dma_start(raw[:, slot, :], wts[bass.ds(i * RAW + slot, 1), :, :].rearrange("a p n -> p (a n)")
                                 ).then_inc(raw_full[slot], 16)
            sp.wait_ge(s("y_ready"), KT)
            for q in range(4):
                sp.dma_start(out[:, 4 * q:4 * q + 4, :], res[:, 4 * q:4 * q + 4, :]).then_inc(out_done, 16)
            sp.wait_ge(out_done, 64)

        @block.gpsimd
        def _(pool):
            n = [0]

            def step(ins):
                n[0] += 1
                ins.then_inc(s("pool_step"), 1)
                pool.wait_ge(s("pool_step"), n[0])

            pool.memset(ones[:, :], 1.0).then_inc(const_ready, 1)
            step(pool.memset(ident[:, :], 0.0))
            pool.affine_select(out=ident[:, :], in_=ident[:, :], compare_op=ALU.not_equal, fill=1.0, base=0,
                               pattern=[[-1, P]], channel_multiplier=1).then_inc(const_ready, 1)
            step(pool.memset(hist[:, :, 0:3], 0.0))
            step(pool.memset(sel[:, :, :], 1.0))
            pool.affine_select(out=sel[:, :, :], in_=sel[:, :, :], compare_op=ALU.is_equal, fill=0.0, base=0,
                               pattern=[[-1, HEADS], [0, P]], channel_multiplier=1).then_inc(s("sel_ready"), 1)
            for lv in range(LEVELS):
                w = 1 << lv
                na = P // (2 * w)
                m = lmask[:, lv, :].rearrange("p (a b r) -> p a b r", b=2, r=w)
                step(pool.memset(lmask[:, lv, :], 1.0))
                step(pool.affine_select(out=m, in_=m, compare_op=ALU.is_ge, fill=0.0, base=-1,
                                        pattern=[[0, na], [1, 2], [0, w]], channel_multiplier=0))
                step(pool.affine_select(out=m, in_=m, compare_op=ALU.is_ge, fill=0.0, base=0,
                                        pattern=[[-2 * w, na], [0, 2], [0, w]], channel_multiplier=1))
                pool.affine_select(out=m, in_=m, compare_op=ALU.is_ge, fill=0.0, base=w - 1,
                                   pattern=[[2 * w, na], [0, 2], [0, w]], channel_multiplier=-1
                                   ).then_inc(s("lmask_ready"), 1)
            for k in range(KT):
                pool.wait_ge(s("xn_hi"), k + 1)
                pool.tensor_tensor(xhl[:, k, 1, :], full[:, k, :], xhl[:, k, 0, :].bitcast(f32), ALU.subtract
                                   ).then_inc(s("xn_lo"), 1)
            pool.wait_ge(s("proj_done"), 1)
            for i in range(8):
                pool.tensor_tensor(squ[:, 2 * i:2 * i + 2, :], proj[:, 2 * i:2 * i + 2, :], proj[:, 2 * i:2 * i + 2, :],
                                   ALU.mult).then_inc(s("qk_sq"), 1)
            for h in range(HEADS):
                pool.wait_ge(s("dexp"), h + 1)
                d = dm[:, h % 2, :].rearrange("p (j c) -> p j c", j=2)
                pool.affine_select(out=d, in_=d, compare_op=ALU.is_ge, fill=0.0, base=0,
                                   pattern=[[0, 2], [1, P]], channel_multiplier=-1).then_inc(s("dmask"), 1)
            for h in range(HEADS):
                pool.tensor_scalar(proj[:, 32 + h, :], proj[:, 32 + h, :], QSCALE, 0.0, ALU.mult, ALU.add
                                   ).then_inc(s("sbq"), 1)
            pool.wait_ge(s("dn_done"), 1)
            step(pool.memset(xb[:, 0, 0, :], -1.0))
            pool.memset(xb[:, 0, 1, :], -1.0).then_inc(s("tri_ready"), 1)
            pool.affine_select(out=xb[:, 0, 0, :], in_=xb[:, 0, 0, :], compare_op=ALU.is_ge, fill=0.0, base=0,
                               pattern=[[-1, P]], channel_multiplier=1).then_inc(s("tri_ready"), 1)
            for h in range(HEADS):
                pool.wait_ge(s("sp_ready"), h + 1)
                for lot in (0, 2 * P):
                    v = SP[h % 2][:, lot:lot + P]
                    ins = pool.affine_select(out=v, in_=v, compare_op=ALU.is_ge, fill=0.0, base=-1,
                                             pattern=[[1, P]], channel_multiplier=-1)
                ins.then_inc(s("sp_mask"), 1)
                pool.wait_ge(s("att_exp"), h + 1)
                for lot in (0, 2 * P):
                    v = AT[h % 2][:, lot:lot + P]
                    ins = pool.affine_select(out=v, in_=v, compare_op=ALU.is_ge, fill=0.0, base=-1,
                                             pattern=[[1, P]], channel_multiplier=-1)
                ins.then_inc(s("att_mask"), 1)
            for k in range(KT):
                pool.wait_ge(s("mixo_tile"), k + 1)
                square_sum(pool, step, mixo, k, squ[:, 0:2, :], k % 2)
            for k in range(KT):
                pool.wait_ge(s("h_tile"), k + 1)
                square_sum(pool, step, res, k, squ[:, 0:2, :], k % 2)
            for k in range(KT):
                pool.wait_ge(s("hn_hi"), k + 1)
                pool.tensor_tensor(xhl[:, k, 1, :], full[:, k, :], xhl[:, k, 0, :].bitcast(f32), ALU.subtract
                                   ).then_inc(s("hn_lo"), 1)
            pool.wait_ge(s("hn_f"), KT)
            pool.memset(fhist[:, :, 0:2], 0.0).then_inc(s("fhist_ready"), 1)
            with pool.Fori(0, UP_STEPS) as i:
                for q in range(GROUP):
                    pool.wait_ge(s("act_hi"), i * 4 + (q + 1))
                    pool.tensor_tensor(act[:, bass.ds(i * 4 + q, 1), 1, :].rearrange("p a t -> p (a t)"),
                                       prod[:, q % 2, :],
                                       act[:, bass.ds(i * 4 + q, 1), 0, :].rearrange("p a t -> p (a t)").bitcast(f32),
                                       ALU.subtract).then_inc(s("act_lo"), 1)
            for k in range(KT):
                pool.wait_ge(s("down_tile"), k + 1)
                square_sum(pool, step, down, k, dsq, k % 2)

        @block.scalar
        def _(act_e):
            def split(c, q, slot):
                act_e.wait_ge(raw_full[slot], q * 16 + 16)
                act_e.wait_ge(chunk_used, c + 1)
                nc.scalar.activation(w_hi[:, slot % 2, :], raw[:, slot, :], ACT.Copy).then_inc(hi_ready, 1)

            def halves(n, j, b, full, full_count):
                act_e.wait_ge(full, full_count)
                act_e.wait_ge(bank_free, n + 1)
                nc.scalar.activation(halfs[j % 4], ps[b][:, T:2 * T], ACT.Copy).then_inc(half_ready, 1)

            def group_halves(g, j):
                if j < GROUP - 1:
                    halves(g * 4 + j, j, j, bank_full, g * 3 + (j + 1))
                else:
                    halves(g * 4 + j, j, j, chunk_used, g * 4 + 6)

            def splits4(i, c0_, q0):
                for j in range(1, 5):
                    split(i * 4 + (c0_ + j), i + (q0 + j // 4), j % 4)

            act_e.dma_start(gains[:, :, :], norm_gains).then_inc(small_in, 16)
            act_e.dma_start(hgains[:, :], head_gains).then_inc(small_in, 16)
            act_e.dma_start(dcw[:, :, :], dn_conv).then_inc(small_in, 16)
            act_e.dma_start(gate[:, 0:2], dn_gate).then_inc(small_in, 16)
            act_e.dma_start(fcw[:, :, :], ffn_cw).then_inc(small_in, 16)
            act_e.dma_start(fcb[:, :], ffn_cb).then_inc(small_in, 16)
            act_e.dma_start(wba[:, :, :], w_ba).then_inc(small_in, 16)

            for q in range(NX):
                act_e.wait_ge(s(f"x_in{q}"), 16)
                nc.scalar.activation(proj[:, 4 * q:4 * q + 4, :], res[:, 4 * q:4 * q + 4, :], ACT.Square
                                     ).then_inc(s("x_sq"), 1)
            act_e.wait_ge(s("x_inv"), 1)
            nc.scalar.activation(rstd[:, :], vrow[:, :], ACT.Sqrt).then_inc(s("x_rstd"), 1)
            for k in range(KT):
                act_e.wait_ge(s("xn_f"), k + 1)
                nc.scalar.activation(xhl[:, k, 0, :], full[:, k, :], ACT.Copy).then_inc(s("xn_hi"), 1)
            act_e.wait_ge(raw_full[0], 16)
            nc.scalar.activation(w_hi[:, 0, :], raw[:, 0, :], ACT.Copy).then_inc(hi_ready, 1)
            with act_e.Fori(0, DN_GROUPS) as g:
                splits4(g, 0, 0)

                def silu(j):
                    act_e.wait_ge(s("conv_step"), g * 16 + (4 * j + 4))
                    nc.scalar.activation(proj[:, bass.ds(g * 4 + j, 1), :].rearrange("p a t -> p (a t)"),
                                         conv[:, j % 2, :], ACT.Silu).then_inc(s("silu_done"), 1)
                for j in range(GROUP):
                    group_halves(g, j)
                    if j:
                        silu(j - 1)
                silu(GROUP - 1)
            with act_e.Fori(DN_GROUPS, IN_GROUPS) as g:
                splits4(g, 0, 0)
                for j in range(GROUP):
                    group_halves(g, j)

            act_e.wait_ge(s("ba_done"), 1)
            n = [0]

            def step(ins):
                n[0] += 1
                ins.then_inc(s("act_step"), 1)
                act_e.wait_ge(s("act_step"), n[0])
            act_e.wait_ge(s("proj_done"), 1)
            nc.scalar.activation(proj[:, 24:32, :], proj[:, 24:32, :], ACT.Silu).then_inc(s("z_done"), 1)
            nc.scalar.activation(small[:, 0, :], ps[4][0:8, 0:T], ACT.Exp, scale=-1.0).then_inc(s("eb"), 1)
            step(nc.scalar.activation(small[:, 1, :], ps[5][0:8, 0:T], ACT.Identity, bias=gate[:, 1:2]))
            step(nc.scalar.activation(small[:, 2, :], small[:, 1, :], ACT.Abs))
            step(nc.scalar.activation(small[:, 3, :], small[:, 2, :], ACT.Exp, scale=-1.0))
            nc.scalar.activation(gate[:, 2:3], gate[:, 0:1], ACT.Exp).then_inc(s("ga"), 1)
            nc.scalar.activation(small[:, 4, :], small[:, 3, :], ACT.Ln, bias=1.0).then_inc(s("ga"), 1)
            act_e.wait_ge(s("gc_ready"), 2)
            nc.scalar.activation(small[:, 5, :], rows[:, 1, :], ACT.Exp).then_inc(s("eg_row"), 1)
            nc.scalar.activation(rows[:, 3, 0:P], rows[:, 1, 0:P], ACT.Exp, scale=-1.0, bias=rows[:, 1, P - 1:P]
                                 ).then_inc(s("ke_row"), 1)
            for i in range(8):
                act_e.wait_ge(s("l2_inv"), i + 1)
                nc.scalar.activation(l2b(i), l2b(i), ACT.Sqrt, scale=(QSCALE * QSCALE if i < 4 else 1.0)
                                     ).then_inc(s("l2_rstd"), 1)
            for h in range(HEADS):
                act_e.wait_ge(s("ddiff"), h + 1)
                nc.scalar.activation(dm[:, h % 2, :], dm[:, h % 2, :], ACT.Exp).then_inc(s("dexp"), 1)
                nc.scalar.activation(eg(h), ps[4 + h % 2][:, T + P:2 * T], ACT.Exp).then_inc(s("eg_ready"), 1)
            for lv in range(LEVELS):
                for g in range(4):
                    i = 4 * lv + g
                    act_e.wait_ge(s("x_mm"), i + 1)
                    if i >= 2:
                        act_e.wait_ge(s("y_mm"), i - 1)
                    nc.scalar.activation(xb[:, g % 2, :, :], ps[4][:, :] if g % 2 == 0 else ps[5][:, :], ACT.Copy
                                         ).then_inc(s("x_sb"), 1)
            for b in range(2):
                act_e.wait_ge(s("w_mm"), b + 1)
                nc.scalar.activation(neg_w(b), ps[5][:, :], ACT.Copy, scale=-1.0).then_inc(s("w_sb"), 1)
                act_e.wait_ge(s("s_mm"), b + 1)
                nc.scalar.activation(state(b), ps[6][:, :], ACT.Copy).then_inc(s("s_sb"), 1)
                for h in range(4 * b, 4 * b + 4):
                    act_e.wait_ge(s("o_mm"), h + 1)
                    nc.scalar.activation(proj[:, h, :], ps[4 + h % 2][:, 0:T], ACT.Copy).then_inc(s("o_sb"), 1)
                    if h >= 2:
                        act_e.wait_ge(s("on_mm"), h - 1)
                    nc.scalar.activation(osb[:, h % 2, :], ps[4 + h % 2][:, 0:T], ACT.Square).then_inc(s("o_sq"), 1)
                for h in range(4 * b, 4 * b + 4):
                    act_e.wait_ge(s("on_inv"), h + 1)
                    nc.scalar.activation(osb[:, 2 + h % 2, :], osb[:, 2 + h % 2, :], ACT.Sqrt).then_inc(s("on_rstd"), 1)
                    act_e.wait_ge(s("mixd_f"), h + 1)
                    nc.scalar.activation(xhl[:, HEADS + h, 0, :], proj[:, h, :], ACT.Copy).then_inc(s("mixd_hi"), 1)
            for h in range(HEADS + 1):
                if h < HEADS:
                    act_e.wait_ge(s("z_mm"), h + 1)
                    if h >= 2:
                        act_e.wait_ge(s("sp_ready"), h - 1)
                    step(nc.scalar.activation(AB[h % 2], ps[4 + h % 2][:, 0:384], ACT.Abs))
                    step(nc.scalar.activation(AB[h % 2], AB[h % 2], ACT.Exp, scale=-1.0))
                    nc.scalar.activation(AB[h % 2], AB[h % 2], ACT.Ln, bias=1.0).then_inc(s("ln_ready"), 1)
                if h >= 1:
                    g = h - 1
                    act_e.wait_ge(s("c_mm"), g + 1)
                    if g >= 2:
                        act_e.wait_ge(s("av_mm"), g - 1)
                    nc.scalar.activation(AT[g % 2], ps[4 + g % 2][:, 0:384], ACT.Exp).then_inc(s("att_exp"), 1)
            for h in range(HEADS + 1):
                if h < HEADS:
                    act_e.wait_ge(s("so_sb"), h + 1)
                    if h >= 2:
                        act_e.wait_ge(s("son_mm"), h - 1)
                    nc.scalar.activation(osb[:, h % 2, :], proj[:, 32 + h, :], ACT.Square).then_inc(s("so_sq"), 1)
                if h:
                    g = h - 1
                    act_e.wait_ge(s("son_inv"), g + 1)
                    nc.scalar.activation(osb[:, 2 + g % 2, :], osb[:, 2 + g % 2, :], ACT.Sqrt
                                         ).then_inc(s("son_rstd"), 1)
                    act_e.wait_ge(s("mixs_f"), g + 1)
                    nc.scalar.activation(xhl[:, g, 0, :], proj[:, 32 + g, :], ACT.Copy).then_inc(s("mixs_hi"), 1)

            with act_e.Fori(IN_GROUPS, IN_GROUPS + OUT_GROUPS) as g:
                splits4(g, 0, 0)
                for j in range(GROUP):
                    group_halves(g, j)
            for stage, (inv, rs) in enumerate((("m_inv", "m_rstd"), ("h_inv", "h_rstd"))):
                act_e.wait_ge(s(inv), 1)
                nc.scalar.activation(rstd[:, :], vrow[:, :], ACT.Sqrt).then_inc(s(rs), 1)
            for k in range(KT):
                act_e.wait_ge(s("hn_f"), k + 1)
                nc.scalar.activation(xhl[:, k, 0, :], full[:, k, :], ACT.Copy).then_inc(s("hn_hi"), 1)

            UC = IN_CHUNKS + OUT_CHUNKS

            def gelu_tile(i, q):
                act_e.wait_ge(s("fconv_step"), i * 24 + (3 * q + 3))
                act_e.wait_ge(s("prod_ready"), i * 4 + (q + 1))
                nc.scalar.activation(gelu[:, q, :], fconv[:, q % 2, :], ACT.Gelu_apprx_tanh
                                     ).then_inc(s("gelu_done"), 1)

            def act_hi(i, q):
                act_e.wait_ge(s("prod_ready"), i * 4 + (q + 5))
                nc.scalar.activation(act[:, bass.ds(i * 4 + q, 1), 0, :].rearrange("p a t -> p (a t)"),
                                     prod[:, q % 2, :], ACT.Copy).then_inc(s("act_hi"), 1)

            def split_in(g, q):
                split(g * 4 + (q + 1), g + (q + 1) // 4, (q + 1) % 4)

            def evacuate(g):
                for q in range(GROUP):
                    group_halves(g, q)

            def gate_slots(i, g):
                for q in range(3):
                    gelu_tile(i, q)
                    if q < 2:
                        split_in(g, q + 2)
                evacuate(g)

            UG = UC // 4
            for q in range(GROUP):
                split_in(UG, q)
            evacuate(UG)
            split_in(UG + 1, 0)
            split_in(UG + 1, 1)
            with act_e.Fori(0, UP_STEPS - 1) as i:
                gate_slots(i, i * 2 + (UG + 1))
                nxt = i * 2 + (UG + 2)
                split_in(nxt, 0)
                gelu_tile(i, 3)
                for q in range(3):
                    split_in(nxt, q + 1)
                    act_hi(i, q)
                evacuate(nxt)
                split_in(i * 2 + (UG + 3), 0)
                act_hi(i, 3)
                split_in(i * 2 + (UG + 3), 1)
            gate_slots(UP_STEPS - 1, UG + 2 * UP_STEPS - 1)
            DC = UC + UP_CHUNKS
            for hf in range(2):
                c = DC + hf * HALF_CHUNKS
                last = hf == 1
                n_here = HALF_CHUNKS - (1 if last else 0)
                k = 1
                while (c + k) % 4:
                    split(c + k, (c + k) // 4, (c + k) % 4)
                    if hf == 0:
                        if k == 1:
                            gelu_tile(UP_STEPS - 1, 3)
                        else:
                            act_hi(UP_STEPS - 1, k - 2)
                    k += 1
                if hf == 0:
                    act_hi(UP_STEPS - 1, GROUP - 2)
                    act_hi(UP_STEPS - 1, GROUP - 1)
                turns = (n_here - k + 1) // 4
                with act_e.Fori(0, turns) as r:
                    for j in range(4):
                        split(r * 4 + (c + k + j), r + (c + k) // 4, j)
                for k in range(k + 4 * turns, n_here + 1):
                    split(c + k, (c + k) // 4, (c + k) % 4)
                for j in range(DOWN_TILES):
                    if j < DOWN_TILES - 1:
                        halves(DC + hf * DOWN_TILES + j, j, j, bank_full, DC // 4 * 3 + hf * (DOWN_TILES - 1) + j + 1)
                    else:
                        halves(DC + hf * DOWN_TILES + j, j, j, chunk_used, c + HALF_CHUNKS + 2)
            act_e.wait_ge(s("f_inv"), 1)
            nc.scalar.activation(rstd[:, :], vrow[:, :], ACT.Sqrt).then_inc(s("f_rstd"), 1)

        @block.vector
        def _(dve):
            V = nc.vector
            n = [0]

            def step(ins):
                n[0] += 1
                ins.then_inc(s("dve_step"), 1)
                dve.wait_ge(s("dve_step"), n[0])

            def split(c, slot):
                dve.wait_ge(hi_ready, c + 1)
                V.tensor_tensor(w_lo[:, slot % 2, :], raw[:, slot, :], w_hi[:, slot % 2, :].bitcast(f32), ALU.subtract
                                ).then_inc(lo_ready, 1)

            def added(n_, j, b, out_):
                dve.wait_ge(half_ready, n_ + 1)
                return V.tensor_tensor(out_, ps[b][:, 0:T], halfs[j % 4], ALU.add).then_inc(bank_free, 1)

            def splits4(i, c0_):
                for j in range(1, 5):
                    split(i * 4 + (c0_ + j), j % 4)

            V.memset(mark[:, 0:1], 0.0).then_inc(bank_free, 4)
            V.memset(mark[:, 1:2], 0.0).then_inc(chunk_used, 2)
            V.memset(mark[:, 2:3], 0.0).then_inc(s("silu_done"), 2)
            dve.wait_ge(s("x_sq"), NX)
            V.tensor_reduce(ssum[:, :], proj[:, 0:KT, :].rearrange("p k t -> p t k"), mybir.AxisListType.X, ALU.add
                            ).then_inc(s("x_ss"), 1)
            dve.wait_ge(s("xsum_mm"), 1)
            step(V.tensor_scalar(vrow[:, :], ps[4][:, 0:T], 1.0 / D, EPS, ALU.mult, ALU.add))
            V.reciprocal(vrow[:, :], vrow[:, :]).then_inc(s("x_inv"), 1)
            dve.wait_ge(small_in, 16 * 7)
            dve.wait_ge(s("x_rstd"), 1)
            for k in range(KT):
                V.scalar_tensor_tensor(full[:, k, :], res[:, k, :], gains[:, 0, k:k + 1], rstd[:, :], ALU.mult, ALU.mult
                                       ).then_inc(s("xn_f"), 1)
            split(0, 0)
            dve.wait_ge(s("pool_step"), 2)
            with dve.Fori(0, DN_GROUPS) as g:
                splits4(g, 0)
                for j in range(GROUP):
                    b = j % 2
                    dve.wait_ge(s("silu_done"), g * 4 + (j + 1))
                    added(g * 4 + j, j, j, hist[:, b, 3:3 + T])
                    for tap in range(4):
                        if tap:
                            dve.wait_ge(s("conv_step"), g * 16 + (4 * j + tap))
                        else:
                            dve.wait_ge(bank_free, g * 4 + (j + 1 + 4))
                        src = hist[:, b, tap:tap + T]
                        w = dcw[:, tap, bass.ds(g * 4 + j, 1)]
                        if tap == 0:
                            V.tensor_scalar(conv[:, b, :], src, w, None, ALU.mult).then_inc(s("conv_step"), 1)
                        else:
                            V.scalar_tensor_tensor(conv[:, b, :], src, w, conv[:, b, :], ALU.mult, ALU.add
                                                   ).then_inc(s("conv_step"), 1)
            with dve.Fori(DN_GROUPS, IN_GROUPS) as g:
                splits4(g, 0)
                for j in range(GROUP):
                    added(g * 4 + j, j, j, proj[:, bass.ds(g * 4 + j, 1), :].rearrange("p a t -> p (a t)"))
            dve.wait_ge(s("silu_done"), 4 * DN_GROUPS + 2)
            dve.wait_ge(bank_free, 4 * IN_GROUPS + 4)
            step(V.memset(mark[:, 0:1], 0.0))
            V.memset(mark[:, 0:1], 0.0).then_inc(s("proj_done"), 1)

            dve.wait_ge(s("eb"), 1)
            step(V.tensor_scalar(small[:, 0, :], small[:, 0, :], 1.0, None, ALU.add))
            step(V.reciprocal(rows[:, 0, :], small[:, 0, :]))
            dve.wait_ge(s("ga"), 2)
            step(V.scalar_tensor_tensor(small[:, 1, :], small[:, 1, :], 0.0, small[:, 4, :], ALU.max, ALU.add))
            step(V.tensor_scalar(small[:, 1, :], small[:, 1, :], gate[:, 2:3], -1.0, ALU.mult, ALU.mult))
            step(V.memset(small[:, 2, :], 1.0))
            for j in range(NJ):
                V.tensor_tensor_scan(rows[:, 1, j * P:(j + 1) * P], small[:, 2, 0:P], small[:, 1, j * P:(j + 1) * P],
                                     0.0, ALU.mult, ALU.add).then_inc(s("gc_ready"), 1)
            dve.wait_ge(s("eg_row"), 1)
            V.tensor_tensor(rows[:, 2, :], rows[:, 0, :], small[:, 5, :], ALU.mult).then_inc(s("bg_row"), 1)
            dve.wait_ge(s("cols_mm"), 1)
            V.tensor_copy(cols[:, :, :].rearrange("p r h -> p (r h)"), ps[6][:, 0:48]).then_inc(s("cols_sb"), 1)
            for i in range(8):
                dve.wait_ge(s("l2_mm"), i + 1)
                if i >= 2:
                    dve.wait_ge(s("l2_done"), i - 1)
                step(V.tensor_scalar(l2b(i), ps[4 + i % 2][:, :], EPS, None, ALU.add))
                V.reciprocal(l2b(i), l2b(i)).then_inc(s("l2_inv"), 1)
                if i >= 1:
                    l2_apply(dve, i - 1)
            l2_apply(dve, 7)
            for h in range(HEADS):
                b = h % 2
                dve.wait_ge(s("bc_mm"), h + 1)
                if h >= 2:
                    dve.wait_ge(s("a_mm"), h - 1)
                V.tensor_tensor(kb[:, b, :], proj[:, 8 + h, :], ps[4 + b][:, 0:T], ALU.mult).then_inc(s("kb_ready"), 1)
                for j in range(NJ):
                    ins = V.tensor_scalar(dm[:, b, j * P:(j + 1) * P], ps[4 + b][:, T + j * P:T + (j + 1) * P],
                                          cols[:, j, h:h + 1], 0.0, ALU.subtract, ALU.min)
                ins.then_inc(s("ddiff"), 1)
                dve.wait_ge(s("a_mm"), h + 1)
                dve.wait_ge(s("dmask"), h + 1)
                d = dm[:, b, :].rearrange("p (j c) -> p j c", j=2)
                a = ps[6 + b][:, :].rearrange("p (j x c) -> p j x c", j=2, x=2)
                V.tensor_tensor(ltri[:, 2 * h:2 * h + 2, :], a[:, :, 0, :], d, ALU.mult)
                V.tensor_tensor(qa[:, 2 * h:2 * h + 2, :], a[:, :, 1, :], d, ALU.mult)
                dve.wait_ge(s("eg_ready"), h + 1)
                V.tensor_tensor(proj[:, h, P:T], proj[:, h, P:T], eg(h), ALU.mult).then_inc(s("qd_ready"), 1)
                dve.wait_ge(s("tok_mm"), h + 1)
                tp = ps[6 + b]
                for j in range(NJ):
                    V.tensor_scalar(proj[:, 16 + h, j * P:(j + 1) * P], tp[:, j * P:(j + 1) * P], cols[:, 2 + j, h:h + 1],
                                    None, ALU.mult)
                V.tensor_scalar(proj[:, 8 + h, 0:P], tp[:, T:T + P], cols[:, 5, h:h + 1], None, ALU.mult)
                V.tensor_scalar(proj[:, 8 + h, P:T], tp[:, T + P:2 * T], cols[:, 4, h:h + 1], None, ALU.mult
                                ).then_inc(s("tok_sb"), 1)
            for u in range(UNITS):
                V.tensor_copy(tmat[:, u, :], ident[:, :])
                ins = V.tensor_copy(tmatT[:, u, :], ident[:, :])
            ins.then_inc(s("t_init"), 1)
            dve.wait_ge(s("lmask_ready"), LEVELS)
            dve.wait_ge(s("tok_sb"), HEADS)

            def level_b(i):
                lv, g = divmod(i, 4)
                if i >= 2:
                    dve.wait_ge(s("x_mm"), i - 1)
                m = lmask[:, lv, :].rearrange("p (a c) -> p a c", a=1).to_broadcast([P, 4, P])
                V.tensor_tensor(bb[:, g % 2, :, :], ltri[:, 4 * g:4 * g + 4, :], m, ALU.mult).then_inc(s("b_ready"), 1)

            level_b(0)
            level_b(1)
            for i in range(4 * LEVELS):
                g = i % 4
                dve.wait_ge(s("y_mm"), i + 1)
                for t_, bank in ((tmat, 6), (tmatT, 7)):
                    v = t_[:, 4 * g:4 * g + 4, :].rearrange("p u n -> p (u n)")
                    ins = V.tensor_tensor(v, v, ps[bank][:, :], ALU.subtract)
                ins.then_inc(s("t_ready"), 1)
                if i + 2 < 4 * LEVELS:
                    level_b(i + 2)
            for b in range(2):
                dve.wait_ge(s("u_mm"), b + 1)
                V.tensor_copy(v_new(b, 0), ps[4][:, :]).then_inc(s("v0_sb"), 1)
                dve.wait_ge(s("v1_mm"), b + 1)
                V.tensor_copy(v_new(b, 1), ps[7][:, :]).then_inc(s("v1_sb"), 1)
                for h in range(4 * b, 4 * b + 4):
                    head_norm_inv(dve, h, "on", 6)
                    if h % 4:
                        dn_gate_out(dve, h - 1)
                dn_gate_out(dve, 4 * b + 3)
            V.memset(mark[:, 0:1], 0.0).then_inc(s("dn_done"), 1)
            for h in range(HEADS + 1):
                if h < HEADS:
                    b = h % 2
                    dve.wait_ge(s("ln_ready"), h + 1)
                    if h >= 2:
                        dve.wait_ge(s("c_mm"), h - 1)
                    V.scalar_tensor_tensor(SP[b], ps[4 + b][:, 0:384], 0.0, AB[b], ALU.max, ALU.add
                                           ).then_inc(s("sp_ready"), 1)
                    dve.wait_ge(s("vt_mm"), h + 1)
                    V.tensor_copy(VT[b], ps[6][:, 0:T]).then_inc(s("vt_sb"), 1)
                if h:
                    dve.wait_ge(s("av_mm"), h)
                    V.tensor_copy(proj[:, 32 + h - 1, :], ps[7][:, 0:T]).then_inc(s("so_sb"), 1)
            for h in range(HEADS):
                head_norm_inv(dve, h, "son", 6)
                if h:
                    sb_out(dve, h - 1)
            sb_out(dve, HEADS - 1)

            with dve.Fori(IN_GROUPS, IN_GROUPS + OUT_GROUPS) as g:
                splits4(g, 0)
                for j in range(GROUP):
                    dve.wait_ge(half_ready, g * 4 + (j + 1))
                    V.tensor_tensor(mixo[:, bass.ds(g * 4 + (j - 4 * IN_GROUPS), 1), :].rearrange("p a t -> p (a t)"),
                                    ps[j][:, 0:T], halfs[j % 4], ALU.add).then_inc(bank_free, 1)
                    dve.wait_ge(bank_free, g * 4 + (j + 5))
                    V.memset(mark[:, 0:1], 0.0).then_inc(s("mixo_tile"), 1)

            def inverse(idx, name, bank):
                dve.wait_ge(s("ss_mm"), idx)
                step(V.tensor_scalar(vrow[:, :], ps[bank][:, 0:T], 1.0 / D, EPS, ALU.mult, ALU.add))
                V.reciprocal(vrow[:, :], vrow[:, :]).then_inc(s(name), 1)

            inverse(1, "m_inv", 4)
            dve.wait_ge(s("m_rstd"), 1)
            for k in range(KT):
                step(V.scalar_tensor_tensor(mixo[:, k, :], mixo[:, k, :], gains[:, 1, k:k + 1], rstd[:, :],
                                            ALU.mult, ALU.mult))
                V.tensor_tensor(res[:, k, :], res[:, k, :], mixo[:, k, :], ALU.add).then_inc(s("h_tile"), 1)
            inverse(2, "h_inv", 4)
            dve.wait_ge(s("h_rstd"), 1)
            for k in range(KT):
                V.scalar_tensor_tensor(full[:, k, :], res[:, k, :], gains[:, 2, k:k + 1], rstd[:, :], ALU.mult, ALU.mult
                                       ).then_inc(s("hn_f"), 1)
            dve.wait_ge(s("fhist_ready"), 1)
            dve.wait_ge(s("hn_lo"), KT)
            UC = IN_CHUNKS + OUT_CHUNKS

            def ffn_conv(i, part, q):
                b = 2 * part + q % 2
                if part == 0:
                    dve.wait_ge(s("gelu_done"), i * 4 + (q + 1))
                else:
                    dve.wait_ge(s("prod_ready"), i * 4 + (q + 3))
                col = bass.ds(i * 4 + (part * FT + q), 1)
                for k in range(3):
                    src = fhist[:, q, k:k + T]
                    if k == 0:
                        ins = V.tensor_scalar(fconv[:, b, :], src, fcw[:, 0, col], fcb[:, col], ALU.mult, ALU.add)
                    else:
                        dve.wait_ge(s("fconv_step"), i * 24 + (12 * part + 3 * q + k))
                        ins = V.scalar_tensor_tensor(fconv[:, b, :], src, fcw[:, k, col], fconv[:, b, :],
                                                     ALU.mult, ALU.add)
                    ins.then_inc(s("fconv_step"), 1)

            def value_tile(i, q):
                ffn_conv(i, 1, q)
                dve.wait_ge(s("fconv_step"), i * 24 + (12 + 3 * q + 3))
                dve.wait_ge(s("gelu_done"), i * 4 + (q + 3))
                dve.wait_ge(s("act_lo"), i * 4 + (q + 1))
                V.tensor_tensor(prod[:, q % 2, :], gelu[:, q, :], fconv[:, 2 + q % 2, :], ALU.mult
                                ).then_inc(s("prod_ready"), 1)

            def up_group(g, work, steps):
                for q in range(GROUP):
                    split(g * 4 + (q + 1), (q + 1) % 4)
                    work(q)
                if steps is not None:
                    dve.wait_ge(s("fconv_step"), steps)
                for q in range(GROUP):
                    added(g * 4 + q, q, q, fhist[:, q, 2:2 + T])
                dve.wait_ge(bank_free, g * 4 + 8)

            V.memset(mark[:, 0:1], 0.0).then_inc(s("gelu_done"), 2)
            V.memset(mark[:, 1:2], 0.0).then_inc(s("prod_ready"), 4)
            V.memset(mark[:, 2:3], 0.0).then_inc(s("act_lo"), 2)
            up_group(UC // 4, lambda q: None, None)
            with dve.Fori(0, UP_STEPS - 1) as i:
                up_group(i * 2 + (UC // 4 + 1), lambda q: ffn_conv(i, 0, q), i * 24 + 12)
                up_group(i * 2 + (UC // 4 + 2), lambda q: value_tile(i, q), i * 24 + 24)
            up_group(UC // 4 + 2 * UP_STEPS - 1, lambda q: ffn_conv(UP_STEPS - 1, 0, q), (UP_STEPS - 1) * 24 + 12)
            DC = UC + UP_CHUNKS
            for hf in range(2):
                c = DC + hf * HALF_CHUNKS
                n_here = HALF_CHUNKS - (1 if hf == 1 else 0)
                k = 1
                while (c + k) % 4:
                    split(c + k, (c + k) % 4)
                    if hf == 0:
                        value_tile(UP_STEPS - 1, k - 1)
                    k += 1
                if hf == 0:
                    value_tile(UP_STEPS - 1, GROUP - 1)
                turns = (n_here - k + 1) // 4
                with dve.Fori(0, turns) as r:
                    for j in range(4):
                        split(r * 4 + (c + k + j), j)
                for k in range(k + 4 * turns, n_here + 1):
                    split(c + k, (c + k) % 4)
                for j in range(DOWN_TILES):
                    t_ = hf * DOWN_TILES + j
                    added(DC + t_, j, j, down[:, t_, :])
                    dve.wait_ge(bank_free, DC + t_ + 5)
                    V.memset(mark[:, 0:1], 0.0).then_inc(s("down_tile"), 1)
            inverse(3, "f_inv", 0)
            dve.wait_ge(s("f_rstd"), 1)
            for k in range(KT):
                step(V.scalar_tensor_tensor(down[:, k, :], down[:, k, :], gains[:, 3, k:k + 1], rstd[:, :],
                                            ALU.mult, ALU.mult))
                V.tensor_tensor(res[:, k, :], res[:, k, :], down[:, k, :], ALU.add).then_inc(s("y_ready"), 1)

        @block.tensor
        def _(pe):
            M = nc.tensor.matmul

            def group(c, n_, kchunks=4):
                for q in range(4):
                    pe.wait_ge(lo_ready, c + (q + 1))
                    for j in range(GROUP):
                        if q == 0:
                            pe.wait_ge(bank_free, n_ + (j + 1))
                        for kk in range(CHUNK_K):
                            k = CHUNK_K * q + kk
                            w = slice(kk * 512 + j * P, kk * 512 + (j + 1) * P)
                            M(ps[j][:, :], w_hi[:, q % 2, w], xhl[:, k, :, :].rearrange("p a t -> p (a t)"),
                              start=(k == 0), stop=False, skip_group_check=True)
                            last = M(ps[j][:, 0:T], w_lo[:, q % 2, w], xhl[:, k, 0, :],
                                     start=False, stop=(k == KT - 1), skip_group_check=True)
                        if q == 3 and j < GROUP - 1:
                            last.then_inc(bank_full, 1)
                    last.then_inc(chunk_used, 1)

            pe.wait_ge(const_ready, 2)
            pe.wait_ge(s("x_ss"), 1)
            M(ps[4][:, 0:T], ones[:, :], ssum[:, :], start=True, stop=True).then_inc(s("xsum_mm"), 1)
            pe.wait_ge(s("xn_f"), KT)
            for k in range(KT):
                M(ps[4][0:8, 0:T], wba[:, k, 0:8], full[:, k, :], start=(k == 0), stop=(k == KT - 1))
            for k in range(KT):
                last = M(ps[5][0:8, 0:T], wba[:, k, 8:16], full[:, k, :], start=(k == 0), stop=(k == KT - 1))
            last.then_inc(s("ba_done"), 1)
            pe.wait_ge(s("xn_lo"), KT)
            with pe.Fori(0, IN_GROUPS) as g:
                group(g * 4, g * 4)

            pe.wait_ge(s("bg_row"), 1)
            pe.wait_ge(s("ke_row"), 1)
            for n_, (r, j) in enumerate(((1, 0), (1, 1), (0, 0), (0, 1), (2, 1), (3, 0))):
                last = nc.tensor.transpose(ps[6][:, 8 * n_:8 * n_ + 8], rows[:, r, j * P:(j + 1) * P], ident[0:8, 0:8])
            last.then_inc(s("cols_mm"), 1)
            pe.wait_ge(s("ga"), 2)
            for i in range(8):
                pe.wait_ge(s("qk_sq"), i + 1)
                if i >= 2:
                    pe.wait_ge(s("l2_inv"), i - 1)
                M(ps[4 + i % 2][:, :], ones[:, :], squ[:, 2 * i:2 * i + 2, :].rearrange("p a t -> p (a t)"),
                  start=True, stop=True).then_inc(s("l2_mm"), 1)
            pe.wait_ge(s("sel_ready"), 1)
            pe.wait_ge(s("l2_done"), 8)
            pe.wait_ge(s("cols_sb"), 1)
            for h in range(HEADS):
                b = h % 2
                if h >= 2:
                    pe.wait_ge(s("ddiff"), h - 1)
                    pe.wait_ge(s("eg_ready"), h - 1)
                M(ps[4 + b][:, :], sel[:, h, :], rows[:, 0:2, :].rearrange("p r t -> p (r t)"), start=True, stop=True
                  ).then_inc(s("bc_mm"), 1)
                pe.wait_ge(s("kb_ready"), h + 1)
                if h >= 2:
                    pe.wait_ge(s("tok_sb"), h - 1)
                for j in range(NJ):
                    cs = slice(j * P, (j + 1) * P)
                    M(ps[6 + b][:, j * T:j * T + P], proj[:, 8 + h, cs], kb[:, b, cs], start=True, stop=True)
                    last = M(ps[6 + b][:, j * T + P:(j + 1) * T], proj[:, 8 + h, cs], proj[:, h, cs],
                             start=True, stop=True)
                last.then_inc(s("a_mm"), 1)
                pe.wait_ge(s("qd_ready"), h + 1)
                for x_, t_ in ((0, 16 + h), (1, 8 + h)):
                    for j in range(NJ):
                        last = nc.tensor.transpose(ps[6 + b][:, (2 * x_ + j) * P:(2 * x_ + j + 1) * P],
                                                   proj[:, t_, j * P:(j + 1) * P], ident[:, :])
                last.then_inc(s("tok_mm"), 1)
            pe.wait_ge(s("t_init"), 1)
            pe.wait_ge(s("tok_sb"), HEADS)

            def x_mm(i):
                lv, g = divmod(i, 4)
                pe.wait_ge(s("b_ready"), i + 1)
                if lv:
                    pe.wait_ge(s("t_ready"), 4 * (lv - 1) + g + 1)
                if i >= 2:
                    pe.wait_ge(s("x_sb"), i - 1)
                for u in range(4):
                    last = M(ps[4 + g % 2][:, u * P:(u + 1) * P], bb[:, g % 2, u, :], tmat[:, 4 * g + u, :],
                             start=True, stop=True)
                last.then_inc(s("x_mm"), 1)

            x_mm(0)
            for i in range(4 * LEVELS):
                g = i % 4
                if i + 1 < 4 * LEVELS:
                    x_mm(i + 1)
                pe.wait_ge(s("x_sb"), i + 1)
                if i:
                    pe.wait_ge(s("t_ready"), i)
                for u in range(4):
                    M(ps[6][:, u * P:(u + 1) * P], tmatT[:, 4 * g + u, :], xb[:, g % 2, u, :], start=True, stop=True)
                    last = M(ps[7][:, u * P:(u + 1) * P], xb[:, g % 2, u, :], tmatT[:, 4 * g + u, :],
                             start=True, stop=True)
                last.then_inc(s("y_mm"), 1)
            pe.wait_ge(s("t_ready"), 4 * LEVELS)
            o_count = [0]
            for b in range(2):
                hs = range(4 * b, 4 * b + 4)
                if b:
                    pe.wait_ge(s("o_sq"), 4)
                    pe.wait_ge(s("on_v"), 4)
                for i, h in enumerate(hs):
                    c = slice(i * P, (i + 1) * P)
                    last = M(ps[4][:, c], tmatT[:, 2 * h, :], proj[:, 16 + h, 0:P], start=True, stop=True)
                last.then_inc(s("u_mm"), 1)
                for i, h in enumerate(hs):
                    c = slice(i * P, (i + 1) * P)
                    last = M(ps[5][:, c], proj[:, 8 + h, P:T], tmatT[:, 2 * h + 1, :], start=True, stop=True)
                last.then_inc(s("w_mm"), 1)
                pe.wait_ge(s("v0_sb"), b + 1)
                for i, h in enumerate(hs):
                    c = slice(i * P, (i + 1) * P)
                    last = M(ps[6][:, c], proj[:, 8 + h, 0:P], v_new(b, 0)[:, c], start=True, stop=True)
                last.then_inc(s("s_mm"), 1)
                pe.wait_ge(s("w_sb"), b + 1)
                pe.wait_ge(s("s_sb"), b + 1)
                for i, h in enumerate(hs):
                    c = slice(i * P, (i + 1) * P)
                    M(ps[7][:, c], tmatT[:, 2 * h + 1, :], proj[:, 16 + h, P:T], start=True, stop=False)
                    last = M(ps[7][:, c], neg_w(b)[:, c], state(b)[:, c], start=False, stop=True)
                last.then_inc(s("v1_mm"), 1)
                pe.wait_ge(s("v1_sb"), b + 1)
                for i, h in enumerate(hs):
                    c = slice(i * P, (i + 1) * P)
                    if h % 4 >= 2:
                        pe.wait_ge(s("o_sq"), h - 1)
                    bank = ps[4 + h % 2]
                    M(bank[:, 0:P], v_new(b, 0)[:, c], qa[:, 2 * h, :], start=True, stop=True)
                    M(bank[:, P:T], state(b)[:, c], proj[:, h, P:T], start=True, stop=False)
                    M(bank[:, P:T], v_new(b, 1)[:, c], qa[:, 2 * h + 1, :], start=False, stop=True
                      ).then_inc(s("o_mm"), 1)
                    if h % 4:
                        norm_mm(pe, h - 1)
                norm_mm(pe, 4 * b + 3)
            pe.wait_ge(s("sbq"), HEADS)
            pe.wait_ge(s("dn_done"), 1)
            pe.wait_ge(s("tri_ready"), 2)
            for h in range(HEADS + 1):
                if h < HEADS:
                    b = h % 2
                    if h >= 2:
                        pe.wait_ge(s("att_exp"), h - 1)
                    M(ps[4 + b][:, 0:T], proj[:, 40 + h, 0:P], proj[:, 32 + h, :], start=True, stop=False,
                      skip_group_check=True)
                    M(ps[4 + b][:, T:T + P], proj[:, 40 + h, P:T], proj[:, 32 + h, P:T], start=False, stop=True,
                      skip_group_check=True).then_inc(s("z_mm"), 1)
                    if h:
                        pe.wait_ge(s("vt_sb"), h)
                    for j in range(NJ):
                        last = nc.tensor.transpose(ps[6][:, j * P:(j + 1) * P], proj[:, 48 + h, j * P:(j + 1) * P],
                                                   ident[:, :])
                    last.then_inc(s("vt_mm"), 1)
                if h:
                    g = h - 1
                    b = g % 2
                    pe.wait_ge(s("sp_mask"), g + 1)
                    tri, neg1 = xb[:, 0, 0, :], xb[:, 0, 1, :]
                    M(ps[4 + b][:, 0:T], tri, SP[b][:, 0:T], start=False, stop=False, skip_group_check=True)
                    M(ps[4 + b][:, P:T], neg1, SP[b][:, T:T + P], start=False, stop=False, skip_group_check=True)
                    M(ps[4 + b][:, T:T + P], tri, SP[b][:, T:T + P], start=False, stop=True, skip_group_check=True
                      ).then_inc(s("c_mm"), 1)
                    pe.wait_ge(s("att_mask"), g + 1)
                    pe.wait_ge(s("vt_sb"), g + 1)
                    if g:
                        pe.wait_ge(s("so_sb"), g)
                    M(ps[7][:, 0:P], VT[b][:, 0:P], AT[b][:, 0:P], start=True, stop=True)
                    M(ps[7][:, P:T], VT[b][:, 0:P], AT[b][:, P:T], start=True, stop=False)
                    M(ps[7][:, P:T], VT[b][:, P:T], AT[b][:, T:T + P], start=False, stop=True
                      ).then_inc(s("av_mm"), 1)
            for h in range(HEADS):
                pe.wait_ge(s("so_sq"), h + 1)
                if h >= 2:
                    pe.wait_ge(s("son_v"), h - 1)
                M(ps[4 + h % 2][:, 0:T], ones[:, :], osb[:, h % 2, :], start=True, stop=True).then_inc(s("son_mm"), 1)

            pe.wait_ge(s("mix_lo"), 2 * HEADS)
            with pe.Fori(IN_GROUPS, IN_GROUPS + OUT_GROUPS) as g:
                group(g * 4, g * 4)
            for i in range(2):
                pe.wait_ge(s("ss_ready"), i + 1)
                M(ps[4][:, 0:T], ones[:, :], ssum[:, :], start=True, stop=True
                  ).then_inc(s("ss_mm"), 1)
            pe.wait_ge(s("hn_lo"), KT)
            UC = IN_CHUNKS + OUT_CHUNKS
            with pe.Fori(UC // 4, UC // 4 + 2 * UP_STEPS) as g:
                group(g * 4, g * 4)
            DC = UC + UP_CHUNKS
            pe.wait_ge(s("act_lo"), FT - 4 + 2)

            def down_chunk(c, k, slot, first, lastc, hf):
                pe.wait_ge(lo_ready, c + 1)
                for j in range(DOWN_TILES):
                    if first and (hf or j < 4):
                        pe.wait_ge(bank_free, (DC + j + 1) if hf == 0 else (DC + j + 5))
                    for kk in range(DOWN_K):
                        w = slice(kk * 1024 + j * P, kk * 1024 + (j + 1) * P)
                        xk = act[:, k + kk, :, :] if isinstance(k, int) else \
                            act[:, bass.ds(k + kk, 1), :, :].rearrange("p o a t -> p (o a) t")
                        M(ps[j][:, :], w_hi[:, slot, w], xk.rearrange("p a t -> p (a t)"),
                          start=(first and kk == 0), stop=False, skip_group_check=True)
                        last = M(ps[j][:, 0:T], w_lo[:, slot, w], xk[:, 0, :], start=False,
                                 stop=(lastc and kk == DOWN_K - 1), skip_group_check=True)
                    if lastc and j < DOWN_TILES - 1:
                        last.then_inc(bank_full, 1)
                last.then_inc(chunk_used, 1)

            for hf in range(2):
                c = DC + hf * HALF_CHUNKS
                for k in range(2):
                    down_chunk(c + k, 2 * k, (c + k) % 2, k == 0, False, hf)
                with pe.Fori(1, HALF_CHUNKS // 2 - 1) as r:
                    for k in range(2):
                        down_chunk(r * 2 + (c + k), r * 4 + 2 * k, (c + k) % 2, False, False, hf)
                pe.wait_ge(s("act_lo"), FT + 2)
                for k in range(HALF_CHUNKS - 2, HALF_CHUNKS):
                    down_chunk(c + k, 2 * k, (c + k) % 2, False, k == HALF_CHUNKS - 1, hf)
            pe.wait_ge(s("ss_ready"), 3)
            M(ps[0][:, 0:T], ones[:, :], ssum[:, :], start=True, stop=True).then_inc(s("ss_mm"), 1)



def weight_chunks(w_in, w_out, w_up, w_down):
    def by_columns(w):
        k, n = w.shape
        return w.reshape(k // (CHUNK_K * P), CHUNK_K, P, n // 512, 512).transpose(3, 0, 2, 1, 4).reshape(-1, P, CHUNK)

    sb3, dn3 = 3 * HEADS * P, 3 * HEADS * P
    z = HEADS * P
    w_in = np.concatenate([w_in[:, sb3:sb3 + dn3 + z], w_in[:, 0:sb3]], axis=1)
    up = by_columns(w_up).reshape(2, UP_STEPS, 4, P, CHUNK).transpose(1, 0, 2, 3, 4).reshape(-1, P, CHUNK)
    dn = w_down.reshape(HALF_CHUNKS, DOWN_K, P, 2, 1024).transpose(3, 0, 2, 1, 4).reshape(-1, P, CHUNK)
    return np.concatenate([by_columns(w_in), by_columns(w_out), up, dn], axis=0)


def kernel(**inputs):
    import numpy as _np
    import concourse.bacc as _bacc
    from concourse import mybir as _mybir
    from concourse.bass_utils import run_bass_kernel_spmd as _run

    a = {k: _np.asarray(v) for k, v in inputs.items()}
    w_in = a["w_in"][0]
    proj_cols = 7 * HEADS * P
    tiles = lambda v: v.reshape(-1, P).T
    arrays = {
        "x": a["x"][0].reshape(T, KT, P).transpose(2, 1, 0),
        "wts": weight_chunks(w_in[:, :proj_cols], a["w_out"][0], a["w_up"][0], a["w_down"][0]),
        "w_ba": w_in[:, proj_cols:].reshape(KT, P, 16).transpose(1, 0, 2),
        "norm_gains": _np.stack([tiles(a[n][0]) for n in ("ln_mix_pre", "ln_mix_post", "ln_ffn_pre", "ln_ffn_post")],
                                axis=1),
        "head_gains": _np.stack([a["sb_out_gain"][0], a["dn_out_gain"][0]], axis=1),
        "dn_conv": a["dn_conv_w"][0].reshape(4, 24, P).transpose(2, 0, 1),
        "dn_gate": _np.stack([a["dn_a_log"][0], a["dn_dt_bias"][0]], axis=1),
        "ffn_cw": a["ffn_conv_w"][0].reshape(3, 2 * FT, P).transpose(2, 0, 1),
        "ffn_cb": tiles(a["ffn_conv_b"][0]),
    }
    nc = _bacc.Bacc("TRN2", target_bir_lowering=False, num_devices=1, dynamic_dma_scratch_size=64)
    feed, args = {}, []
    for name, v in arrays.items():
        v = _np.ascontiguousarray(v)
        feed[f"in_{name}"] = v
        args.append(nc.dram_tensor(f"in_{name}", v.shape, _mybir.dt.from_np(v.dtype), kind="ExternalInput").ap())
    out = nc.dram_tensor("out_y", (P, KT, T), _mybir.dt.float32, kind="ExternalOutput").ap()
    hybrid_block_kernel(nc, *args, out)
    r = _run(nc, [feed], core_ids=[0])
    y = r.results[0]["out_y"]
    return _np.ascontiguousarray(y.transpose(2, 1, 0).reshape(1, T, D))
```

```python
from contextlib import ExitStack

import numpy as np
import concourse.bass as bass
from concourse import mybir

P = 128
T = 256
D = 2048
KT = D // P
DFF = 5632
FT = DFF // P
HEADS = 8
NJ = T // P
EPS = 1e-6
QSCALE = float(P) ** -0.5
GROUP = 4
CHUNK_K = 4
CHUNK = 2048
RAW = 4
PIECE = CHUNK // 4
RING = 8
AHEAD = 6
BATCHES = 2
BH = HEADS // BATCHES
IN_GROUPS = 14
OUT_GROUPS = 4
UP_STEPS = FT // GROUP
IN_CHUNKS = IN_GROUPS * 4
OUT_CHUNKS = OUT_GROUPS * 4
UP_CHUNKS = UP_STEPS * 8
DOWN_K = 2
DOWN_TILES = 8
HALF_CHUNKS = FT // DOWN_K
DOWN_CHUNKS = 2 * HALF_CHUNKS
CHUNKS = IN_CHUNKS + OUT_CHUNKS + UP_CHUNKS + DOWN_CHUNKS
LEVELS = 7
UNITS = BH * NJ
GROUP_TILE = [8 * r + BH * b for b in range(BATCHES) for r in range(4)] + [32 + 4 * g for g in range(6)]
PLACE = {}
for _b, _l2 in enumerate((50, 131)):
    _hd, _inv, _rec = _l2 + 9, _l2 + 23, _l2 + 57
    for _i in range(4):
        PLACE["l2", 4 * _b + _i] = _l2 + _i
        PLACE["l2b", 4 * _b + _i] = _l2 + 5 + _i
        for _n, _name in ((0, "bc"), (2, "a"), (3, "tok")):
            PLACE[_name, BH * _b + _i] = _hd + 3 * _i + _n
        PLACE["o", BH * _b + _i] = _rec + 9 + 2 * _i
        PLACE["norm", BH * _b + _i] = _rec + 11 + 2 * _i
    for _i in range(2):
        PLACE["normb", 2 * _b + _i] = _rec + 20 + 2 * _i
    for _i in range(2 * LEVELS):
        PLACE["x", 2 * LEVELS * _b + _i] = _inv + 9 * _i // 4
        PLACE["y", 2 * LEVELS * _b + _i] = _inv + 9 * _i // 4 + 3
    for _name, _n in (("u", 0), ("w", 1), ("s", 3), ("v1", 6)):
        PLACE[_name, _b] = _rec + _n


def hybrid_block_kernel(nc, x, wts, w_ba, norm_gains, head_gains, dn_conv, dn_gate, ffn_cw, ffn_cb, out):
    f32 = mybir.dt.float32
    f32r = mybir.dt.float32r
    ALU = mybir.AluOpType
    ACT = mybir.ActivationFunctionType
    ctx = ExitStack()
    with ctx:
        def sb(name, shape, dt=f32):
            return ctx.enter_context(nc.sbuf_tensor(name, shape, dt))

        def sem(name):
            return ctx.enter_context(nc.semaphore(name))

        res = sb("residual", [P, KT, T])
        raw = sb("raw", [P, RAW, CHUNK])
        w_hi = sb("w_hi", [P, RING, PIECE], f32r)
        w_lo = sb("w_lo", [P, RING, PIECE], f32r)
        half = sb("half", [P, 2, T])
        ident = sb("ident", [P, P])
        ones = sb("ones", [P, P])
        gains = sb("gains", [P, 4, KT])
        hgains = sb("hgains", [P, 2])
        dcw = sb("dcw", [P, 4, 24])
        fcw = sb("fcw", [P, 3, 2 * FT])
        fcb = sb("fcb", [P, 2 * FT])
        rstd = sb("rstd", [P, T])
        vrow = sb("vrow", [P, T])
        gate_mark = sb("gate_mark", [P, 8])
        gate, mark = gate_mark[0:8, 0:4], gate_mark[:, 4:8]
        cols = sb("cols", [P, 6, HEADS])
        ssum = sb("ssum", [P, T])
        halfs = [half[:, 0, :], half[:, 1, :], rstd[:, :], vrow[:, :]]
        base = (nc.sbuf_base + 63) // 64 * 64
        xhl = nc.alloc_sbuf_tensor_at("xhl", [P, KT, 2, T], f32r, offset=base)
        down = nc.alloc_sbuf_tensor_at("down", [P, KT, T], f32, offset=base)
        dsq = nc.alloc_sbuf_tensor_at("dsq", [P, 2, T], f32, offset=base + KT * T * 4)
        base += KT * 2 * T * 4
        room = (nc.sbuf_usable_end - base) // 4
        arena = nc.alloc_sbuf_tensor_at("arena", [P, room], f32, offset=base)
        act = nc.alloc_sbuf_tensor_at("ffn_act", [P, FT, 2, T], f32r, offset=base)
        used = [0]

        def cut(n):
            a = used[0]
            used[0] += n
            assert used[0] <= room, (used[0], room)
            return arena[:, a:a + n]

        proj = cut(56 * T).rearrange("p (n t) -> p n t", t=T)
        tmat = cut(UNITS * P).rearrange("p (u n) -> p u n", n=P)
        tmatT = cut(UNITS * P).rearrange("p (u n) -> p u n", n=P)
        ltri = cut(UNITS * P).rearrange("p (u n) -> p u n", n=P)
        qa = cut(UNITS * P).rearrange("p (u n) -> p u n", n=P)
        kb = cut(2 * T).rearrange("p (b t) -> p b t", t=T)
        dm = cut(2 * T).rearrange("p (b t) -> p b t", t=T)
        lmask = cut(LEVELS * P).rearrange("p (l n) -> p l n", n=P)
        xb = cut(2 * 4 * P).rearrange("p (b u n) -> p b u n", b=2, n=P)
        bb = cut(2 * 4 * P).rearrange("p (b u n) -> p b u n", b=2, n=P)
        rows = cut(4 * T)[0:8, :].rearrange("p (r t) -> p r t", t=T)
        sel = cut(4 * T)[0:8, :].rearrange("p (h m) -> p h m", m=P)
        nrow = cut(T)[0:8, :]
        esel = cut(8 * 8).rearrange("p (h m) -> p h m", m=8)
        osb = cut(4 * T).rearrange("p (b n) -> p b n", n=T)
        a0 = 56 * T
        full = arena[:, a0:a0 + KT * T].rearrange("p (k t) -> p k t", t=T)
        squ = full
        small = xb[0:8, :, :, :].rearrange("p b u n -> p (b u n)").rearrange("p (r t) -> p r t", t=T)
        small2 = bb[0:8, :, :, :].rearrange("p b u n -> p (b u n)").rearrange("p (r t) -> p r t", t=T)
        conv = proj[:, 52:56, :]
        mixo = arena[:, 0:KT * T].rearrange("p (n t) -> p n t", t=T)
        f0 = FT * 2 * T
        fhist = arena[:, f0:f0 + 4 * (T + 2)].rearrange("p (b t) -> p b t", b=4)
        f1 = f0 + 4 * (T + 2)
        fconv = arena[:, f1:f1 + 4 * T].rearrange("p (b t) -> p b t", b=4)
        gelu = arena[:, f1 + 4 * T:f1 + 8 * T].rearrange("p (b t) -> p b t", b=4)
        prod = arena[:, f1 + 8 * T:f1 + 10 * T].rearrange("p (b t) -> p b t", b=2)
        assert f1 + 10 * T <= room, (f1 + 10 * T, room)
        wba = arena[:, 40 * T:41 * T].rearrange("p (k n) -> p k n", n=16)

        ps = [ctx.enter_context(nc.psum_tensor(f"bank{i}", [P, 512], f32)) for i in range(8)]

        raw_full = [sem(f"raw_full{i}") for i in range(RAW)]
        hi_ready = sem("hi_ready")
        lo_ready = sem("lo_ready")
        piece_used = sem("piece_used")
        half_ready = sem("half_ready")
        bank_free = sem("bank_free")
        small_in = sem("small_in")
        x_in = sem("x_in")
        const_ready = sem("const_ready")
        out_done = sem("out_done")
        T_ = dict()

        def s(name):
            if name not in T_:
                T_[name] = sem(name)
            return T_[name]

        sums = [0]

        def square_sum(pool, step, src, k, buf, slot):
            if k == 0:
                if sums[0]:
                    pool.wait_ge(s("ss_mm"), sums[0])
                ins = pool.tensor_tensor(ssum[:, :], src[:, k, :], src[:, k, :], ALU.mult)
                sums[0] += 1
            else:
                step(pool.tensor_tensor(buf[:, slot, :], src[:, k, :], src[:, k, :], ALU.mult))
                ins = pool.tensor_tensor(ssum[:, :], ssum[:, :], buf[:, slot, :], ALU.add)
            if k == KT - 1:
                ins.then_inc(s("ss_ready"), 1)
            else:
                step(ins)

        spb = arena[:, a0:a0 + 4 * 1024].rearrange("p (b n) -> p b n", n=1024)
        SP = [spb[:, i, 0:384] for i in range(4)]
        AT = [spb[:, i, 384:768] for i in range(4)]
        VT = [spb[:, i, 768:1024] for i in range(4)]
        ZB = [ps[4], ps[5], ps[6], ps[3]]

        def l2_squares(i):
            return qa[:, 4 * (i % 2):4 * (i % 2) + 4, :].rearrange("p u n -> p (u n)")

        def l2_pair(i):
            b, r = divmod(i, 4)
            t0 = 8 * (r // 2) + BH * b + 2 * (r % 2)
            return proj[:, t0:t0 + 2, :]

        def eg(h):
            return tmat[:, h % BH, :]

        def flat(v):
            return v.rearrange("p u n -> p (u n)")

        neg_w, state = flat(tmat[:, 0:4, :]), flat(tmat[:, 4:8, :])
        v_new = [flat(ltri[:, 0:4, :]), flat(ltri[:, 4:8, :])]

        def flat_t(v):
            return v.rearrange("p n t -> p (n t)")

        block = ctx.enter_context(nc.Block())
        x_v = x
        NX = 4

        @block.sync
        def _(sp):
            for q in range(NX):
                sp.dma_start(res[:, 4 * q:4 * q + 4, :], x_v[:, 4 * q:4 * q + 4, :]).then_inc(s(f"x_in{q}"), 16)
            for slot in range(RAW):
                sp.dma_start(raw[:, slot, :], wts[slot, :, :]).then_inc(raw_full[slot], 16)
            with sp.Fori(1, CHUNKS // RAW) as i:
                for slot in range(RAW):
                    sp.wait_ge(lo_ready, i * (4 * RAW) + 4 * (slot + 1 - RAW))
                    sp.dma_start(raw[:, slot, :], wts[bass.ds(i * RAW + slot, 1), :, :].rearrange("a p n -> p (a n)")
                                 ).then_inc(raw_full[slot], 16)
            sp.wait_ge(s("y_ready"), KT)
            for q in range(4):
                sp.dma_start(out[:, 4 * q:4 * q + 4, :], res[:, 4 * q:4 * q + 4, :]).then_inc(out_done, 16)
            sp.wait_ge(out_done, 64)

        @block.gpsimd
        def _(pool):
            n = [0]

            def step(ins):
                n[0] += 1
                ins.then_inc(s("pool_step"), 1)
                pool.wait_ge(s("pool_step"), n[0])

            pool.memset(ones[:, :], 1.0).then_inc(const_ready, 1)
            step(pool.memset(ident[:, :], 0.0))
            pool.affine_select(out=ident[:, :], in_=ident[:, :], compare_op=ALU.not_equal, fill=1.0, base=0,
                               pattern=[[-1, P]], channel_multiplier=1).then_inc(const_ready, 1)
            step(pool.memset(sel[:, :, :], 1.0))
            pool.affine_select(out=sel[:, :, :], in_=sel[:, :, :], compare_op=ALU.is_equal, fill=0.0, base=0,
                               pattern=[[-1, HEADS], [0, P]], channel_multiplier=1).then_inc(s("sel_ready"), 1)
            step(pool.memset(esel[:, :, :], 1.0))
            pool.affine_select(out=esel[:, :, :], in_=esel[:, :, :], compare_op=ALU.is_equal, fill=0.0, base=0,
                               pattern=[[-1, 8], [1, 8]], channel_multiplier=0).then_inc(s("sel_ready"), 1)
            for lv in range(LEVELS):
                w = 1 << lv
                na = P // (2 * w)
                m = lmask[:, lv, :].rearrange("p (a b r) -> p a b r", b=2, r=w)
                step(pool.memset(lmask[:, lv, :], 1.0))
                step(pool.affine_select(out=m, in_=m, compare_op=ALU.is_ge, fill=0.0, base=-1,
                                        pattern=[[0, na], [1, 2], [0, w]], channel_multiplier=0))
                step(pool.affine_select(out=m, in_=m, compare_op=ALU.is_ge, fill=0.0, base=0,
                                        pattern=[[-2 * w, na], [0, 2], [0, w]], channel_multiplier=1))
                pool.affine_select(out=m, in_=m, compare_op=ALU.is_ge, fill=0.0, base=w - 1,
                                   pattern=[[2 * w, na], [0, 2], [0, w]], channel_multiplier=-1
                                   ).then_inc(s("lmask_ready"), 1)
            for k in range(KT):
                pool.wait_ge(s("xn_hi"), k + 1)
                pool.tensor_tensor(xhl[:, k, 1, :], full[:, k, :], xhl[:, k, 0, :].bitcast(f32), ALU.subtract
                                   ).then_inc(s("xn_lo"), 1)
            for b in range(BATCHES):
                for i in range(4 * b, 4 * b + 4):
                    pool.wait_ge(s("silu_done"), 4 * b + 1 + (i % 4) // 2)
                    if i % 4 >= 2:
                        pool.wait_ge(s("l2_mm"), i - 1)
                    elif b:
                        pool.wait_ge(s("o_mm"), BH)
                    else:
                        pool.wait_ge(s("xn_lo"), KT)
                        pool.wait_ge(s("ba_done"), 1)
                    pool.tensor_tensor(l2_squares(i).rearrange("p (a t) -> p a t", t=T), l2_pair(i), l2_pair(i),
                                       ALU.mult).then_inc(s("qk_sq"), 1)
                for h in range(BH * b, BH * b + BH):
                    pool.wait_ge(s("dexp"), h + 1)
                    d = dm[:, h % 2, :].rearrange("p (j c) -> p j c", j=2)
                    pool.affine_select(out=d, in_=d, compare_op=ALU.is_ge, fill=0.0, base=0,
                                       pattern=[[0, 2], [1, P]], channel_multiplier=-1).then_inc(s("dmask"), 1)
            pool.wait_ge(bank_free, 4 + 4 * (8 + HEADS // GROUP))
            for h in range(HEADS):
                pool.tensor_scalar(proj[:, 32 + h, :], proj[:, 32 + h, :], QSCALE, 0.0, ALU.mult, ALU.add
                                   ).then_inc(s("sbq"), 1)
            pool.wait_ge(s("dn_done"), 1)
            step(pool.memset(xb[:, 0, 0, :], -1.0))
            pool.memset(xb[:, 0, 1, :], -1.0).then_inc(s("tri_ready"), 1)
            pool.affine_select(out=xb[:, 0, 0, :], in_=xb[:, 0, 0, :], compare_op=ALU.is_ge, fill=0.0, base=0,
                               pattern=[[-1, P]], channel_multiplier=1).then_inc(s("tri_ready"), 1)
            for t in range(HEADS + 2):
                if t < HEADS:
                    pool.wait_ge(s("sp_ready"), t + 1)
                    for lot in (0, 2 * P):
                        v = SP[t % 4][:, lot:lot + P]
                        ins = pool.affine_select(out=v, in_=v, compare_op=ALU.is_ge, fill=0.0, base=-1,
                                                 pattern=[[1, P]], channel_multiplier=-1)
                    ins.then_inc(s("sp_mask"), 1)
                if t >= 2:
                    pool.wait_ge(s("att_exp"), t - 1)
                    for lot in (0, 2 * P):
                        v = AT[(t - 2) % 4][:, lot:lot + P]
                        ins = pool.affine_select(out=v, in_=v, compare_op=ALU.is_ge, fill=0.0, base=-1,
                                                 pattern=[[1, P]], channel_multiplier=-1)
                    ins.then_inc(s("att_mask"), 1)
            for k in range(KT):
                pool.wait_ge(s("mixo_tile"), k + 1)
                square_sum(pool, step, mixo, k, squ[:, 0:2, :], k % 2)
            for k in range(KT):
                pool.wait_ge(s("h_tile"), k + 1)
                square_sum(pool, step, res, k, squ[:, 0:2, :], k % 2)
            for k in range(KT):
                pool.wait_ge(s("hn_hi"), k + 1)
                pool.tensor_tensor(xhl[:, k, 1, :], full[:, k, :], xhl[:, k, 0, :].bitcast(f32), ALU.subtract
                                   ).then_inc(s("hn_lo"), 1)
            pool.wait_ge(s("hn_f"), KT)
            pool.memset(fhist[:, :, 0:2], 0.0).then_inc(s("fhist_ready"), 1)
            with pool.Fori(0, UP_STEPS) as i:
                for q in range(GROUP):
                    pool.wait_ge(s("act_hi"), i * 4 + (q + 1))
                    pool.tensor_tensor(act[:, bass.ds(i * 4 + q, 1), 1, :].rearrange("p a t -> p (a t)"),
                                       prod[:, q % 2, :],
                                       act[:, bass.ds(i * 4 + q, 1), 0, :].rearrange("p a t -> p (a t)").bitcast(f32),
                                       ALU.subtract).then_inc(s("act_lo"), 1)
            for k in range(KT):
                pool.wait_ge(s("down_tile"), k + 1)
                square_sum(pool, step, down, k, dsq, k % 2)

        @block.scalar
        def _(act_e):
            def split(g, i):
                slot, quarter = (i // 4) % RAW, i % 4
                if quarter == 0:
                    act_e.wait_ge(raw_full[slot], (g + i // 16) * 16 + 16)
                act_e.wait_ge(piece_used, g * 16 + (i + 1))
                nc.scalar.activation(w_hi[:, i % RING, :], raw[:, slot, quarter * PIECE:(quarter + 1) * PIECE], ACT.Copy
                                     ).then_inc(hi_ready, 1)

            def halves(n, j, b, used):
                act_e.wait_ge(piece_used, used)
                act_e.wait_ge(bank_free, n + 1)
                nc.scalar.activation(halfs[j % 4], ps[b][:, T:2 * T], ACT.Copy).then_inc(half_ready, 1)

            def group_halves(g, j):
                halves(g * 4 + j, j, j, g * 16 + (RING + 12 + j + 1))

            def slots(g, a, b):
                for r in range(a, b):
                    if r < 16:
                        split(g, AHEAD + r)
                    if r >= 13:
                        group_halves(g, r - 13)

            act_e.dma_start(gains[:, :, :], norm_gains).then_inc(small_in, 16)
            act_e.dma_start(hgains[:, :], head_gains).then_inc(small_in, 16)
            act_e.dma_start(dcw[:, :, :], dn_conv).then_inc(small_in, 16)
            act_e.dma_start(gate[:, 0:2], dn_gate).then_inc(small_in, 16)
            act_e.dma_start(fcw[:, :, :], ffn_cw).then_inc(small_in, 16)
            act_e.dma_start(fcb[:, :], ffn_cb).then_inc(small_in, 16)
            act_e.dma_start(wba[:, :, :], w_ba).then_inc(small_in, 16)

            for q in range(NX):
                act_e.wait_ge(s(f"x_in{q}"), 16)
                nc.scalar.activation(proj[:, 4 * q:4 * q + 4, :], res[:, 4 * q:4 * q + 4, :], ACT.Square
                                     ).then_inc(s("x_sq"), 1)
            act_e.wait_ge(s("x_inv"), 1)
            nc.scalar.activation(rstd[:, :], vrow[:, :], ACT.Sqrt).then_inc(s("x_rstd"), 1)
            for k in range(KT):
                act_e.wait_ge(s("xn_f"), k + 1)
                nc.scalar.activation(xhl[:, k, 0, :], full[:, k, :], ACT.Copy).then_inc(s("xn_hi"), 1)
            for i in range(AHEAD):
                split(0, i)
            at = [-1]

            def follow(place):
                while at[0] < place:
                    at[0] += 1
                    p = at[0]
                    g, r = divmod(p, 16)
                    if p < 16 * IN_GROUPS:
                        split(g, AHEAD + r)
                    if (p - 13) % 16 < GROUP and 13 <= p < 16 * IN_GROUPS + 1:
                        group_halves((p - 13) // 16, (p - 13) % 16)
                    if r == 10 and 1 <= g <= 8:
                        t0 = GROUP_TILE[g - 1]
                        if g % 4:
                            act_e.wait_ge(s("conv_done"), 4 * (g - 1 - (g - 1) // 4) + 4)
                            src = conv[:, :, :]
                        else:
                            act_e.wait_ge(bank_free, 4 * g + 4)
                            src = proj[:, t0:t0 + 4, :]
                        nc.scalar.activation(proj[:, t0:t0 + 4, :], src, ACT.Silu).then_inc(s("silu_done"), 1)

            follow(0)
            n = [0]

            def step(ins):
                n[0] += 1
                ins.then_inc(s("act_step"), 1)
                act_e.wait_ge(s("act_step"), n[0])
            act_e.wait_ge(s("ba_done"), 1)
            nc.scalar.activation(small[:, 0, :], ps[4][0:8, 0:T], ACT.Exp, scale=-1.0).then_inc(s("eb"), 1)
            step(nc.scalar.activation(small[:, 1, :], ps[5][0:8, 0:T], ACT.Identity, bias=gate[:, 1:2]))
            step(nc.scalar.activation(small[:, 2, :], small[:, 1, :], ACT.Abs))
            step(nc.scalar.activation(small[:, 3, :], small[:, 2, :], ACT.Exp, scale=-1.0))
            nc.scalar.activation(gate[:, 2:3], gate[:, 0:1], ACT.Exp).then_inc(s("ga"), 1)
            nc.scalar.activation(small2[:, 0, :], small[:, 3, :], ACT.Ln, bias=1.0).then_inc(s("ga"), 1)
            follow(4)
            act_e.wait_ge(s("gc_ready"), 2)
            nc.scalar.activation(small2[:, 1, :], rows[:, 1, :], ACT.Exp).then_inc(s("eg_row"), 1)
            nc.scalar.activation(rows[:, 3, 0:P], rows[:, 1, 0:P], ACT.Exp, scale=-1.0, bias=rows[:, 1, P - 1:P]
                                 ).then_inc(s("ke_row"), 1)
            for b in range(BATCHES):
                heads = range(BH * b, BH * b + BH)
                follow(PLACE["l2", 4 * b + 3] + 2)
                act_e.wait_ge(s("l2_inv"), b + 1)
                nc.scalar.activation(nrow, nrow, ACT.Sqrt).then_inc(s("l2_rstd"), 1)
                for h in heads:
                    follow(PLACE["bc", h] + 1)
                    act_e.wait_ge(s("ddiff"), h + 1)
                    nc.scalar.activation(dm[:, h % 2, :], dm[:, h % 2, :], ACT.Exp).then_inc(s("dexp"), 1)
                    nc.scalar.activation(eg(h), ps[4 + h % 2][:, T + P:2 * T], ACT.Exp).then_inc(s("eg_ready"), 1)
                for i in range(2 * LEVELS * b, 2 * LEVELS * (b + 1)):
                    follow(PLACE["x", i] + 1)
                    act_e.wait_ge(s("x_mm"), i + 1)
                    if i >= 2:
                        act_e.wait_ge(s("y_mm"), i - 1)
                    nc.scalar.activation(xb[:, i % 2, :, :], ps[4][:, :] if i % 2 == 0 else ps[5][:, :], ACT.Copy
                                         ).then_inc(s("x_sb"), 1)
                follow(PLACE["w", b] + 1)
                act_e.wait_ge(s("w_mm"), b + 1)
                nc.scalar.activation(neg_w, ps[5][:, :], ACT.Copy, scale=-1.0).then_inc(s("w_sb"), 1)
                follow(PLACE["s", b] + 1)
                act_e.wait_ge(s("s_mm"), b + 1)
                nc.scalar.activation(state, ps[6][:, :], ACT.Copy).then_inc(s("s_sb"), 1)
                for h in heads:
                    follow(PLACE["o", h] + 1)
                    act_e.wait_ge(s("o_mm"), h + 1)
                    if h >= 4:
                        act_e.wait_ge(s("on_mm"), h - 3)
                    nc.scalar.activation(osb[:, h % 4, :], ps[4 + h % 2][:, 0:T], ACT.Square).then_inc(s("o_sq"), 1)
                    nc.scalar.activation(proj[:, h, :], ps[4 + h % 2][:, 0:T], ACT.Copy).then_inc(s("o_sb"), 1)
                follow(PLACE["norm", BH * b + 3] + 2)
                act_e.wait_ge(s("on_inv"), b + 1)
                nc.scalar.activation(nrow, nrow, ACT.Sqrt).then_inc(s("on_rstd"), 1)
            follow(16 * IN_GROUPS + 1)
            act_e.wait_ge(s("mixd_f"), HEADS // 2)
            act_e.wait_ge(piece_used, 4 * IN_CHUNKS + RING)
            nc.scalar.activation(xhl[:, HEADS:2 * HEADS, 0, :], proj[:, 0:HEADS, :], ACT.Copy).then_inc(s("mixd_hi"), 1)
            for t in range(HEADS + 3):
                if t < HEADS:
                    act_e.wait_ge(s("z_mm"), t + 1)
                    if t >= 4:
                        act_e.wait_ge(s("c_mm"), t - 3)
                    step(nc.scalar.activation(SP[t % 4], ZB[t % 4][:, 0:384], ACT.Abs))
                    step(nc.scalar.activation(SP[t % 4], SP[t % 4], ACT.Exp, scale=-1.0))
                    nc.scalar.activation(SP[t % 4], SP[t % 4], ACT.Ln, bias=1.0).then_inc(s("ln_ready"), 1)
                if 2 <= t < HEADS + 2:
                    g = t - 2
                    act_e.wait_ge(s("c_mm"), g + 1)
                    if g >= 4:
                        act_e.wait_ge(s("av_mm"), g - 3)
                    nc.scalar.activation(AT[g % 4], ZB[g % 4][:, 0:384], ACT.Exp).then_inc(s("att_exp"), 1)
                if t >= 3:
                    g = t - 3
                    act_e.wait_ge(s("so_sb"), g + 1)
                    if g >= 4:
                        act_e.wait_ge(s("son_mm"), g - 3)
                    nc.scalar.activation(osb[:, g % 4, :], proj[:, 32 + g, :], ACT.Square).then_inc(s("so_sq"), 1)
            act_e.wait_ge(s("son_inv"), 1)
            nc.scalar.activation(nrow, nrow, ACT.Sqrt).then_inc(s("son_rstd"), 1)
            for i in range(HEADS // 2):
                act_e.wait_ge(s("mixs_f"), i + 1)
                nc.scalar.activation(xhl[:, 2 * i:2 * i + 2, 0, :], proj[:, 32 + 2 * i:34 + 2 * i, :], ACT.Copy
                                     ).then_inc(s("mixs_hi"), 1)

            with act_e.Fori(IN_GROUPS, IN_GROUPS + OUT_GROUPS) as g:
                slots(g, 0, 17)
            for stage, (inv, rs) in enumerate((("m_inv", "m_rstd"), ("h_inv", "h_rstd"))):
                act_e.wait_ge(s(inv), 1)
                nc.scalar.activation(rstd[:, :], vrow[:, :], ACT.Sqrt).then_inc(s(rs), 1)
            for k in range(KT):
                act_e.wait_ge(s("hn_f"), k + 1)
                nc.scalar.activation(xhl[:, k, 0, :], full[:, k, :], ACT.Copy).then_inc(s("hn_hi"), 1)

            UC = IN_CHUNKS + OUT_CHUNKS

            def gelu_tile(i, q):
                act_e.wait_ge(s("fconv_step"), i * 24 + (3 * q + 3))
                act_e.wait_ge(s("prod_ready"), i * 4 + (q + 1))
                nc.scalar.activation(gelu[:, q, :], fconv[:, q % 2, :], ACT.Gelu_apprx_tanh
                                     ).then_inc(s("gelu_done"), 1)

            def act_hi(i, q):
                act_e.wait_ge(s("prod_ready"), i * 4 + (q + 5))
                nc.scalar.activation(act[:, bass.ds(i * 4 + q, 1), 0, :].rearrange("p a t -> p (a t)"),
                                     prod[:, q % 2, :], ACT.Copy).then_inc(s("act_hi"), 1)

            def with_work(g, work):
                slots(g, 0, 6)
                work(0)
                slots(g, 6, 9)
                work(1)
                slots(g, 9, 12)
                work(2)
                slots(g, 12, 15)
                work(3)
                slots(g, 15, 17)

            def gate_slots(i, g):
                with_work(g, lambda q: gelu_tile(i, q))

            UG = UC // 4
            slots(UG, 0, 17)
            with act_e.Fori(0, UP_STEPS - 1) as i:
                gate_slots(i, i * 2 + (UG + 1))
                with_work(i * 2 + (UG + 2), lambda q: act_hi(i, q))
            gate_slots(UP_STEPS - 1, UG + 2 * UP_STEPS - 1)
            DC = UC + UP_CHUNKS
            for q in range(GROUP):
                for r in range(0 if q == 0 else 3 * q + 3, 3 * q + 6):
                    split(DC // 4, AHEAD + r)
                act_hi(UP_STEPS - 1, q)
            for hf in range(2):
                c = DC + hf * HALF_CHUNKS
                p0 = 4 * c + AHEAD + (15 if hf == 0 else 0)
                p1 = min(4 * (c + HALF_CHUNKS) + AHEAD, 4 * CHUNKS)
                p2 = min((p0 + 15) // 16 * 16, p1)
                for p in range(p0, p2):
                    split(p // 16, p % 16)
                with act_e.Fori(p2 // 16, p1 // 16) as r:
                    for i in range(16):
                        split(r, i)
                for p in range(p1 // 16 * 16, p1):
                    split(p // 16, p % 16)
                for j in range(DOWN_TILES):
                    halves(DC + hf * DOWN_TILES + j, j, j, RING + 4 * (c + HALF_CHUNKS - 1) + j // 2 + 1)
            act_e.wait_ge(s("f_inv"), 1)
            nc.scalar.activation(rstd[:, :], vrow[:, :], ACT.Sqrt).then_inc(s("f_rstd"), 1)

        @block.vector
        def _(dve):
            V = nc.vector
            n = [0]

            def step(ins):
                n[0] += 1
                ins.then_inc(s("dve_step"), 1)
                dve.wait_ge(s("dve_step"), n[0])

            def split(g, i):
                slot, quarter = (i // 4) % RAW, i % 4
                dve.wait_ge(hi_ready, g * 16 + (i + 1))
                V.tensor_tensor(w_lo[:, i % RING, :], raw[:, slot, quarter * PIECE:(quarter + 1) * PIECE],
                                w_hi[:, i % RING, :].bitcast(f32), ALU.subtract).then_inc(lo_ready, 1)

            def added(n_, j, b, out_):
                dve.wait_ge(half_ready, n_ + 1)
                return V.tensor_tensor(out_, ps[b][:, 0:T], halfs[j % 4], ALU.add).then_inc(bank_free, 1)

            V.memset(mark[:, 0:1], 0.0).then_inc(bank_free, 4)
            V.memset(mark[:, 1:2], 0.0).then_inc(piece_used, RING)
            dve.wait_ge(s("x_sq"), NX)
            V.tensor_reduce(ssum[:, :], proj[:, 0:KT, :].rearrange("p k t -> p t k"), mybir.AxisListType.X, ALU.add
                            ).then_inc(s("x_ss"), 1)
            dve.wait_ge(s("xsum_mm"), 1)
            step(V.tensor_scalar(vrow[:, :], ps[4][:, 0:T], 1.0 / D, EPS, ALU.mult, ALU.add))
            V.reciprocal(vrow[:, :], vrow[:, :]).then_inc(s("x_inv"), 1)
            dve.wait_ge(small_in, 16 * 7)
            dve.wait_ge(s("x_rstd"), 1)
            for k in range(KT):
                V.scalar_tensor_tensor(full[:, k, :], res[:, k, :], gains[:, 0, k:k + 1], rstd[:, :], ALU.mult, ALU.mult
                                       ).then_inc(s("xn_f"), 1)
            for i in range(AHEAD):
                split(0, i)
            at = [-1]

            def conv_tile(g, j):
                n_ = 4 * (g - g // 4) + j
                t = GROUP_TILE[g] + j
                dve.wait_ge(bank_free, 4 * g + j + 5)
                if g:
                    dve.wait_ge(s("silu_done"), g)
                for tap in range(4):
                    lag = tap
                    w = dcw[:, 3 - lag, t:t + 1]
                    if lag:
                        dve.wait_ge(s("conv_step"), 3 * n_ + lag)
                        ins = V.scalar_tensor_tensor(conv[:, j, lag:T], proj[:, t, 0:T - lag], w, conv[:, j, lag:T],
                                                     ALU.mult, ALU.add)
                    else:
                        ins = V.tensor_scalar(conv[:, j, :], proj[:, t, :], w, None, ALU.mult)
                    ins.then_inc(s("conv_done") if lag == 3 else s("conv_step"), 1)

            def follow(place):
                while at[0] < place:
                    at[0] += 1
                    p = at[0]
                    g, r = divmod(p, 16)
                    if p < 16 * IN_GROUPS:
                        split(g, AHEAD + r)
                    if (p - 13) % 16 < GROUP and 13 <= p < 16 * IN_GROUPS + 1:
                        g_, j = divmod(p - 13, 16)
                        if g_ == IN_GROUPS - 1 and j == 0:
                            dve.wait_ge(s("silu_done"), 8)
                        added(4 * g_ + j, j, j, proj[:, GROUP_TILE[g_] + j, :])
                    if r in (1, 3, 5, 7) and 1 <= g <= 7 and g != 4:
                        conv_tile(g - 1, r // 2)

            follow(0)
            dve.wait_ge(s("eb"), 1)
            step(V.tensor_scalar(small[:, 0, :], small[:, 0, :], 1.0, None, ALU.add))
            step(V.reciprocal(rows[:, 0, :], small[:, 0, :]))
            dve.wait_ge(s("ga"), 2)
            step(V.scalar_tensor_tensor(small[:, 1, :], small[:, 1, :], 0.0, small2[:, 0, :], ALU.max, ALU.add))
            step(V.tensor_scalar(small[:, 1, :], small[:, 1, :], gate[:, 2:3], -1.0, ALU.mult, ALU.mult))
            step(V.memset(small[:, 2, :], 1.0))
            for j in range(NJ):
                V.tensor_tensor_scan(rows[:, 1, j * P:(j + 1) * P], small[:, 2, 0:P], small[:, 1, j * P:(j + 1) * P],
                                     0.0, ALU.mult, ALU.add).then_inc(s("gc_ready"), 1)
            dve.wait_ge(s("eg_row"), 1)
            V.tensor_tensor(rows[:, 2, :], rows[:, 0, :], small2[:, 1, :], ALU.mult).then_inc(s("bg_row"), 1)
            follow(11)
            dve.wait_ge(s("cols_mm"), 1)
            V.tensor_copy(cols[:, :, :].rearrange("p r h -> p (r h)"), ps[6][:, 0:48]).then_inc(s("cols_sb"), 1)
            for batch in range(BATCHES):
                follow(PLACE["l2", 4 * batch + 3] + 1)
                dve.wait_ge(s("l2_mm"), 4 * batch + 4)
                step(V.tensor_scalar(nrow, ps[4][0:8, 0:T], EPS, None, ALU.add))
                V.reciprocal(nrow, nrow).then_inc(s("l2_inv"), 1)
                for i in range(4 * batch, 4 * batch + 4):
                    follow(PLACE["l2b", i] + 1)
                    dve.wait_ge(s("l2_bc"), i + 1)
                    V.scalar_tensor_tensor(l2_pair(i), l2_pair(i), QSCALE if i % 4 < 2 else 1.0,
                                           ps[4 + i % 2][:, :].rearrange("p (a t) -> p a t", t=T), ALU.mult, ALU.mult
                                           ).then_inc(s("l2_done"), 1)
                for h in range(BH * batch, BH * batch + BH):
                    b = h % 2
                    u = 2 * (h % BH)
                    follow(PLACE["bc", h] + 1)
                    dve.wait_ge(s("bc_mm"), h + 1)
                    if h >= 2:
                        dve.wait_ge(s("a_mm"), h - 1)
                    V.tensor_tensor(kb[:, b, :], proj[:, 8 + h, :], ps[4 + b][:, 0:T], ALU.mult
                                    ).then_inc(s("kb_ready"), 1)
                    for j in range(NJ):
                        ins = V.tensor_scalar(dm[:, b, j * P:(j + 1) * P], ps[4 + b][:, T + j * P:T + (j + 1) * P],
                                              cols[:, j, h:h + 1], 0.0, ALU.subtract, ALU.min)
                    ins.then_inc(s("ddiff"), 1)
                    follow(PLACE["a", h] + 1)
                    dve.wait_ge(s("a_mm"), h + 1)
                    dve.wait_ge(s("dmask"), h + 1)
                    d = dm[:, b, :].rearrange("p (j c) -> p j c", j=2)
                    a = ps[6 + b][:, :].rearrange("p (j x c) -> p j x c", j=2, x=2)
                    V.tensor_tensor(ltri[:, u:u + 2, :], a[:, :, 0, :], d, ALU.mult)
                    V.tensor_tensor(qa[:, u:u + 2, :], a[:, :, 1, :], d, ALU.mult)
                    dve.wait_ge(s("eg_ready"), h + 1)
                    V.tensor_tensor(proj[:, h, P:T], proj[:, h, P:T], eg(h), ALU.mult).then_inc(s("qd_ready"), 1)
                    follow(PLACE["tok", h] + 1)
                    dve.wait_ge(s("tok_mm"), h + 1)
                    tp = ps[6 + b]
                    for j in range(NJ):
                        V.tensor_scalar(proj[:, 16 + h, j * P:(j + 1) * P], tp[:, j * P:(j + 1) * P],
                                        cols[:, 2 + j, h:h + 1], None, ALU.mult)
                    V.tensor_scalar(proj[:, 8 + h, 0:P], tp[:, T:T + P], cols[:, 5, h:h + 1], None, ALU.mult)
                    V.tensor_scalar(proj[:, 8 + h, P:T], tp[:, T + P:2 * T], cols[:, 4, h:h + 1], None, ALU.mult
                                    ).then_inc(s("tok_sb"), 1)
                eye = ident[:, :].rearrange("p (a c) -> p a c", a=1).to_broadcast([P, UNITS, P])
                V.tensor_copy(tmat[:, :, :], eye)
                V.tensor_copy(tmatT[:, :, :], eye).then_inc(s("t_init"), 1)
                dve.wait_ge(s("lmask_ready"), LEVELS)
                dve.wait_ge(s("tok_sb"), BH * (batch + 1))
                dve.wait_ge(s("t_init"), batch + 1)
                i0 = 2 * LEVELS * batch

                def level_b(i):
                    lv, g = divmod(i - i0, 2)
                    if i >= 2:
                        dve.wait_ge(s("x_mm"), i - 1)
                    m = lmask[:, lv, :].rearrange("p (a c) -> p a c", a=1).to_broadcast([P, 4, P])
                    V.tensor_tensor(bb[:, g, :, :], ltri[:, 4 * g:4 * g + 4, :], m, ALU.mult).then_inc(s("b_ready"), 1)

                level_b(i0)
                level_b(i0 + 1)
                follow(PLACE["x", i0] + 1)
                level_b(i0 + 2)
                for i in range(i0, i0 + 2 * LEVELS):
                    g = i % 2
                    follow(PLACE["y", i] + 1)
                    dve.wait_ge(s("y_mm"), i + 1)
                    for t_, bank in ((tmat, 6), (tmatT, 7)):
                        if t_ is tmat and i - i0 >= 2 * (LEVELS - 1):
                            continue
                        v = flat(t_[:, 4 * g:4 * g + 4, :])
                        ins = V.tensor_tensor(v, v, ps[bank][:, :], ALU.subtract)
                    ins.then_inc(s("t_ready"), 1)
                    if i + 3 < i0 + 2 * LEVELS:
                        level_b(i + 3)
                follow(PLACE["u", batch] + 1)
                dve.wait_ge(s("u_mm"), batch + 1)
                V.tensor_copy(v_new[0], ps[4][:, :]).then_inc(s("v0_sb"), 1)
                follow(PLACE["v1", batch] + 1)
                dve.wait_ge(s("v1_mm"), batch + 1)
                V.tensor_copy(v_new[1], ps[7][:, :]).then_inc(s("v1_sb"), 1)
                follow(PLACE["norm", BH * batch + BH - 1] + 1)
                dve.wait_ge(s("on_mm"), BH * (batch + 1))
                step(V.tensor_scalar(nrow, ps[6][0:8, 0:T], 1.0 / P, EPS, ALU.mult, ALU.add))
                V.reciprocal(nrow, nrow).then_inc(s("on_inv"), 1)
                for i in range(2 * batch, 2 * batch + 2):
                    follow(PLACE["normb", i] + 1)
                    dve.wait_ge(s("on_bc"), i + 1)
                    dve.wait_ge(s("o_sb"), 2 * i + 2)
                    o = flat_t(proj[:, 2 * i:2 * i + 2, :])
                    V.scalar_tensor_tensor(o, o, hgains[:, 1:2], ps[6 + i % 2][:, :], ALU.mult, ALU.mult
                                           ).then_inc(s("mixd_n"), 1)
                    dve.wait_ge(s("mixd_n"), i + 1)
                    V.tensor_tensor(o, o, flat_t(proj[:, 24 + 2 * i:26 + 2 * i, :]), ALU.mult).then_inc(s("mixd_f"), 1)
            follow(16 * IN_GROUPS + 1)
            V.memset(mark[:, 0:1], 0.0).then_inc(s("dn_done"), 1)
            dve.wait_ge(s("mixd_hi"), 1)
            V.tensor_tensor(xhl[:, HEADS:2 * HEADS, 1, :], proj[:, 0:HEADS, :],
                            xhl[:, HEADS:2 * HEADS, 0, :].bitcast(f32), ALU.subtract).then_inc(s("mix_lo"), 1)
            for t in range(HEADS + 3):
                if t < HEADS:
                    dve.wait_ge(s("vt_mm"), t + 1)
                    if t >= 4:
                        dve.wait_ge(s("av_mm"), t - 3)
                    V.tensor_copy(VT[t % 4], ps[7][:, 0:T]).then_inc(s("vt_sb"), 1)
                    dve.wait_ge(s("ln_ready"), t + 1)
                    V.scalar_tensor_tensor(SP[t % 4], ZB[t % 4][:, 0:384], 0.0, SP[t % 4], ALU.max, ALU.add
                                           ).then_inc(s("sp_ready"), 1)
                if t >= 3:
                    g = t - 3
                    dve.wait_ge(s("av_mm"), g + 1)
                    V.tensor_copy(proj[:, 32 + g, :], ps[g % 2][:, 0:T]).then_inc(s("so_sb"), 1)
            dve.wait_ge(s("son_mm"), HEADS)
            step(V.tensor_scalar(nrow, ps[2][0:8, 0:T], 1.0 / P, EPS, ALU.mult, ALU.add))
            V.reciprocal(nrow, nrow).then_inc(s("son_inv"), 1)
            for i in range(HEADS // 2 + 1):
                if i < HEADS // 2:
                    dve.wait_ge(s("son_bc"), i + 1)
                    dve.wait_ge(s("so_sb"), HEADS)
                    o = flat_t(proj[:, 32 + 2 * i:34 + 2 * i, :])
                    V.scalar_tensor_tensor(o, o, hgains[:, 0:1], ps[4 + i][:, :], ALU.mult, ALU.mult
                                           ).then_inc(s("mixs_f"), 1)
                if i:
                    dve.wait_ge(s("mixs_hi"), i)
                    V.tensor_tensor(xhl[:, 2 * i - 2:2 * i, 1, :], proj[:, 30 + 2 * i:32 + 2 * i, :],
                                    xhl[:, 2 * i - 2:2 * i, 0, :].bitcast(f32), ALU.subtract).then_inc(s("mix_lo"), 1)

            with dve.Fori(IN_GROUPS, IN_GROUPS + OUT_GROUPS) as g:
                for r in range(13):
                    split(g, AHEAD + r)
                for j in range(GROUP):
                    if j:
                        split(g, AHEAD + 12 + j)
                    dve.wait_ge(half_ready, g * 4 + (j + 1))
                    V.tensor_tensor(mixo[:, bass.ds(g * 4 + (j - 4 * IN_GROUPS), 1), :].rearrange("p a t -> p (a t)"),
                                    ps[j][:, 0:T], halfs[j % 4], ALU.add).then_inc(bank_free, 1)
                    dve.wait_ge(bank_free, g * 4 + (j + 5))
                    V.memset(mark[:, 0:1], 0.0).then_inc(s("mixo_tile"), 1)

            def inverse(idx, name, bank):
                dve.wait_ge(s("ss_mm"), idx)
                step(V.tensor_scalar(vrow[:, :], ps[bank][:, 0:T], 1.0 / D, EPS, ALU.mult, ALU.add))
                V.reciprocal(vrow[:, :], vrow[:, :]).then_inc(s(name), 1)

            inverse(1, "m_inv", 4)
            dve.wait_ge(s("m_rstd"), 1)
            for k in range(KT):
                step(V.scalar_tensor_tensor(mixo[:, k, :], mixo[:, k, :], gains[:, 1, k:k + 1], rstd[:, :],
                                            ALU.mult, ALU.mult))
                V.tensor_tensor(res[:, k, :], res[:, k, :], mixo[:, k, :], ALU.add).then_inc(s("h_tile"), 1)
            inverse(2, "h_inv", 4)
            dve.wait_ge(s("h_rstd"), 1)
            for k in range(KT):
                V.scalar_tensor_tensor(full[:, k, :], res[:, k, :], gains[:, 2, k:k + 1], rstd[:, :], ALU.mult, ALU.mult
                                       ).then_inc(s("hn_f"), 1)
            dve.wait_ge(s("fhist_ready"), 1)
            dve.wait_ge(s("hn_lo"), KT)
            UC = IN_CHUNKS + OUT_CHUNKS

            def ffn_conv(i, part, q):
                b = 2 * part + q % 2
                if part == 0:
                    dve.wait_ge(s("gelu_done"), i * 4 + (q + 1))
                else:
                    dve.wait_ge(s("prod_ready"), i * 4 + (q + 3))
                col = bass.ds(i * 4 + (part * FT + q), 1)
                for k in range(3):
                    src = fhist[:, q, k:k + T]
                    if k == 0:
                        ins = V.tensor_scalar(fconv[:, b, :], src, fcw[:, 0, col], fcb[:, col], ALU.mult, ALU.add)
                    else:
                        dve.wait_ge(s("fconv_step"), i * 24 + (12 * part + 3 * q + k))
                        ins = V.scalar_tensor_tensor(fconv[:, b, :], src, fcw[:, k, col], fconv[:, b, :],
                                                     ALU.mult, ALU.add)
                    ins.then_inc(s("fconv_step"), 1)

            def value_tile(i, q):
                ffn_conv(i, 1, q)
                dve.wait_ge(s("fconv_step"), i * 24 + (12 + 3 * q + 3))
                dve.wait_ge(s("gelu_done"), i * 4 + (q + 3))
                dve.wait_ge(s("act_lo"), i * 4 + (q + 1))
                V.tensor_tensor(prod[:, q % 2, :], gelu[:, q, :], fconv[:, 2 + q % 2, :], ALU.mult
                                ).then_inc(s("prod_ready"), 1)

            def up_group(g, work, steps):
                for q in range(GROUP):
                    for r in range(3 * q, 3 * q + 3):
                        split(g, AHEAD + r)
                    work(q)
                split(g, AHEAD + 12)
                if steps is not None:
                    dve.wait_ge(s("fconv_step"), steps)
                for q in range(GROUP):
                    if q:
                        split(g, AHEAD + 12 + q)
                    added(g * 4 + q, q, q, fhist[:, q, 2:2 + T])
                dve.wait_ge(bank_free, g * 4 + 8)

            V.memset(mark[:, 0:1], 0.0).then_inc(s("gelu_done"), 2)
            V.memset(mark[:, 1:2], 0.0).then_inc(s("prod_ready"), 4)
            V.memset(mark[:, 2:3], 0.0).then_inc(s("act_lo"), 2)
            up_group(UC // 4, lambda q: None, None)
            with dve.Fori(0, UP_STEPS - 1) as i:
                up_group(i * 2 + (UC // 4 + 1), lambda q: ffn_conv(i, 0, q), i * 24 + 12)
                up_group(i * 2 + (UC // 4 + 2), lambda q: value_tile(i, q), i * 24 + 24)
            up_group(UC // 4 + 2 * UP_STEPS - 1, lambda q: ffn_conv(UP_STEPS - 1, 0, q), (UP_STEPS - 1) * 24 + 12)
            DC = UC + UP_CHUNKS
            for q in range(GROUP):
                for r in range(3 * q, 3 * q + 3):
                    split(DC // 4, AHEAD + r)
                value_tile(UP_STEPS - 1, q)
            for hf in range(2):
                c = DC + hf * HALF_CHUNKS
                p0 = 4 * c + AHEAD + (12 if hf == 0 else 0)
                p1 = min(4 * (c + HALF_CHUNKS) + AHEAD, 4 * CHUNKS)
                p2 = min((p0 + 15) // 16 * 16, p1)
                for p in range(p0, p2):
                    split(p // 16, p % 16)
                with dve.Fori(p2 // 16, p1 // 16) as r:
                    for i in range(16):
                        split(r, i)
                for p in range(p1 // 16 * 16, p1):
                    split(p // 16, p % 16)
                for j in range(DOWN_TILES):
                    t_ = hf * DOWN_TILES + j
                    added(DC + t_, j, j, down[:, t_, :])
                    dve.wait_ge(bank_free, DC + t_ + 5)
                    V.memset(mark[:, 0:1], 0.0).then_inc(s("down_tile"), 1)
            inverse(3, "f_inv", 0)
            dve.wait_ge(s("f_rstd"), 1)
            for k in range(KT):
                step(V.scalar_tensor_tensor(down[:, k, :], down[:, k, :], gains[:, 3, k:k + 1], rstd[:, :],
                                            ALU.mult, ALU.mult))
                V.tensor_tensor(res[:, k, :], res[:, k, :], down[:, k, :], ALU.add).then_inc(s("y_ready"), 1)

        @block.tensor
        def _(pe):
            M = nc.tensor.matmul

            def tile_piece(g, r):
                q, j = divmod(r, GROUP)
                pe.wait_ge(lo_ready, g * 16 + (r + 1))
                if q == 0:
                    pe.wait_ge(bank_free, g * 4 + (j + 1))
                for kk in range(CHUNK_K):
                    k = CHUNK_K * q + kk
                    w = slice(kk * P, (kk + 1) * P)
                    M(ps[j][:, :], w_hi[:, r % RING, w], xhl[:, k, :, :].rearrange("p a t -> p (a t)"),
                      start=(k == 0), stop=False, skip_group_check=True)
                    last = M(ps[j][:, 0:T], w_lo[:, r % RING, w], xhl[:, k, 0, :],
                             start=False, stop=(k == KT - 1), skip_group_check=True)
                last.then_inc(piece_used, 1)

            def group(g):
                for r in range(16):
                    tile_piece(g, r)

            pe.wait_ge(const_ready, 2)
            pe.wait_ge(s("x_ss"), 1)
            M(ps[4][:, 0:T], ones[:, :], ssum[:, :], start=True, stop=True).then_inc(s("xsum_mm"), 1)
            pe.wait_ge(s("xn_f"), KT)
            for k in range(KT):
                M(ps[4][0:8, 0:T], wba[:, k, 0:8], full[:, k, :], start=(k == 0), stop=(k == KT - 1))
            for k in range(KT):
                last = M(ps[5][0:8, 0:T], wba[:, k, 8:16], full[:, k, :], start=(k == 0), stop=(k == KT - 1))
            last.then_inc(s("ba_done"), 1)
            pe.wait_ge(s("xn_lo"), KT)
            at = [0]

            def follow(place):
                while at[0] < min(place, 16 * IN_GROUPS):
                    g, r = divmod(at[0], 16)
                    at[0] += 1
                    tile_piece(g, r)

            def x_mm(i):
                lv, g = divmod(i % (2 * LEVELS), 2)
                follow(PLACE["x", i])
                pe.wait_ge(s("b_ready"), i + 1)
                if lv:
                    pe.wait_ge(s("t_ready"), i - 1)
                if i >= 2:
                    pe.wait_ge(s("x_sb"), i - 1)
                for u in range(4):
                    last = M(ps[4 + g][:, u * P:(u + 1) * P], bb[:, g, u, :], tmat[:, 4 * g + u, :],
                             start=True, stop=True)
                last.then_inc(s("x_mm"), 1)

            def norm_mm(h):
                follow(PLACE["norm", h])
                pe.wait_ge(s("o_sq"), h + 1)
                M(ps[6][0:8, 0:T], esel[:, h, :], osb[:, h % 4, :], start=(h % BH == 0), stop=(h % BH == BH - 1)
                  ).then_inc(s("on_mm"), 1)

            follow(10)
            pe.wait_ge(s("bg_row"), 1)
            pe.wait_ge(s("ke_row"), 1)
            for n_, (r, j) in enumerate(((1, 0), (1, 1), (0, 0), (0, 1), (2, 1), (3, 0))):
                last = nc.tensor.transpose(ps[6][:, 8 * n_:8 * n_ + 8], rows[:, r, j * P:(j + 1) * P], ident[0:8, 0:8])
            last.then_inc(s("cols_mm"), 1)
            pe.wait_ge(s("ga"), 2)
            pe.wait_ge(s("sel_ready"), 2)
            for b_ in range(BATCHES):
                heads = range(BH * b_, BH * b_ + BH)
                i0 = 2 * LEVELS * b_
                for i in range(4 * b_, 4 * b_ + 4):
                    follow(PLACE["l2", i])
                    pe.wait_ge(s("qk_sq"), i + 1)
                    if b_:
                        pe.wait_ge(s("o_sb"), BH)
                    for a in range(2):
                        last = M(ps[4][0:8, 0:T], esel[:, 2 * (i % 4) + a, :], l2_squares(i)[:, a * T:(a + 1) * T],
                                 start=(i % 4 == 0 and a == 0), stop=(i % 4 == 3 and a == 1))
                    last.then_inc(s("l2_mm"), 1)
                for i in range(4 * b_, 4 * b_ + 4):
                    follow(PLACE["l2b", i])
                    pe.wait_ge(s("l2_rstd"), b_ + 1)
                    if i % 4 >= 2:
                        pe.wait_ge(s("l2_done"), i - 1)
                    for a in range(2):
                        last = M(ps[4 + i % 2][:, a * T:(a + 1) * T], sel[:, 2 * (i % 4) + a, :], nrow,
                                 start=True, stop=True)
                    last.then_inc(s("l2_bc"), 1)
                pe.wait_ge(s("cols_sb"), 1)
                for h in heads:
                    b = h % 2
                    follow(PLACE["bc", h])
                    pe.wait_ge(s("l2_done"), 4 * b_ + 4)
                    if h >= 2:
                        pe.wait_ge(s("ddiff"), h - 1)
                        pe.wait_ge(s("eg_ready"), h - 1)
                    M(ps[4 + b][:, :], sel[:, h, :], rows[:, 0:2, :].rearrange("p r t -> p (r t)"),
                      start=True, stop=True).then_inc(s("bc_mm"), 1)
                    follow(PLACE["a", h])
                    pe.wait_ge(s("kb_ready"), h + 1)
                    if h >= 2:
                        pe.wait_ge(s("tok_sb"), h - 1)
                    if b_:
                        pe.wait_ge(s("mixd_n"), BH // 2)
                    for j in range(NJ):
                        cs = slice(j * P, (j + 1) * P)
                        M(ps[6 + b][:, j * T:j * T + P], proj[:, 8 + h, cs], kb[:, b, cs], start=True, stop=True)
                        last = M(ps[6 + b][:, j * T + P:(j + 1) * T], proj[:, 8 + h, cs], proj[:, h, cs],
                                 start=True, stop=True)
                    last.then_inc(s("a_mm"), 1)
                    follow(PLACE["tok", h])
                    pe.wait_ge(s("qd_ready"), h + 1)
                    pe.wait_ge(s("silu_done"), 4 * b_ + 3)
                    for x_, t_ in ((0, 16 + h), (1, 8 + h)):
                        for j in range(NJ):
                            last = nc.tensor.transpose(ps[6 + b][:, (2 * x_ + j) * P:(2 * x_ + j + 1) * P],
                                                       proj[:, t_, j * P:(j + 1) * P], ident[:, :])
                    last.then_inc(s("tok_mm"), 1)
                follow(PLACE["x", i0])
                pe.wait_ge(s("t_init"), b_ + 1)
                pe.wait_ge(s("tok_sb"), BH * (b_ + 1))

                x_mm(i0)
                for i in range(i0, i0 + 2 * LEVELS):
                    g = i % 2
                    if i + 1 < i0 + 2 * LEVELS:
                        x_mm(i + 1)
                    follow(PLACE["y", i])
                    pe.wait_ge(s("x_sb"), i + 1)
                    if i:
                        pe.wait_ge(s("t_ready"), i)
                    for u in range(4):
                        if i - i0 < 2 * (LEVELS - 1):
                            M(ps[6][:, u * P:(u + 1) * P], tmatT[:, 4 * g + u, :], xb[:, g, u, :],
                              start=True, stop=True)
                        last = M(ps[7][:, u * P:(u + 1) * P], xb[:, g, u, :], tmatT[:, 4 * g + u, :],
                                 start=True, stop=True)
                    last.then_inc(s("y_mm"), 1)
                follow(PLACE["u", b_])
                pe.wait_ge(s("t_ready"), i0 + 2 * LEVELS)
                for i, h in enumerate(heads):
                    c = slice(i * P, (i + 1) * P)
                    last = M(ps[4][:, c], tmatT[:, 2 * i, :], proj[:, 16 + h, 0:P], start=True, stop=True)
                last.then_inc(s("u_mm"), 1)
                follow(PLACE["w", b_])
                for i, h in enumerate(heads):
                    c = slice(i * P, (i + 1) * P)
                    last = M(ps[5][:, c], proj[:, 8 + h, P:T], tmatT[:, 2 * i + 1, :], start=True, stop=True)
                last.then_inc(s("w_mm"), 1)
                follow(PLACE["s", b_])
                pe.wait_ge(s("v0_sb"), b_ + 1)
                for i, h in enumerate(heads):
                    c = slice(i * P, (i + 1) * P)
                    last = M(ps[6][:, c], proj[:, 8 + h, 0:P], v_new[0][:, c], start=True, stop=True)
                last.then_inc(s("s_mm"), 1)
                follow(PLACE["v1", b_])
                pe.wait_ge(s("w_sb"), b_ + 1)
                pe.wait_ge(s("s_sb"), b_ + 1)
                for i, h in enumerate(heads):
                    c = slice(i * P, (i + 1) * P)
                    M(ps[7][:, c], tmatT[:, 2 * i + 1, :], proj[:, 16 + h, P:T], start=True, stop=False)
                    last = M(ps[7][:, c], neg_w[:, c], state[:, c], start=False, stop=True)
                last.then_inc(s("v1_mm"), 1)
                follow(PLACE["o", BH * b_])
                pe.wait_ge(s("v1_sb"), b_ + 1)
                for i, h in enumerate(heads):
                    c = slice(i * P, (i + 1) * P)
                    follow(PLACE["o", h])
                    if i >= 2:
                        pe.wait_ge(s("o_sb"), h - 1)
                    bank = ps[4 + h % 2]
                    M(bank[:, 0:P], v_new[0][:, c], qa[:, 2 * i, :], start=True, stop=True)
                    M(bank[:, P:T], state[:, c], proj[:, h, P:T], start=True, stop=False)
                    M(bank[:, P:T], v_new[1][:, c], qa[:, 2 * i + 1, :], start=False, stop=True
                      ).then_inc(s("o_mm"), 1)
                    if i:
                        norm_mm(h - 1)
                norm_mm(BH * b_ + BH - 1)
                for i in range(2 * b_, 2 * b_ + 2):
                    follow(PLACE["normb", i])
                    pe.wait_ge(s("on_rstd"), b_ + 1)
                    for a in range(2):
                        last = M(ps[6 + i % 2][:, a * T:(a + 1) * T], sel[:, 2 * i + a, :], nrow, start=True, stop=True)
                    last.then_inc(s("on_bc"), 1)
            follow(16 * IN_GROUPS)
            pe.wait_ge(s("x_sb"), 4 * LEVELS)
            pe.wait_ge(s("sbq"), HEADS)
            pe.wait_ge(s("dn_done"), 1)
            pe.wait_ge(s("tri_ready"), 2)
            pe.wait_ge(bank_free, 4 * IN_GROUPS + 4)
            for t in range(HEADS + 4):
                if t < HEADS:
                    zb = ZB[t % 4]
                    if t >= 4:
                        pe.wait_ge(s("att_exp"), t - 3)
                    M(zb[:, 0:T], proj[:, 40 + t, 0:P], proj[:, 32 + t, :], start=True, stop=False,
                      skip_group_check=True)
                    M(zb[:, T:T + P], proj[:, 40 + t, P:T], proj[:, 32 + t, P:T], start=False, stop=True,
                      skip_group_check=True).then_inc(s("z_mm"), 1)
                    if t:
                        pe.wait_ge(s("vt_sb"), t)
                    for j in range(NJ):
                        last = nc.tensor.transpose(ps[7][:, j * P:(j + 1) * P],
                                                   proj[:, 48 + t, j * P:(j + 1) * P], ident[:, :])
                    last.then_inc(s("vt_mm"), 1)
                if 2 <= t < HEADS + 2:
                    g = t - 2
                    zb = ZB[g % 4]
                    pe.wait_ge(s("sp_mask"), g + 1)
                    tri, neg1 = xb[:, 0, 0, :], xb[:, 0, 1, :]
                    M(zb[:, 0:T], tri, SP[g % 4][:, 0:T], start=False, stop=False, skip_group_check=True)
                    M(zb[:, P:T], neg1, SP[g % 4][:, T:T + P], start=False, stop=False, skip_group_check=True)
                    M(zb[:, T:T + P], tri, SP[g % 4][:, T:T + P], start=False, stop=True, skip_group_check=True
                      ).then_inc(s("c_mm"), 1)
                if 3 <= t < HEADS + 3:
                    g = t - 3
                    pe.wait_ge(s("att_mask"), g + 1)
                    pe.wait_ge(s("vt_sb"), g + 1)
                    if g >= 2:
                        pe.wait_ge(s("so_sb"), g - 1)
                    ob, v, at_ = ps[g % 2], VT[g % 4], AT[g % 4]
                    M(ob[:, 0:P], v[:, 0:P], at_[:, 0:P], start=True, stop=True)
                    M(ob[:, P:T], v[:, 0:P], at_[:, P:T], start=True, stop=False)
                    M(ob[:, P:T], v[:, P:T], at_[:, T:T + P], start=False, stop=True).then_inc(s("av_mm"), 1)
                if t >= 4:
                    g = t - 4
                    pe.wait_ge(s("so_sq"), g + 1)
                    M(ps[2][0:8, 0:T], esel[:, g, :], osb[:, g % 4, :], start=(g == 0), stop=(g == HEADS - 1)
                      ).then_inc(s("son_mm"), 1)
            for i in range(HEADS // 2):
                pe.wait_ge(s("son_rstd"), 1)
                for a in range(2):
                    last = M(ps[4 + i][:, a * T:(a + 1) * T], sel[:, 2 * i + a, :], nrow, start=True, stop=True)
                last.then_inc(s("son_bc"), 1)

            pe.wait_ge(s("mix_lo"), HEADS // 2 + 1)
            with pe.Fori(IN_GROUPS, IN_GROUPS + OUT_GROUPS) as g:
                group(g)
            for i in range(2):
                pe.wait_ge(s("ss_ready"), i + 1)
                M(ps[4][:, 0:T], ones[:, :], ssum[:, :], start=True, stop=True
                  ).then_inc(s("ss_mm"), 1)
            pe.wait_ge(s("hn_lo"), KT)
            UC = IN_CHUNKS + OUT_CHUNKS
            with pe.Fori(UC // 4, UC // 4 + 2 * UP_STEPS) as g:
                group(g)
            DC = UC + UP_CHUNKS
            pe.wait_ge(s("act_lo"), FT - 4 + 2)

            def down_chunk(c, k, slot, first, lastc, hf):
                for j in range(DOWN_TILES):
                    piece, part = j // 2, j % 2
                    if part == 0:
                        pe.wait_ge(lo_ready, c * 4 + (piece + 1))
                    if first and (hf or j < 4):
                        pe.wait_ge(bank_free, (DC + j + 1) if hf == 0 else (DC + j + 5))
                    for kk in range(DOWN_K):
                        w = slice((DOWN_K * part + kk) * P, (DOWN_K * part + kk + 1) * P)
                        xk = act[:, k + kk, :, :] if isinstance(k, int) else \
                            act[:, bass.ds(k + kk, 1), :, :].rearrange("p o a t -> p (o a) t")
                        M(ps[j][:, :], w_hi[:, 4 * slot + piece, w], xk.rearrange("p a t -> p (a t)"),
                          start=(first and kk == 0), stop=False, skip_group_check=True)
                        last = M(ps[j][:, 0:T], w_lo[:, 4 * slot + piece, w], xk[:, 0, :], start=False,
                                 stop=(lastc and kk == DOWN_K - 1), skip_group_check=True)
                    if part == 1:
                        last.then_inc(piece_used, 1)

            for hf in range(2):
                c = DC + hf * HALF_CHUNKS
                for k in range(2):
                    down_chunk(c + k, 2 * k, (c + k) % 2, k == 0, False, hf)
                with pe.Fori(1, HALF_CHUNKS // 2 - 1) as r:
                    for k in range(2):
                        down_chunk(r * 2 + (c + k), r * 4 + 2 * k, (c + k) % 2, False, False, hf)
                pe.wait_ge(s("act_lo"), FT + 2)
                for k in range(HALF_CHUNKS - 2, HALF_CHUNKS):
                    down_chunk(c + k, 2 * k, (c + k) % 2, False, k == HALF_CHUNKS - 1, hf)
            pe.wait_ge(s("ss_ready"), 3)
            M(ps[0][:, 0:T], ones[:, :], ssum[:, :], start=True, stop=True).then_inc(s("ss_mm"), 1)



def weight_chunks(w_in, w_out, w_up, w_down):
    def by_columns(w):
        k, n = w.shape
        return w.reshape(k // (CHUNK_K * P), CHUNK_K, P, n // 512, 4, P).transpose(3, 0, 2, 4, 1, 5
                                                                                  ).reshape(-1, P, CHUNK)

    sb3, width = 3 * HEADS * P, BH * P
    dn = w_in[:, sb3:].reshape(-1, 4, BATCHES, width).transpose(0, 2, 1, 3).reshape(w_in.shape[0], -1)
    w_in = np.concatenate([dn, w_in[:, 0:sb3]], axis=1)
    up = by_columns(w_up).reshape(2, UP_STEPS, 4, P, CHUNK).transpose(1, 0, 2, 3, 4).reshape(-1, P, CHUNK)
    dn = w_down.reshape(HALF_CHUNKS, DOWN_K, P, 2, DOWN_TILES, P).transpose(3, 0, 2, 4, 1, 5).reshape(-1, P, CHUNK)
    return np.concatenate([by_columns(w_in), by_columns(w_out), up, dn], axis=0)


def kernel(**inputs):
    import numpy as _np
    import concourse.bacc as _bacc
    from concourse import mybir as _mybir
    from concourse.bass_utils import run_bass_kernel_spmd as _run

    a = {k: _np.asarray(v) for k, v in inputs.items()}
    w_in = a["w_in"][0]
    proj_cols = 7 * HEADS * P
    tiles = lambda v: v.reshape(-1, P).T
    arrays = {
        "x": a["x"][0].reshape(T, KT, P).transpose(2, 1, 0),
        "wts": weight_chunks(w_in[:, :proj_cols], a["w_out"][0], a["w_up"][0], a["w_down"][0]),
        "w_ba": w_in[:, proj_cols:].reshape(KT, P, 16).transpose(1, 0, 2),
        "norm_gains": _np.stack([tiles(a[n][0]) for n in ("ln_mix_pre", "ln_mix_post", "ln_ffn_pre", "ln_ffn_post")],
                                axis=1),
        "head_gains": _np.stack([a["sb_out_gain"][0], a["dn_out_gain"][0]], axis=1),
        "dn_conv": a["dn_conv_w"][0].reshape(4, 24, P).transpose(2, 0, 1),
        "dn_gate": _np.stack([a["dn_a_log"][0], a["dn_dt_bias"][0]], axis=1),
        "ffn_cw": a["ffn_conv_w"][0].reshape(3, 2 * FT, P).transpose(2, 0, 1),
        "ffn_cb": tiles(a["ffn_conv_b"][0]),
    }
    nc = _bacc.Bacc("TRN2", target_bir_lowering=False, num_devices=1, dynamic_dma_scratch_size=64)
    feed, args = {}, []
    for name, v in arrays.items():
        v = _np.ascontiguousarray(v)
        feed[f"in_{name}"] = v
        args.append(nc.dram_tensor(f"in_{name}", v.shape, _mybir.dt.from_np(v.dtype), kind="ExternalInput").ap())
    out = nc.dram_tensor("out_y", (P, KT, T), _mybir.dt.float32, kind="ExternalOutput").ap()
    hybrid_block_kernel(nc, *args, out)
    r = _run(nc, [feed], core_ids=[0])
    y = r.results[0]["out_y"]
    return _np.ascontiguousarray(y.transpose(2, 1, 0).reshape(1, T, D))
```

```python
from contextlib import ExitStack

import numpy as np
import concourse.bass as bass
from concourse import mybir

P = 128
T = 256
D = 2048
KT = D // P
DFF = 5632
FT = DFF // P
HEADS = 8
NJ = T // P
EPS = 1e-6
QSCALE = float(P) ** -0.5
GROUP = 4
CHUNK_K = 4
CHUNK = 2048
RAW = 4
PIECE = CHUNK // 4
RING = 8
AHEAD = 6
BATCHES = 2
BH = HEADS // BATCHES
IN_GROUPS = 14
OUT_GROUPS = 4
UP_STEPS = FT // GROUP
IN_CHUNKS = IN_GROUPS * 4
OUT_CHUNKS = OUT_GROUPS * 4
UP_CHUNKS = UP_STEPS * 8
DOWN_K = 2
DOWN_TILES = 8
HALF_CHUNKS = FT // DOWN_K
DOWN_CHUNKS = 2 * HALF_CHUNKS
CHUNKS = IN_CHUNKS + OUT_CHUNKS + UP_CHUNKS + DOWN_CHUNKS
LEVELS = 7
HALF = P // 2
EARLY = 3
SB_PLACE = 212
UNITS = BH * NJ
GROUP_TILE = [8 * r + BH * b for b in range(BATCHES) for r in range(4)] + [32 + 4 * g for g in range(6)]
PLACE = {}
for _b, _l2 in enumerate((50, 128)):
    _hd, _inv, _rec = _l2 + 9, _l2 + 23, _l2 + 57
    for _i in range(4):
        PLACE["l2", 4 * _b + _i] = _l2 + _i
        PLACE["l2b", 4 * _b + _i] = _l2 + 5 + _i
        for _n, _name in ((0, "bc"), (2, "a"), (4, "tok")):
            PLACE[_name, BH * _b + _i] = _hd + 3 * _i + _n
        PLACE["o", BH * _b + _i] = _rec + 9 + 2 * _i
        PLACE["norm", BH * _b + _i] = _rec + 11 + 2 * _i
    for _i in range(2):
        PLACE["normb", 2 * _b + _i] = _rec + 20 + 2 * _i
    for _i in range(2 * LEVELS):
        PLACE["x", 2 * LEVELS * _b + _i] = _inv + 9 * _i // 4
        PLACE["y", 2 * LEVELS * _b + _i] = _inv + 9 * _i // 4 + 3
    for _name, _n in (("u", 0), ("w", 1), ("s", 3), ("v1", 6)):
        PLACE[_name, _b] = _rec + _n


def hybrid_block_kernel(nc, x, wts, w_ba, norm_gains, head_gains, dn_conv, dn_gate, ffn_cw, ffn_cb, out):
    f32 = mybir.dt.float32
    f32r = mybir.dt.float32r
    ALU = mybir.AluOpType
    ACT = mybir.ActivationFunctionType
    ctx = ExitStack()
    with ctx:
        def sb(name, shape, dt=f32):
            return ctx.enter_context(nc.sbuf_tensor(name, shape, dt))

        def sem(name):
            return ctx.enter_context(nc.semaphore(name))

        res = sb("residual", [P, KT, T])
        raw = sb("raw", [P, RAW, CHUNK])
        w_hi = sb("w_hi", [P, RING, PIECE], f32r)
        w_lo = sb("w_lo", [P, RING, PIECE], f32r)
        half = sb("half", [P, 2, T])
        ident = sb("ident", [P, P])
        ones = sb("ones", [P, P])
        gains = sb("gains", [P, 4, KT])
        hgains = sb("hgains", [P, 2])
        dcw = sb("dcw", [P, 4, 24])
        fcw = sb("fcw", [P, 3, 2 * FT])
        fcb = sb("fcb", [P, 2 * FT])
        rstd = sb("rstd", [P, T])
        vrow = sb("vrow", [P, T])
        gate_mark = sb("gate_mark", [P, 8])
        gate, mark = gate_mark[0:8, 0:4], gate_mark[:, 4:8]
        cols = sb("cols", [P, 6, HEADS])
        ssum = sb("ssum", [P, T])
        token_scale = sb("token_scale", [P, T])
        halfs = [half[:, 0, :], half[:, 1, :], rstd[:, :], vrow[:, :]]
        base = (nc.sbuf_base + 63) // 64 * 64
        xhl = nc.alloc_sbuf_tensor_at("xhl", [P, KT, 2, T], f32r, offset=base)
        down = nc.alloc_sbuf_tensor_at("down", [P, KT, T], f32, offset=base)
        dsq = nc.alloc_sbuf_tensor_at("dsq", [P, 4, T], f32, offset=base + KT * T * 4)
        base += KT * 2 * T * 4
        room = (nc.sbuf_usable_end - base) // 4
        arena = nc.alloc_sbuf_tensor_at("arena", [P, room], f32, offset=base)
        act = nc.alloc_sbuf_tensor_at("ffn_act", [P, FT, 2, T], f32r, offset=base)
        used = [0]

        def cut(n):
            a = used[0]
            used[0] += n
            assert used[0] <= room, (used[0], room)
            return arena[:, a:a + n]

        proj = cut(56 * T).rearrange("p (n t) -> p n t", t=T)
        tmat = cut(UNITS * P).rearrange("p (u n) -> p u n", n=P)
        tmatT = cut(UNITS * P).rearrange("p (u n) -> p u n", n=P)
        ltri = cut(UNITS * P).rearrange("p (u n) -> p u n", n=P)
        qa = cut(UNITS * P).rearrange("p (u n) -> p u n", n=P)
        kb = cut(2 * T).rearrange("p (b t) -> p b t", t=T)
        dm = cut(2 * T).rearrange("p (b t) -> p b t", t=T)
        lmask = cut(LEVELS * P).rearrange("p (l n) -> p l n", n=P)
        xb = cut(2 * 4 * P).rearrange("p (b u n) -> p b u n", b=2, n=P)
        bb = cut(2 * 4 * P).rearrange("p (b u n) -> p b u n", b=2, n=P)
        rows = cut(4 * T)[0:8, :].rearrange("p (r t) -> p r t", t=T)
        sel = cut(4 * T)[0:8, :].rearrange("p (h m) -> p h m", m=P)
        nrow = cut(T)[0:8, :]
        esel = cut(8 * 8).rearrange("p (h m) -> p h m", m=8)
        osb = cut(4 * T).rearrange("p (b n) -> p b n", n=T)
        a0 = 56 * T
        full = arena[:, a0:a0 + KT * T].rearrange("p (k t) -> p k t", t=T)
        squ = full
        small = xb[0:8, :, :, :].rearrange("p b u n -> p (b u n)").rearrange("p (r t) -> p r t", t=T)
        small2 = bb[0:8, :, :, :].rearrange("p b u n -> p (b u n)").rearrange("p (r t) -> p r t", t=T)
        conv = proj[:, 52:56, :]
        mixo = arena[:, 0:KT * T].rearrange("p (n t) -> p n t", t=T)
        f0 = FT * 2 * T
        hsq = arena[:, KT * T:2 * KT * T].rearrange("p (n t) -> p n t", t=T)
        fhist = arena[:, f0:f0 + 4 * (T + 2)].rearrange("p (b t) -> p b t", b=4)
        f1 = f0 + 4 * (T + 2)
        fconv = arena[:, f1:f1 + 4 * T].rearrange("p (b t) -> p b t", b=4)
        gelu = arena[:, f1 + 4 * T:f1 + 8 * T].rearrange("p (b t) -> p b t", b=4)
        prod = arena[:, f1 + 8 * T:f1 + 10 * T].rearrange("p (b t) -> p b t", b=2)
        assert f1 + 10 * T <= room, (f1 + 10 * T, room)
        wba = arena[:, 40 * T:40 * T + KT * 40].rearrange("p (k n) -> p k n", n=40)

        ps = [ctx.enter_context(nc.psum_tensor(f"bank{i}", [P, 512], f32)) for i in range(8)]

        raw_full = [sem(f"raw_full{i}") for i in range(RAW)]
        hi_ready = sem("hi_ready")
        lo_ready = sem("lo_ready")
        piece_used = sem("piece_used")
        half_ready = sem("half_ready")
        bank_free = sem("bank_free")
        small_in = sem("small_in")
        x_in = sem("x_in")
        const_ready = sem("const_ready")
        out_done = sem("out_done")
        T_ = dict()

        def s(name):
            if name not in T_:
                T_[name] = sem(name)
            return T_[name]

        def square_sum(pool, name, buf):
            for k in range(1, KT):
                pool.wait_ge(s(f"{name}_sq"), k + 1)
                if k > 1:
                    pool.wait_ge(s(f"{name}_add"), k - 1)
                pool.tensor_tensor(ssum[:, :], buf[:, 0, :] if k == 1 else ssum[:, :], buf[:, k % 4, :], ALU.add
                                   ).then_inc(s(f"{name}_add"), 1)

        def square(act_e, name, src, k, buf):
            if k >= 4:
                act_e.wait_ge(s(f"{name}_add"), k - 3)
            nc.scalar.activation(buf[:, k % 4, :], src[:, k, :], ACT.Square).then_inc(s(f"{name}_sq"), 1)

        def times_gain(act_e, name, src, k, gain):
            act_e.wait_ge(s(f"{name}_sq"), k + 1)
            nc.scalar.activation(src[:, k, :], src[:, k, :], ACT.Copy, scale=gain).then_inc(s(f"{name}_gain"), 1)

        spb = arena[:, a0:a0 + 4 * 1024].rearrange("p (b n) -> p b n", n=1024)
        SP = [spb[:, i, 0:384] for i in range(4)]
        AT = [spb[:, i, 384:768] for i in range(4)]
        VT = [spb[:, i, 768:1024] for i in range(4)]
        ZB = [ps[4], ps[5], ps[6], ps[3]]

        def l2_squares(i):
            return qa[:, 4 * (i % 2):4 * (i % 2) + 4, :].rearrange("p u n -> p (u n)")

        def l2_pair(i):
            b, r = divmod(i, 4)
            t0 = 8 * (r // 2) + BH * b + 2 * (r % 2)
            return proj[:, t0:t0 + 2, :]

        def eg(h):
            return tmat[:, h % BH, :]

        def flat(v):
            return v.rearrange("p u n -> p (u n)")

        neg_w, state = flat(tmat[:, 0:4, :]), flat(tmat[:, 4:8, :])
        v_new = [flat(ltri[:, 0:4, :]), flat(ltri[:, 4:8, :])]

        def half_columns(v, lv, side):
            w = 1 << lv
            if len(v.shape) == 3:
                return v.rearrange("p u (a b r) -> p u a b r", b=2, r=w)[:, :, :, side, :]
            return v.rearrange("p (a b r) -> p a b r", b=2, r=w)[:, :, side, :]

        def flat_t(v):
            return v.rearrange("p n t -> p (n t)")

        block = ctx.enter_context(nc.Block())
        x_v = x
        NX = 4

        @block.sync
        def _(sp):
            for q in range(NX):
                sp.dma_start(res[:, 4 * q:4 * q + 4, :], x_v[:, 4 * q:4 * q + 4, :]).then_inc(s(f"x_in{q}"), 16)
                sp.dma_start(raw[:, q, :], wts[q, :, :]).then_inc(raw_full[q], 16)
            with sp.Fori(1, CHUNKS // RAW) as i:
                for slot in range(RAW):
                    sp.wait_ge(lo_ready, i * (4 * RAW) + 4 * (slot + 1 - RAW))
                    sp.dma_start(raw[:, slot, :], wts[bass.ds(i * RAW + slot, 1), :, :].rearrange("a p n -> p (a n)")
                                 ).then_inc(raw_full[slot], 16)
            for q in range(4):
                sp.wait_ge(s("y_ready"), q + 1)
                sp.dma_start(out[:, 4 * q:4 * q + 4, :], res[:, 4 * q:4 * q + 4, :]).then_inc(out_done, 16)
            sp.wait_ge(out_done, 64)

        @block.gpsimd
        def _(pool):
            n = [0]

            def step(ins):
                n[0] += 1
                ins.then_inc(s("pool_step"), 1)
                pool.wait_ge(s("pool_step"), n[0])

            pool.memset(ones[:, :], 1.0).then_inc(const_ready, 1)
            step(pool.memset(ident[:, :], 0.0))
            pool.affine_select(out=ident[:, :], in_=ident[:, :], compare_op=ALU.not_equal, fill=1.0, base=0,
                               pattern=[[-1, P]], channel_multiplier=1).then_inc(const_ready, 1)
            for k in range(KT):
                pool.wait_ge(s("xn_hi"), k + 1)
                pool.tensor_tensor(xhl[:, k, 1, :], full[:, k, :], xhl[:, k, 0, :].bitcast(f32), ALU.subtract
                                   ).then_inc(s("xn_lo"), 1)
            step(pool.memset(sel[:, :, :], 1.0))
            pool.affine_select(out=sel[:, :, :], in_=sel[:, :, :], compare_op=ALU.is_equal, fill=0.0, base=0,
                               pattern=[[-1, HEADS], [0, P]], channel_multiplier=1).then_inc(s("sel_ready"), 1)
            step(pool.memset(esel[:, :, :], 1.0))
            pool.affine_select(out=esel[:, :, :], in_=esel[:, :, :], compare_op=ALU.is_equal, fill=0.0, base=0,
                               pattern=[[-1, 8], [1, 8]], channel_multiplier=0).then_inc(s("sel_ready"), 1)
            def level_masks():
                for lv in range(LEVELS):
                    w = 1 << lv
                    na = P // (2 * w)
                    m = lmask[:, lv, :].rearrange("p (a b r) -> p a b r", b=2, r=w)
                    step(pool.memset(lmask[:, lv, :], 1.0))
                    step(pool.affine_select(out=m, in_=m, compare_op=ALU.is_ge, fill=0.0, base=-1,
                                            pattern=[[0, na], [1, 2], [0, w]], channel_multiplier=0))
                    step(pool.affine_select(out=m, in_=m, compare_op=ALU.is_ge, fill=0.0, base=0,
                                            pattern=[[-2 * w, na], [0, 2], [0, w]], channel_multiplier=1))
                    pool.affine_select(out=m, in_=m, compare_op=ALU.is_ge, fill=0.0, base=w - 1,
                                       pattern=[[2 * w, na], [0, 2], [0, w]], channel_multiplier=-1
                                       ).then_inc(s("lmask_ready"), 1)

            at = [-1]

            def follow(place):
                while at[0] < place:
                    at[0] += 1
                    g, j = divmod(at[0] - 13, 16)
                    if j < GROUP and 0 <= g < IN_GROUPS:
                        n_ = 4 * g + j
                        pool.wait_ge(bank_free, n_ + 5)
                        if n_ == 0:
                            pool.wait_ge(s("x_rstd"), 1)
                        tile = proj[:, GROUP_TILE[g] + j, :]
                        pool.tensor_tensor(tile, tile, token_scale[:, :], ALU.mult).then_inc(s("scaled"), 1)
                        if 32 <= GROUP_TILE[g] < 40:
                            pool.wait_ge(s("scaled"), n_ + 1)
                            pool.tensor_scalar(tile, tile, QSCALE, 0.0, ALU.mult, ALU.add).then_inc(s("sbq"), 1)

            follow(20)
            level_masks()
            for b in range(BATCHES):
                for i in range(4 * b, 4 * b + 4):
                    follow(PLACE["l2", i] - 2)
                    pool.wait_ge(s("silu_done"), 4 * b + 1 + (i % 4) // 2)
                    if i % 4 >= 2:
                        pool.wait_ge(s("l2_mm"), i - 1)
                    elif b:
                        pool.wait_ge(s("o_mm"), BH)
                    else:
                        pool.wait_ge(s("xn_lo"), KT)
                        pool.wait_ge(s("ba_done"), 1)
                    pool.tensor_tensor(l2_squares(i).rearrange("p (a t) -> p a t", t=T), l2_pair(i), l2_pair(i),
                                       ALU.mult).then_inc(s("qk_sq"), 1)
                for h in range(BH * b, BH * b + BH):
                    follow(PLACE["bc", h])
                    pool.wait_ge(s("dexp"), h + 1)
                    d = dm[:, h % 2, :].rearrange("p (j c) -> p j c", j=2)
                    pool.affine_select(out=d, in_=d, compare_op=ALU.is_ge, fill=0.0, base=0,
                                       pattern=[[0, 2], [1, P]], channel_multiplier=-1).then_inc(s("dmask"), 1)
            follow(SB_PLACE)
            pool.wait_ge(s("y_mm"), 4 * LEVELS)
            step(pool.memset(xb[:, 0, 0, :], -1.0))
            pool.memset(xb[:, 0, 1, :], -1.0).then_inc(s("tri_ready"), 1)
            pool.affine_select(out=xb[:, 0, 0, :], in_=xb[:, 0, 0, :], compare_op=ALU.is_ge, fill=0.0, base=0,
                               pattern=[[-1, P]], channel_multiplier=1).then_inc(s("tri_ready"), 1)
            follow(16 * IN_GROUPS)
            for b in range(BATCHES):
                for h in range(BH * b, BH * b + BH):
                    pool.wait_ge(s("sp_ready"), h + 1)
                    for lot in (0, 2 * P):
                        v = SP[h % BH][:, lot:lot + P]
                        ins = pool.affine_select(out=v, in_=v, compare_op=ALU.is_ge, fill=0.0, base=-1,
                                                 pattern=[[1, P]], channel_multiplier=-1)
                    ins.then_inc(s("sp_mask"), 1)
                for h in range(BH * b, BH * b + BH):
                    pool.wait_ge(s("att_exp"), h + 1)
                    for lot in (0, 2 * P):
                        v = AT[h % BH][:, lot:lot + P]
                        ins = pool.affine_select(out=v, in_=v, compare_op=ALU.is_ge, fill=0.0, base=-1,
                                                 pattern=[[1, P]], channel_multiplier=-1)
                    ins.then_inc(s("att_mask"), 1)
            square_sum(pool, "m", squ)
            pool.memset(fhist[:, :, 0:2], 0.0).then_inc(s("fhist_ready"), 1)
            for k in range(KT):
                pool.wait_ge(s("hn_hi"), k + 1)
                pool.tensor_tensor(xhl[:, k, 1, :], full[:, k, :], xhl[:, k, 0, :].bitcast(f32), ALU.subtract
                                   ).then_inc(s("hn_lo"), 1)
            pool.wait_ge(s("h_rstd"), 1)
            UG = (IN_CHUNKS + OUT_CHUNKS) // 4

            def up_scale(g):
                for q in range(GROUP):
                    pool.wait_ge(bank_free, g * 4 + (q + 5))
                    tile = fhist[:, q, 2:2 + T]
                    pool.tensor_tensor(tile, tile, token_scale[:, :], ALU.mult).then_inc(s("up_scaled"), 1)

            def act_lo(i):
                for q in range(GROUP):
                    pool.wait_ge(s("act_hi"), i * 4 + (q + 1))
                    k = slice(i * 4 + q, i * 4 + q + 1) if isinstance(i, int) else bass.ds(i * 4 + q, 1)
                    pool.tensor_tensor(act[:, k, 1, :].rearrange("p a t -> p (a t)"), prod[:, q % 2, :],
                                       act[:, k, 0, :].rearrange("p a t -> p (a t)").bitcast(f32),
                                       ALU.subtract).then_inc(s("act_lo"), 1)

            up_scale(UG)
            with pool.Fori(0, UP_STEPS - 1) as i:
                up_scale(i * 2 + (UG + 1))
                act_lo(i)
                up_scale(i * 2 + (UG + 2))
            up_scale(UG + 2 * UP_STEPS - 1)
            act_lo(UP_STEPS - 1)
            square_sum(pool, "f", dsq)

        @block.scalar
        def _(act_e):
            def split(g, i):
                slot, quarter = (i // 4) % RAW, i % 4
                if quarter == 0:
                    act_e.wait_ge(raw_full[slot], (g + i // 16) * 16 + 16)
                act_e.wait_ge(piece_used, g * 16 + (i + 1))
                nc.scalar.activation(w_hi[:, i % RING, :], raw[:, slot, quarter * PIECE:(quarter + 1) * PIECE], ACT.Copy
                                     ).then_inc(hi_ready, 1)

            def halves(n, j, b, used):
                act_e.wait_ge(piece_used, used)
                act_e.wait_ge(bank_free, n + 1)
                nc.scalar.activation(halfs[j % 4], ps[b][:, T:2 * T], ACT.Copy).then_inc(half_ready, 1)

            def group_halves(g, j):
                halves(g * 4 + j, j, j, g * 16 + (RING + 12 + j + 1))

            def slots(g, a, b):
                for r in range(a, b):
                    if r < 16:
                        split(g, AHEAD + r)
                    if r >= 13:
                        group_halves(g, r - 13)

            act_e.dma_start(gains[:, :, :], norm_gains).then_inc(s("gains_in"), 16)
            act_e.dma_start(hgains[:, :], head_gains).then_inc(small_in, 16)
            act_e.dma_start(dcw[:, :, :], dn_conv).then_inc(small_in, 16)
            act_e.dma_start(gate[:, 0:2], dn_gate).then_inc(small_in, 16)
            act_e.dma_start(fcw[:, :, :], ffn_cw).then_inc(small_in, 16)
            act_e.dma_start(fcb[:, :], ffn_cb).then_inc(small_in, 16)
            act_e.dma_start(wba[:, :, :], w_ba).then_inc(small_in, 16)

            at = [-1]

            def follow(place):
                while at[0] < place:
                    at[0] += 1
                    p = at[0]
                    g, r = divmod(p, 16)
                    if p < 16 * IN_GROUPS:
                        split(g, AHEAD + r)
                    if (p - 13) % 16 < GROUP and 13 <= p < 16 * IN_GROUPS + 1:
                        group_halves((p - 13) // 16, (p - 13) % 16)
                    if r == 10 and 1 <= g <= 8:
                        t0 = GROUP_TILE[g - 1]
                        if g % 4:
                            act_e.wait_ge(s("conv_done"), 4 * (g - 1 - (g - 1) // 4) + 4)
                            src = conv[:, :, :]
                        else:
                            act_e.wait_ge(s("scaled"), 4 * g)
                            src = proj[:, t0:t0 + 4, :]
                        nc.scalar.activation(proj[:, t0:t0 + 4, :], src, ACT.Silu).then_inc(s("silu_done"), 1)

            def input_hi(q):
                for k in range(4 * q, 4 * q + 4):
                    act_e.wait_ge(s("xn_f"), k + 1)
                    nc.scalar.activation(xhl[:, k, 0, :], full[:, k, :], ACT.Copy).then_inc(s("xn_hi"), 1)

            input_hi(0)
            for i in range(4):
                split(0, i)
            input_hi(1)
            split(0, 4)
            split(0, 5)
            input_hi(2)
            follow(1)
            input_hi(3)
            follow(3)
            for q in range(NX):
                nc.scalar.activation(proj[:, 4 * q:4 * q + 4, :], res[:, 4 * q:4 * q + 4, :], ACT.Square
                                     ).then_inc(s("x_sq"), 1)
            follow(12)
            act_e.wait_ge(s("x_inv"), 1)
            nc.scalar.activation(token_scale[:, :], token_scale[:, :], ACT.Sqrt).then_inc(s("x_rstd"), 1)
            follow(14)
            n = [0]

            def step(ins):
                n[0] += 1
                ins.then_inc(s("act_step"), 1)
                act_e.wait_ge(s("act_step"), n[0])
            act_e.wait_ge(s("ba_sb"), 1)
            nc.scalar.activation(small[:, 0, :], small[:, 0, :], ACT.Exp, scale=-1.0).then_inc(s("eb"), 1)
            step(nc.scalar.activation(small[:, 1, :], small[:, 1, :], ACT.Identity, bias=gate[:, 1:2]))
            step(nc.scalar.activation(small[:, 2, :], small[:, 1, :], ACT.Abs))
            step(nc.scalar.activation(small[:, 3, :], small[:, 2, :], ACT.Exp, scale=-1.0))
            nc.scalar.activation(gate[:, 2:3], gate[:, 0:1], ACT.Exp).then_inc(s("ga"), 1)
            nc.scalar.activation(small2[:, 0, :], small[:, 3, :], ACT.Ln, bias=1.0).then_inc(s("ga"), 1)
            follow(19)
            act_e.wait_ge(s("gc_ready"), 2)
            nc.scalar.activation(small2[:, 1, :], rows[:, 1, :], ACT.Exp).then_inc(s("eg_row"), 1)
            nc.scalar.activation(rows[:, 3, 0:P], rows[:, 1, 0:P], ACT.Exp, scale=-1.0, bias=rows[:, 1, P - 1:P]
                                 ).then_inc(s("ke_row"), 1)
            for b in range(BATCHES):
                heads = range(BH * b, BH * b + BH)
                follow(PLACE["l2", 4 * b + 3] + 2)
                act_e.wait_ge(s("l2_inv"), b + 1)
                nc.scalar.activation(nrow, nrow, ACT.Sqrt).then_inc(s("l2_rstd"), 1)
                for h in heads:
                    follow(PLACE["bc", h])
                    act_e.wait_ge(s("ddiff"), h + 1)
                    nc.scalar.activation(dm[:, h % 2, :], dm[:, h % 2, :], ACT.Exp).then_inc(s("dexp"), 1)
                    nc.scalar.activation(eg(h), ps[4 + h % 2][:, T + P:2 * T], ACT.Exp).then_inc(s("eg_ready"), 1)
                for i in range(2 * LEVELS * b, 2 * LEVELS * (b + 1)):
                    follow(PLACE["x", i])
                    act_e.wait_ge(s("x_mm"), i + 1)
                    if i >= 2:
                        act_e.wait_ge(s("y_mm"), i - 1)
                    nc.scalar.activation(xb[:, i % 2, :, :], ps[4][:, :] if i % 2 == 0 else ps[5][:, :], ACT.Copy
                                         ).then_inc(s("x_sb"), 1)
                follow(PLACE["w", b])
                act_e.wait_ge(s("w_mm"), b + 1)
                nc.scalar.activation(neg_w, ps[5][:, :], ACT.Copy, scale=-1.0).then_inc(s("w_sb"), 1)
                follow(PLACE["s", b])
                act_e.wait_ge(s("s_mm"), b + 1)
                nc.scalar.activation(state, ps[6][:, :], ACT.Copy).then_inc(s("s_sb"), 1)
                for h in heads:
                    follow(PLACE["o", h])
                    act_e.wait_ge(s("o_mm"), h + 1)
                    if h >= 4:
                        act_e.wait_ge(s("on_mm"), h - 3)
                    nc.scalar.activation(osb[:, h % 4, :], ps[4 + h % 2][:, 0:T], ACT.Square).then_inc(s("o_sq"), 1)
                    nc.scalar.activation(proj[:, h, :], ps[4 + h % 2][:, 0:T], ACT.Copy).then_inc(s("o_sb"), 1)
                follow(PLACE["norm", BH * b + 3] + 2)
                act_e.wait_ge(s("on_inv"), b + 1)
                nc.scalar.activation(nrow, nrow, ACT.Sqrt).then_inc(s("on_rstd"), 1)
            def sb_exp(h):
                act_e.wait_ge(s("z_mm"), h + 1)
                if h >= BH:
                    act_e.wait_ge(s("c_mm"), h - BH + 1)
                step(nc.scalar.activation(SP[h % BH], ZB[h % BH][:, 0:384], ACT.Abs))
                nc.scalar.activation(SP[h % BH], SP[h % BH], ACT.Exp, scale=-1.0).then_inc(s("sb_e"), 1)

            def sb_ln(h):
                act_e.wait_ge(s("sb_e"), h + 1)
                nc.scalar.activation(SP[h % BH], SP[h % BH], ACT.Ln, bias=1.0).then_inc(s("ln_ready"), 1)

            def sb_att(h):
                act_e.wait_ge(s("c_mm"), h + 1)
                if h >= BH:
                    act_e.wait_ge(s("av_mm"), h - BH + 1)
                nc.scalar.activation(AT[h % BH], ZB[h % BH][:, 0:384], ACT.Exp).then_inc(s("att_exp"), 1)

            def sb_square(h):
                act_e.wait_ge(s("so_sb"), h + 1)
                if h >= BH:
                    act_e.wait_ge(s("son_mm"), h - BH + 1)
                nc.scalar.activation(osb[:, h % 4, :], proj[:, 32 + h, :], ACT.Square).then_inc(s("so_sq"), 1)

            follow(SB_PLACE)
            for h in range(EARLY):
                sb_exp(h)
            follow(SB_PLACE + 4)
            for h in range(EARLY):
                sb_ln(h)
            follow(16 * IN_GROUPS + 1)
            for h in range(EARLY, BH):
                sb_exp(h)
            for h in range(EARLY, BH):
                sb_ln(h)
            act_e.wait_ge(s("mixd_f"), HEADS // 2)
            act_e.wait_ge(piece_used, 4 * IN_CHUNKS + RING)
            nc.scalar.activation(xhl[:, 0:HEADS, 0, :], proj[:, 0:HEADS, :], ACT.Copy).then_inc(s("mixd_hi"), 1)
            for h in range(BH):
                sb_att(h)
            for h in range(BH):
                sb_exp(BH + h)
            for h in range(BH):
                sb_ln(BH + h)
            for h in range(BH):
                sb_square(h)
            for h in range(BH):
                sb_att(BH + h)
            for h in range(BH):
                sb_square(BH + h)
            act_e.wait_ge(s("son_inv"), 1)
            nc.scalar.activation(nrow, nrow, ACT.Sqrt).then_inc(s("son_rstd"), 1)
            for i in range(HEADS // 2):
                act_e.wait_ge(s("mixs_f"), i + 1)
                nc.scalar.activation(xhl[:, HEADS + 2 * i:HEADS + 2 * i + 2, 0, :], proj[:, 32 + 2 * i:34 + 2 * i, :], ACT.Copy
                                     ).then_inc(s("mixs_hi"), 1)

            for g in range(IN_GROUPS, IN_GROUPS + OUT_GROUPS):
                slots(g, 0, 13)
                k0 = 4 * (g - IN_GROUPS)
                for j in range(GROUP + 1):
                    if j < GROUP:
                        slots(g, 13 + j, 14 + j)
                    if j:
                        act_e.wait_ge(bank_free, 4 * g + j + 4)
                        square(act_e, "m", mixo, k0 + j - 1, squ)
                for k in range(k0, k0 + GROUP):
                    times_gain(act_e, "m", mixo, k, gains[:, 1, k:k + 1])
            act_e.wait_ge(s("m_inv"), 1)
            nc.scalar.activation(rstd[:, :], vrow[:, :], ACT.Sqrt).then_inc(s("m_rstd"), 1)
            UG = IN_GROUPS + OUT_GROUPS

            def hidden_tiles(q):
                act_e.wait_ge(s("h_ready"), q + 1)
                for k in range(4 * q, 4 * q + 4):
                    nc.scalar.activation(full[:, k, :], res[:, k, :], ACT.Copy, scale=gains[:, 2, k:k + 1]
                                         ).then_inc(s("hn_f"), 1)
                for k in range(4 * q, 4 * q + 4):
                    act_e.wait_ge(s("hn_f"), k + 1)
                    nc.scalar.activation(xhl[:, k, 0, :], full[:, k, :], ACT.Copy).then_inc(s("hn_hi"), 1)

            hidden_tiles(0)
            hidden_tiles(1)
            hidden_tiles(2)
            slots(UG, 0, 3)
            hidden_tiles(3)
            slots(UG, 3, 8)
            for q in range(4):
                nc.scalar.activation(hsq[:, 4 * q:4 * q + 4, :], res[:, 4 * q:4 * q + 4, :], ACT.Square
                                     ).then_inc(s("h_sq"), 1)
            slots(UG, 8, 16)
            act_e.wait_ge(s("h_inv"), 1)
            nc.scalar.activation(token_scale[:, :], token_scale[:, :], ACT.Sqrt).then_inc(s("h_rstd"), 1)
            slots(UG, 16, 17)

            UC = IN_CHUNKS + OUT_CHUNKS

            def gelu_tile(i, q):
                act_e.wait_ge(s("fconv_step"), i * 24 + (3 * q + 3))
                act_e.wait_ge(s("prod_ready"), i * 4 + (q + 1))
                nc.scalar.activation(gelu[:, q, :], fconv[:, q % 2, :], ACT.Gelu_apprx_tanh
                                     ).then_inc(s("gelu_done"), 1)

            def act_hi(i, q):
                act_e.wait_ge(s("prod_ready"), i * 4 + (q + 5))
                nc.scalar.activation(act[:, bass.ds(i * 4 + q, 1), 0, :].rearrange("p a t -> p (a t)"),
                                     prod[:, q % 2, :], ACT.Copy).then_inc(s("act_hi"), 1)

            def with_work(g, work):
                slots(g, 0, 6)
                work(0)
                slots(g, 6, 9)
                work(1)
                slots(g, 9, 12)
                work(2)
                slots(g, 12, 15)
                work(3)
                slots(g, 15, 17)

            def gate_slots(i, g):
                with_work(g, lambda q: gelu_tile(i, q))

            with act_e.Fori(0, UP_STEPS - 1) as i:
                gate_slots(i, i * 2 + (UG + 1))
                with_work(i * 2 + (UG + 2), lambda q: act_hi(i, q))
            gate_slots(UP_STEPS - 1, UG + 2 * UP_STEPS - 1)
            DC = UC + UP_CHUNKS
            for q in range(GROUP):
                for r in range(0 if q == 0 else 3 * q + 3, 3 * q + 6):
                    split(DC // 4, AHEAD + r)
                act_hi(UP_STEPS - 1, q)
            for hf in range(2):
                c = DC + hf * HALF_CHUNKS
                p0 = 4 * c + AHEAD + (15 if hf == 0 else 0)
                p1 = min(4 * (c + HALF_CHUNKS) + AHEAD, 4 * CHUNKS)
                p2 = min((p0 + 15) // 16 * 16 + 16 * hf, p1)
                for n_, p in enumerate(range(p0, p2)):
                    split(p // 16, p % 16)
                    if hf == 1 and n_ % 2 == 1 and n_ < 2 * DOWN_TILES:
                        act_e.wait_ge(bank_free, DC + n_ // 2 + 5)
                        square(act_e, "f", down, n_ // 2, dsq)
                        times_gain(act_e, "f", down, n_ // 2, gains[:, 3, n_ // 2:n_ // 2 + 1])
                with act_e.Fori(p2 // 16, p1 // 16) as r:
                    for i in range(16):
                        split(r, i)
                for p in range(p1 // 16 * 16, p1):
                    split(p // 16, p % 16)
                for j in range(DOWN_TILES):
                    halves(DC + hf * DOWN_TILES + j, j, j, RING + 4 * (c + HALF_CHUNKS - 1) + j // 2 + 1)
                    if hf == 1 and j:
                        act_e.wait_ge(bank_free, DC + DOWN_TILES + j + 4)
                        square(act_e, "f", down, DOWN_TILES + j - 1, dsq)
            act_e.wait_ge(bank_free, DC + KT + 4)
            square(act_e, "f", down, KT - 1, dsq)
            for k in range(DOWN_TILES, KT):
                times_gain(act_e, "f", down, k, gains[:, 3, k:k + 1])
            act_e.wait_ge(s("f_inv"), 1)
            nc.scalar.activation(rstd[:, :], vrow[:, :], ACT.Sqrt).then_inc(s("f_rstd"), 1)

        @block.vector
        def _(dve):
            V = nc.vector
            n = [0]

            def step(ins):
                n[0] += 1
                ins.then_inc(s("dve_step"), 1)
                dve.wait_ge(s("dve_step"), n[0])

            def split(g, i):
                slot, quarter = (i // 4) % RAW, i % 4
                dve.wait_ge(hi_ready, g * 16 + (i + 1))
                V.tensor_tensor(w_lo[:, i % RING, :], raw[:, slot, quarter * PIECE:(quarter + 1) * PIECE],
                                w_hi[:, i % RING, :].bitcast(f32), ALU.subtract).then_inc(lo_ready, 1)

            def added(n_, j, b, out_):
                dve.wait_ge(half_ready, n_ + 1)
                return V.tensor_tensor(out_, ps[b][:, 0:T], halfs[j % 4], ALU.add).then_inc(bank_free, 1)

            V.memset(mark[:, 0:1], 0.0).then_inc(bank_free, 4)
            V.memset(mark[:, 1:2], 0.0).then_inc(piece_used, RING)
            at = [-1]

            def conv_tile(g, j):
                n_ = 4 * (g - g // 4) + j
                t = GROUP_TILE[g] + j
                dve.wait_ge(s("scaled"), 4 * g + j + 1)
                if g:
                    dve.wait_ge(s("silu_done"), g)
                for tap in range(4):
                    lag = tap
                    w = dcw[:, 3 - lag, t:t + 1]
                    if lag:
                        dve.wait_ge(s("conv_step"), 3 * n_ + lag)
                        ins = V.scalar_tensor_tensor(conv[:, j, lag:T], proj[:, t, 0:T - lag], w, conv[:, j, lag:T],
                                                     ALU.mult, ALU.add)
                    else:
                        ins = V.tensor_scalar(conv[:, j, :], proj[:, t, :], w, None, ALU.mult)
                    ins.then_inc(s("conv_done") if lag == 3 else s("conv_step"), 1)

            def follow(place):
                while at[0] < place:
                    at[0] += 1
                    p = at[0]
                    g, r = divmod(p, 16)
                    if p < 16 * IN_GROUPS:
                        split(g, AHEAD + r)
                    if (p - 13) % 16 < GROUP and 13 <= p < 16 * IN_GROUPS + 1:
                        g_, j = divmod(p - 13, 16)
                        if g_ == IN_GROUPS - 1 and j == 0:
                            dve.wait_ge(s("silu_done"), 8)
                        added(4 * g_ + j, j, j, proj[:, GROUP_TILE[g_] + j, :])
                    if r in (1, 3, 5, 7) and 1 <= g <= 7 and g != 4:
                        conv_tile(g - 1, r // 2)

            def input_tiles(q):
                dve.wait_ge(s(f"x_in{q}"), 16)
                for k in range(4 * q, 4 * q + 4):
                    V.tensor_scalar(full[:, k, :], res[:, k, :], gains[:, 0, k:k + 1], None, ALU.mult
                                    ).then_inc(s("xn_f"), 1)

            dve.wait_ge(s("gains_in"), 16)
            input_tiles(0)
            for i in range(4):
                split(0, i)
            input_tiles(1)
            split(0, 4)
            split(0, 5)
            input_tiles(2)
            follow(1)
            input_tiles(3)
            follow(3)
            dve.wait_ge(s("x_sq"), NX)
            for j in range(NJ):
                follow(3 + 2 * j)
                part = slice(j * P, (j + 1) * P)
                V.tensor_reduce(ssum[:, part], proj[:, 0:KT, part].rearrange("p k t -> p t k"),
                                mybir.AxisListType.X, ALU.add).then_inc(s("x_ss"), 1)
            follow(12)
            dve.wait_ge(s("x_ss"), NJ)
            dve.wait_ge(s("xsum_mm"), 1)
            step(V.tensor_scalar(token_scale[:, :], ps[4][:, 0:T], 1.0 / D, EPS, ALU.mult, ALU.add))
            V.reciprocal(token_scale[:, :], token_scale[:, :]).then_inc(s("x_inv"), 1)
            follow(13)
            dve.wait_ge(small_in, 16 * 6)
            dve.wait_ge(s("x_rstd"), 1)
            dve.wait_ge(s("ba_done"), 1)
            V.tensor_tensor(small[:, 0, :], ps[5][0:8, 0:T], token_scale[0:8, :], ALU.mult)
            V.tensor_tensor(small[:, 1, :], ps[5][32:40, 0:T], token_scale[32:40, :], ALU.mult).then_inc(s("ba_sb"), 1)
            follow(16)
            dve.wait_ge(s("eb"), 1)
            step(V.tensor_scalar(small[:, 0, :], small[:, 0, :], 1.0, None, ALU.add))
            step(V.reciprocal(rows[:, 0, :], small[:, 0, :]))
            follow(18)
            dve.wait_ge(s("ga"), 2)
            step(V.scalar_tensor_tensor(small[:, 1, :], small[:, 1, :], 0.0, small2[:, 0, :], ALU.max, ALU.add))
            step(V.tensor_scalar(small[:, 1, :], small[:, 1, :], gate[:, 2:3], -1.0, ALU.mult, ALU.mult))
            step(V.memset(small[:, 2, :], 1.0))
            for j in range(NJ):
                V.tensor_tensor_scan(rows[:, 1, j * P:(j + 1) * P], small[:, 2, 0:P], small[:, 1, j * P:(j + 1) * P],
                                     0.0, ALU.mult, ALU.add).then_inc(s("gc_ready"), 1)
            follow(21)
            dve.wait_ge(s("eg_row"), 1)
            V.tensor_tensor(rows[:, 2, :], rows[:, 0, :], small2[:, 1, :], ALU.mult).then_inc(s("bg_row"), 1)
            follow(41)
            dve.wait_ge(s("cols_mm"), 1)
            V.tensor_copy(cols[:, :, :].rearrange("p r h -> p (r h)"), ps[6][:, 0:48]).then_inc(s("cols_sb"), 1)
            for batch in range(BATCHES):
                follow(PLACE["l2", 4 * batch + 3])
                dve.wait_ge(s("l2_mm"), 4 * batch + 4)
                step(V.tensor_scalar(nrow, ps[4][0:8, 0:T], EPS, None, ALU.add))
                V.reciprocal(nrow, nrow).then_inc(s("l2_inv"), 1)
                for i in range(4 * batch, 4 * batch + 4):
                    follow(PLACE["l2b", i])
                    dve.wait_ge(s("l2_bc"), i + 1)
                    V.scalar_tensor_tensor(l2_pair(i), l2_pair(i), QSCALE if i % 4 < 2 else 1.0,
                                           ps[4 + i % 2][:, :].rearrange("p (a t) -> p a t", t=T), ALU.mult, ALU.mult
                                           ).then_inc(s("l2_done"), 1)
                def head_gates(h):
                    b = h % 2
                    follow(PLACE["bc", h])
                    dve.wait_ge(s("bc_mm"), h + 1)
                    if h >= 2:
                        dve.wait_ge(s("a_mm"), h - 1)
                    V.tensor_tensor(kb[:, b, :], proj[:, 8 + h, :], ps[4 + b][:, 0:T], ALU.mult
                                    ).then_inc(s("kb_ready"), 1)
                    for j in range(NJ):
                        ins = V.tensor_scalar(dm[:, b, j * P:(j + 1) * P], ps[4 + b][:, T + j * P:T + (j + 1) * P],
                                              cols[:, j, h:h + 1], 0.0, ALU.subtract, ALU.min)
                    ins.then_inc(s("ddiff"), 1)

                def head_products(h):
                    b = h % 2
                    u = 2 * (h % BH)
                    follow(PLACE["a", h])
                    dve.wait_ge(s("a_mm"), h + 1)
                    dve.wait_ge(s("dmask"), h + 1)
                    d = dm[:, b, :].rearrange("p (j c) -> p j c", j=2)
                    a = ps[6 + b][:, :].rearrange("p (j x c) -> p j x c", j=2, x=2)
                    V.tensor_tensor(ltri[:, u:u + 2, :], a[:, :, 0, :], d, ALU.mult)
                    V.tensor_tensor(qa[:, u:u + 2, :], a[:, :, 1, :], d, ALU.mult)
                    dve.wait_ge(s("eg_ready"), h + 1)
                    V.tensor_tensor(proj[:, h, P:T], proj[:, h, P:T], eg(h), ALU.mult).then_inc(s("qd_ready"), 1)

                def head_tokens(h):
                    follow(PLACE["tok", h])
                    dve.wait_ge(s("tok_mm"), h + 1)
                    tp = ps[6 + h % 2]
                    for j in range(NJ):
                        V.tensor_scalar(proj[:, 16 + h, j * P:(j + 1) * P], tp[:, j * P:(j + 1) * P],
                                        cols[:, 2 + j, h:h + 1], None, ALU.mult)
                    V.tensor_scalar(proj[:, 8 + h, 0:P], tp[:, T:T + P], cols[:, 5, h:h + 1], None, ALU.mult)
                    V.tensor_scalar(proj[:, 8 + h, P:T], tp[:, T + P:2 * T], cols[:, 4, h:h + 1], None, ALU.mult
                                    ).then_inc(s("tok_sb"), 1)

                eye = ident[:, :].rearrange("p (a c) -> p a c", a=1).to_broadcast([P, UNITS, P])
                dve.wait_ge(s("l2_bc"), 4 * batch + 4)
                V.tensor_copy(tmatT[:, :, :], eye)
                for t_ in range(BH + 1):
                    h = BH * batch + t_
                    if t_ < BH:
                        head_gates(h)
                    else:
                        dve.wait_ge(s("qd_ready"), h)
                        V.tensor_copy(tmat[:, :, :], eye).then_inc(s("t_init"), 1)
                    if t_:
                        head_tokens(h - 1)
                    if t_ < BH:
                        head_products(h)
                dve.wait_ge(s("lmask_ready"), LEVELS)
                dve.wait_ge(s("tok_sb"), BH * (batch + 1))
                dve.wait_ge(s("t_init"), batch + 1)
                i0 = 2 * LEVELS * batch

                def level_b(i):
                    lv, g = divmod(i - i0, 2)
                    if i >= 2:
                        dve.wait_ge(s("x_mm"), i - 1)
                    m = lmask[:, lv, :].rearrange("p (a c) -> p a c", a=1).to_broadcast([P, 4, P])
                    V.tensor_tensor(bb[:, g, :, :], ltri[:, 4 * g:4 * g + 4, :], m, ALU.mult).then_inc(s("b_ready"), 1)

                level_b(i0)
                level_b(i0 + 1)
                follow(PLACE["x", i0])
                level_b(i0 + 2)
                for i in range(i0, i0 + 2 * LEVELS):
                    g = i % 2
                    follow(PLACE["y", i])
                    dve.wait_ge(s("y_mm"), i + 1)
                    lv = (i - i0) // 2
                    for side, t_ in enumerate((tmat, tmatT)):
                        if side == 0 and lv == LEVELS - 1:
                            continue
                        v = half_columns(t_[:, 4 * g:4 * g + 4, :], lv, side)
                        y = ps[6 + g][:, side * T:(side + 1) * T].rearrange("p (u a r) -> p u a r", u=4, r=1 << lv)
                        ins = V.tensor_tensor(v, v, y, ALU.subtract)
                    ins.then_inc(s("t_ready"), 1)
                    if i + 3 < i0 + 2 * LEVELS:
                        level_b(i + 3)
                follow(PLACE["u", batch])
                dve.wait_ge(s("u_mm"), batch + 1)
                V.tensor_copy(v_new[0], ps[4][:, :]).then_inc(s("v0_sb"), 1)
                follow(PLACE["v1", batch])
                dve.wait_ge(s("v1_mm"), batch + 1)
                V.tensor_copy(v_new[1], ps[7][:, :]).then_inc(s("v1_sb"), 1)
                follow(PLACE["norm", BH * batch + BH - 1])
                dve.wait_ge(s("on_mm"), BH * (batch + 1))
                step(V.tensor_scalar(nrow, ps[6][0:8, 0:T], 1.0 / P, EPS, ALU.mult, ALU.add))
                V.reciprocal(nrow, nrow).then_inc(s("on_inv"), 1)
                for i in range(2 * batch, 2 * batch + 2):
                    follow(PLACE["normb", i])
                    dve.wait_ge(s("on_bc"), i + 1)
                    dve.wait_ge(s("o_sb"), 2 * i + 2)
                    o = flat_t(proj[:, 2 * i:2 * i + 2, :])
                    V.scalar_tensor_tensor(o, o, hgains[:, 1:2], ps[6 + i % 2][:, :], ALU.mult, ALU.mult
                                           ).then_inc(s("mixd_n"), 1)
                    dve.wait_ge(s("mixd_n"), i + 1)
                    V.tensor_tensor(o, o, flat_t(proj[:, 24 + 2 * i:26 + 2 * i, :]), ALU.mult).then_inc(s("mixd_f"), 1)
            def sb_v(h):
                dve.wait_ge(s("vt_mm"), h + 1)
                if h >= BH:
                    dve.wait_ge(s("av_mm"), h - BH + 1)
                V.tensor_copy(VT[h % BH], ps[7][:, 0:T]).then_inc(s("vt_sb"), 1)

            def sb_softplus(h):
                dve.wait_ge(s("ln_ready"), h + 1)
                V.scalar_tensor_tensor(SP[h % BH], ZB[h % BH][:, 0:384], 0.0, SP[h % BH], ALU.max, ALU.add
                                       ).then_inc(s("sp_ready"), 1)

            def sb_o(h):
                dve.wait_ge(s("av_mm"), h + 1)
                V.tensor_copy(proj[:, 32 + h, :], ps[h % 2][:, 0:T]).then_inc(s("so_sb"), 1)

            follow(SB_PLACE + 5)
            for h in range(EARLY):
                sb_softplus(h)
            follow(16 * IN_GROUPS + 1)
            for h in range(BH):
                sb_v(h)
            for h in range(EARLY, BH):
                sb_softplus(h)
            dve.wait_ge(s("mixd_hi"), 1)
            V.tensor_tensor(xhl[:, 0:HEADS, 1, :], proj[:, 0:HEADS, :],
                            xhl[:, 0:HEADS, 0, :].bitcast(f32), ALU.subtract).then_inc(s("mix_lo"), 1)
            for h in range(BH):
                sb_o(h)
                sb_v(BH + h)
            for h in range(BH, HEADS):
                sb_softplus(h)
            for h in range(BH, HEADS):
                sb_o(h)
            dve.wait_ge(s("son_mm"), HEADS)
            step(V.tensor_scalar(nrow, ps[2][0:8, 0:T], 1.0 / P, EPS, ALU.mult, ALU.add))
            V.reciprocal(nrow, nrow).then_inc(s("son_inv"), 1)
            for i in range(HEADS // 2 + 1):
                if i < HEADS // 2:
                    dve.wait_ge(s("son_bc"), i + 1)
                    dve.wait_ge(s("so_sb"), HEADS)
                    o = flat_t(proj[:, 32 + 2 * i:34 + 2 * i, :])
                    V.scalar_tensor_tensor(o, o, hgains[:, 0:1], ps[4 + i][:, :], ALU.mult, ALU.mult
                                           ).then_inc(s("mixs_f"), 1)
                if i:
                    dve.wait_ge(s("mixs_hi"), i)
                    k = slice(HEADS + 2 * i - 2, HEADS + 2 * i)
                    V.tensor_tensor(xhl[:, k, 1, :], proj[:, 30 + 2 * i:32 + 2 * i, :],
                                    xhl[:, k, 0, :].bitcast(f32), ALU.subtract).then_inc(s("mix_lo"), 1)

            with dve.Fori(IN_GROUPS, IN_GROUPS + OUT_GROUPS) as g:
                for r in range(13):
                    split(g, AHEAD + r)
                for j in range(GROUP):
                    if j:
                        split(g, AHEAD + 12 + j)
                    dve.wait_ge(half_ready, g * 4 + (j + 1))
                    V.tensor_tensor(mixo[:, bass.ds(g * 4 + (j - 4 * IN_GROUPS), 1), :].rearrange("p a t -> p (a t)"),
                                    ps[j][:, 0:T], halfs[j % 4], ALU.add).then_inc(bank_free, 1)

            def inverse(row, mm, name, bank):
                dve.wait_ge(s(mm), 1)
                step(V.tensor_scalar(row, ps[bank][:, 0:T], 1.0 / D, EPS, ALU.mult, ALU.add))
                V.reciprocal(row, row).then_inc(s(name), 1)

            def residual(src, name, q, ready):
                dve.wait_ge(s(f"{name}_gain"), 4 * q + 4)
                v = src[:, 4 * q:4 * q + 4, :]
                each = rstd[:, :].rearrange("p (a t) -> p a t", a=1).to_broadcast([P, 4, T])
                step(V.tensor_tensor(v, v, each, ALU.mult))
                r_ = res[:, 4 * q:4 * q + 4, :]
                V.tensor_tensor(r_, r_, v, ALU.add).then_inc(s(ready), 1)

            UG = IN_GROUPS + OUT_GROUPS
            inverse(vrow[:, :], "m_sum", "m_inv", 4)
            dve.wait_ge(s("m_rstd"), 1)
            for q in range(4):
                residual(mixo, "m", q, "h_ready")
            for r in range(8):
                split(UG, AHEAD + r)
            dve.wait_ge(s("h_sq"), 4)
            V.tensor_reduce(ssum[:, :], hsq.rearrange("p k t -> p t k"), mybir.AxisListType.X, ALU.add
                            ).then_inc(s("h_ss"), 1)
            for r in range(8, 13):
                split(UG, AHEAD + r)
            dve.wait_ge(s("fhist_ready"), 1)
            for q in range(GROUP):
                if q:
                    split(UG, AHEAD + 12 + q)
                added_up = (UG * 4 + q, q, q, fhist[:, q, 2:2 + T])
                if q < GROUP - 1:
                    added(*added_up)
            inverse(token_scale[:, :], "h_sum", "h_inv", 4)
            added(*added_up)
            UC = IN_CHUNKS + OUT_CHUNKS

            def ffn_conv(i, part, q):
                b = 2 * part + q % 2
                if part == 0:
                    dve.wait_ge(s("gelu_done"), i * 4 + (q + 1))
                else:
                    dve.wait_ge(s("prod_ready"), i * 4 + (q + 3))
                dve.wait_ge(s("up_scaled"), i * 8 + (4 * part + q + 1))
                col = bass.ds(i * 4 + (part * FT + q), 1)
                for k in range(3):
                    src = fhist[:, q, k:k + T]
                    if k == 0:
                        ins = V.tensor_scalar(fconv[:, b, :], src, fcw[:, 0, col], fcb[:, col], ALU.mult, ALU.add)
                    else:
                        dve.wait_ge(s("fconv_step"), i * 24 + (12 * part + 3 * q + k))
                        ins = V.scalar_tensor_tensor(fconv[:, b, :], src, fcw[:, k, col], fconv[:, b, :],
                                                     ALU.mult, ALU.add)
                    ins.then_inc(s("fconv_step"), 1)

            def value_tile(i, q):
                ffn_conv(i, 1, q)
                dve.wait_ge(s("fconv_step"), i * 24 + (12 + 3 * q + 3))
                dve.wait_ge(s("gelu_done"), i * 4 + (q + 3))
                dve.wait_ge(s("act_lo"), i * 4 + (q + 1))
                V.tensor_tensor(prod[:, q % 2, :], gelu[:, q, :], fconv[:, 2 + q % 2, :], ALU.mult
                                ).then_inc(s("prod_ready"), 1)

            def up_group(g, work, steps):
                for q in range(GROUP):
                    for r in range(3 * q, 3 * q + 3):
                        split(g, AHEAD + r)
                    work(q)
                split(g, AHEAD + 12)
                if steps is not None:
                    dve.wait_ge(s("fconv_step"), steps)
                for q in range(GROUP):
                    if q:
                        split(g, AHEAD + 12 + q)
                    added(g * 4 + q, q, q, fhist[:, q, 2:2 + T])

            V.memset(mark[:, 0:1], 0.0).then_inc(s("gelu_done"), 2)
            V.memset(mark[:, 1:2], 0.0).then_inc(s("prod_ready"), 4)
            V.memset(mark[:, 2:3], 0.0).then_inc(s("act_lo"), 2)
            with dve.Fori(0, UP_STEPS - 1) as i:
                up_group(i * 2 + (UC // 4 + 1), lambda q: ffn_conv(i, 0, q), i * 24 + 12)
                up_group(i * 2 + (UC // 4 + 2), lambda q: value_tile(i, q), i * 24 + 24)
            up_group(UC // 4 + 2 * UP_STEPS - 1, lambda q: ffn_conv(UP_STEPS - 1, 0, q), (UP_STEPS - 1) * 24 + 12)
            DC = UC + UP_CHUNKS
            for q in range(GROUP):
                for r in range(3 * q, 3 * q + 3):
                    split(DC // 4, AHEAD + r)
                value_tile(UP_STEPS - 1, q)
            for hf in range(2):
                c = DC + hf * HALF_CHUNKS
                p0 = 4 * c + AHEAD + (12 if hf == 0 else 0)
                p1 = min(4 * (c + HALF_CHUNKS) + AHEAD, 4 * CHUNKS)
                p2 = min((p0 + 15) // 16 * 16, p1)
                for p in range(p0, p2):
                    split(p // 16, p % 16)
                with dve.Fori(p2 // 16, p1 // 16) as r:
                    for i in range(16):
                        split(r, i)
                for p in range(p1 // 16 * 16, p1):
                    split(p // 16, p % 16)
                for j in range(DOWN_TILES):
                    t_ = hf * DOWN_TILES + j
                    added(DC + t_, j, j, down[:, t_, :])
            inverse(vrow[:, :], "f_sum", "f_inv", 0)
            dve.wait_ge(s("f_rstd"), 1)
            for q in range(4):
                residual(down, "f", q, "y_ready")

        @block.tensor
        def _(pe):
            M = nc.tensor.matmul

            def tile_piece(g, r):
                q, j = divmod(r, GROUP)
                pe.wait_ge(lo_ready, g * 16 + (r + 1))
                if q == 0:
                    pe.wait_ge(bank_free, g * 4 + (j + 1))
                for kk in range(CHUNK_K):
                    k = CHUNK_K * q + kk
                    w = slice(kk * P, (kk + 1) * P)
                    M(ps[j][:, :], w_hi[:, r % RING, w], xhl[:, k, :, :].rearrange("p a t -> p (a t)"),
                      start=(k == 0), stop=False, skip_group_check=True)
                    last = M(ps[j][:, 0:T], w_lo[:, r % RING, w], xhl[:, k, 0, :],
                             start=False, stop=(k == KT - 1), skip_group_check=True)
                last.then_inc(piece_used, 1)

            def group(g):
                for r in range(16):
                    tile_piece(g, r)

            pe.wait_ge(const_ready, 2)
            at = [0]

            def follow(place):
                while at[0] < min(place, 16 * IN_GROUPS):
                    g, r = divmod(at[0], 16)
                    at[0] += 1
                    if g == 0 and r % 4 == 0:
                        pe.wait_ge(s("xn_lo"), r + 4)
                    tile_piece(g, r)

            def x_mm(i):
                lv, g = divmod(i % (2 * LEVELS), 2)
                follow(PLACE["x", i])
                pe.wait_ge(s("b_ready"), i + 1)
                if lv:
                    pe.wait_ge(s("t_ready"), i - 1)
                if i >= 2:
                    pe.wait_ge(s("x_sb"), i - 1)
                for u in range(4):
                    last = M(ps[4 + g][:, u * P:(u + 1) * P], bb[:, g, u, :], tmat[:, 4 * g + u, :],
                             start=True, stop=True)
                last.then_inc(s("x_mm"), 1)

            def norm_mm(h):
                follow(PLACE["norm", h])
                pe.wait_ge(s("o_sq"), h + 1)
                M(ps[6][0:8, 0:T], esel[:, h, :], osb[:, h % 4, :], start=(h % BH == 0), stop=(h % BH == BH - 1)
                  ).then_inc(s("on_mm"), 1)

            follow(11)
            pe.wait_ge(s("x_ss"), NJ)
            M(ps[4][:, 0:T], ones[:, :], ssum[:, :], start=True, stop=True).then_inc(s("xsum_mm"), 1)
            follow(12)
            pe.wait_ge(small_in, 16 * 6)
            for k in range(KT):
                last = M(ps[5][0:40, 0:T], wba[:, k, :], full[:, k, :], start=(k == 0), stop=(k == KT - 1))
            last.then_inc(s("ba_done"), 1)
            follow(40)
            pe.wait_ge(s("bg_row"), 1)
            pe.wait_ge(s("ke_row"), 1)
            for n_, (r, j) in enumerate(((1, 0), (1, 1), (0, 0), (0, 1), (2, 1), (3, 0))):
                last = nc.tensor.transpose(ps[6][:, 8 * n_:8 * n_ + 8], rows[:, r, j * P:(j + 1) * P], ident[0:8, 0:8])
            last.then_inc(s("cols_mm"), 1)
            pe.wait_ge(s("ga"), 2)
            pe.wait_ge(s("sel_ready"), 2)
            for b_ in range(BATCHES):
                heads = range(BH * b_, BH * b_ + BH)
                i0 = 2 * LEVELS * b_
                for i in range(4 * b_, 4 * b_ + 4):
                    follow(PLACE["l2", i])
                    pe.wait_ge(s("qk_sq"), i + 1)
                    if b_:
                        pe.wait_ge(s("o_sb"), BH)
                    for a in range(2):
                        last = M(ps[4][0:8, 0:T], esel[:, 2 * (i % 4) + a, :], l2_squares(i)[:, a * T:(a + 1) * T],
                                 start=(i % 4 == 0 and a == 0), stop=(i % 4 == 3 and a == 1))
                    last.then_inc(s("l2_mm"), 1)
                for i in range(4 * b_, 4 * b_ + 4):
                    follow(PLACE["l2b", i])
                    pe.wait_ge(s("l2_rstd"), b_ + 1)
                    if i % 4 >= 2:
                        pe.wait_ge(s("l2_done"), i - 1)
                    for a in range(2):
                        last = M(ps[4 + i % 2][:, a * T:(a + 1) * T], sel[:, 2 * (i % 4) + a, :], nrow,
                                 start=True, stop=True)
                    last.then_inc(s("l2_bc"), 1)
                pe.wait_ge(s("cols_sb"), 1)
                def head_gates(h):
                    follow(PLACE["bc", h])
                    pe.wait_ge(s("l2_done"), 4 * b_ + 4)
                    if h >= 2:
                        pe.wait_ge(s("ddiff"), h - 1)
                        pe.wait_ge(s("eg_ready"), h - 1)
                    M(ps[4 + h % 2][:, :], sel[:, h, :], rows[:, 0:2, :].rearrange("p r t -> p (r t)"),
                      start=True, stop=True).then_inc(s("bc_mm"), 1)

                def head_products(h):
                    bank = ps[6 + h % 2]
                    follow(PLACE["a", h])
                    pe.wait_ge(s("kb_ready"), h + 1)
                    if h >= 2:
                        pe.wait_ge(s("tok_sb"), h - 1)
                    if b_:
                        pe.wait_ge(s("mixd_n"), BH // 2)
                    for j in range(NJ):
                        cs = slice(j * P, (j + 1) * P)
                        M(bank[:, j * T:j * T + P], proj[:, 8 + h, cs], kb[:, h % 2, cs], start=True, stop=True)
                        last = M(bank[:, j * T + P:(j + 1) * T], proj[:, 8 + h, cs], proj[:, h, cs],
                                 start=True, stop=True)
                    last.then_inc(s("a_mm"), 1)

                def head_tokens(h):
                    follow(PLACE["tok", h])
                    pe.wait_ge(s("qd_ready"), h + 1)
                    pe.wait_ge(s("silu_done"), 4 * b_ + 3)
                    for x_, t_ in ((0, 16 + h), (1, 8 + h)):
                        for j in range(NJ):
                            last = nc.tensor.transpose(ps[6 + h % 2][:, (2 * x_ + j) * P:(2 * x_ + j + 1) * P],
                                                       proj[:, t_, j * P:(j + 1) * P], ident[:, :])
                    last.then_inc(s("tok_mm"), 1)

                for t_ in range(BH + 1):
                    h = BH * b_ + t_
                    if t_ < BH:
                        head_gates(h)
                    if t_:
                        head_tokens(h - 1)
                    if t_ < BH:
                        head_products(h)
                follow(PLACE["x", i0])
                pe.wait_ge(s("t_init"), b_ + 1)
                pe.wait_ge(s("tok_sb"), BH * (b_ + 1))

                x_mm(i0)
                for i in range(i0, i0 + 2 * LEVELS):
                    g = i % 2
                    if i + 1 < i0 + 2 * LEVELS:
                        x_mm(i + 1)
                    follow(PLACE["y", i])
                    pe.wait_ge(s("x_sb"), i + 1)
                    lv = (i - i0) // 2
                    for u in range(4):
                        c = slice(u * HALF, (u + 1) * HALF)
                        if lv < LEVELS - 1:
                            M(ps[6 + g][:, 0:T][:, c].rearrange("p (a r) -> p a r", r=1 << lv), tmatT[:, 4 * g + u, :],
                              half_columns(xb[:, g, u, :], lv, 0), start=True, stop=True)
                        last = M(ps[6 + g][:, T:2 * T][:, c].rearrange("p (a r) -> p a r", r=1 << lv), xb[:, g, u, :],
                                 half_columns(tmatT[:, 4 * g + u, :], lv, 1), start=True, stop=True)
                    last.then_inc(s("y_mm"), 1)
                follow(PLACE["u", b_])
                pe.wait_ge(s("t_ready"), i0 + 2 * LEVELS)
                for i, h in enumerate(heads):
                    c = slice(i * P, (i + 1) * P)
                    last = M(ps[4][:, c], tmatT[:, 2 * i, :], proj[:, 16 + h, 0:P], start=True, stop=True)
                last.then_inc(s("u_mm"), 1)
                follow(PLACE["w", b_])
                for i, h in enumerate(heads):
                    c = slice(i * P, (i + 1) * P)
                    last = M(ps[5][:, c], proj[:, 8 + h, P:T], tmatT[:, 2 * i + 1, :], start=True, stop=True)
                last.then_inc(s("w_mm"), 1)
                follow(PLACE["s", b_])
                pe.wait_ge(s("v0_sb"), b_ + 1)
                for i, h in enumerate(heads):
                    c = slice(i * P, (i + 1) * P)
                    last = M(ps[6][:, c], proj[:, 8 + h, 0:P], v_new[0][:, c], start=True, stop=True)
                last.then_inc(s("s_mm"), 1)
                follow(PLACE["v1", b_])
                pe.wait_ge(s("w_sb"), b_ + 1)
                pe.wait_ge(s("s_sb"), b_ + 1)
                for i, h in enumerate(heads):
                    c = slice(i * P, (i + 1) * P)
                    M(ps[7][:, c], tmatT[:, 2 * i + 1, :], proj[:, 16 + h, P:T], start=True, stop=False)
                    last = M(ps[7][:, c], neg_w[:, c], state[:, c], start=False, stop=True)
                last.then_inc(s("v1_mm"), 1)
                follow(PLACE["o", BH * b_])
                pe.wait_ge(s("v1_sb"), b_ + 1)
                for i, h in enumerate(heads):
                    c = slice(i * P, (i + 1) * P)
                    follow(PLACE["o", h])
                    if i >= 2:
                        pe.wait_ge(s("o_sb"), h - 1)
                    bank = ps[4 + h % 2]
                    M(bank[:, 0:P], v_new[0][:, c], qa[:, 2 * i, :], start=True, stop=True)
                    M(bank[:, P:T], state[:, c], proj[:, h, P:T], start=True, stop=False)
                    M(bank[:, P:T], v_new[1][:, c], qa[:, 2 * i + 1, :], start=False, stop=True
                      ).then_inc(s("o_mm"), 1)
                    if i:
                        norm_mm(h - 1)
                norm_mm(BH * b_ + BH - 1)
                for i in range(2 * b_, 2 * b_ + 2):
                    follow(PLACE["normb", i])
                    pe.wait_ge(s("on_rstd"), b_ + 1)
                    for a in range(2):
                        last = M(ps[6 + i % 2][:, a * T:(a + 1) * T], sel[:, 2 * i + a, :], nrow, start=True, stop=True)
                    last.then_inc(s("on_bc"), 1)
            def sb_z(h):
                zb = ZB[h % BH]
                if h >= BH:
                    pe.wait_ge(s("att_exp"), h - BH + 1)
                M(zb[:, 0:T], proj[:, 40 + h, 0:P], proj[:, 32 + h, :], start=True, stop=False, skip_group_check=True)
                M(zb[:, T:T + P], proj[:, 40 + h, P:T], proj[:, 32 + h, P:T], start=False, stop=True,
                  skip_group_check=True).then_inc(s("z_mm"), 1)

            def sb_v(h):
                if h:
                    pe.wait_ge(s("vt_sb"), h)
                for j in range(NJ):
                    last = nc.tensor.transpose(ps[7][:, j * P:(j + 1) * P], proj[:, 48 + h, j * P:(j + 1) * P],
                                               ident[:, :])
                last.then_inc(s("vt_mm"), 1)

            def sb_c(h):
                zb, sp_ = ZB[h % BH], SP[h % BH]
                pe.wait_ge(s("sp_mask"), h + 1)
                tri, neg1 = xb[:, 0, 0, :], xb[:, 0, 1, :]
                M(zb[:, 0:T], tri, sp_[:, 0:T], start=False, stop=False, skip_group_check=True)
                M(zb[:, P:T], neg1, sp_[:, T:T + P], start=False, stop=False, skip_group_check=True)
                M(zb[:, T:T + P], tri, sp_[:, T:T + P], start=False, stop=True, skip_group_check=True
                  ).then_inc(s("c_mm"), 1)

            def sb_av(h):
                pe.wait_ge(s("att_mask"), h + 1)
                pe.wait_ge(s("vt_sb"), h + 1)
                if h >= 2:
                    pe.wait_ge(s("so_sb"), h - 1)
                ob, v, at_ = ps[h % 2], VT[h % BH], AT[h % BH]
                M(ob[:, 0:P], v[:, 0:P], at_[:, 0:P], start=True, stop=True)
                M(ob[:, P:T], v[:, 0:P], at_[:, P:T], start=True, stop=False)
                M(ob[:, P:T], v[:, P:T], at_[:, T:T + P], start=False, stop=True).then_inc(s("av_mm"), 1)

            def sb_sum(h):
                pe.wait_ge(s("so_sq"), h + 1)
                M(ps[2][0:8, 0:T], esel[:, h, :], osb[:, h % 4, :], start=(h == 0), stop=(h == HEADS - 1)
                  ).then_inc(s("son_mm"), 1)

            follow(SB_PLACE)
            pe.wait_ge(s("sbq"), HEADS)
            pe.wait_ge(s("scaled"), 4 * (8 + 2 * HEADS // GROUP))
            pe.wait_ge(s("o_sb"), HEADS)
            pe.wait_ge(s("mixd_n"), HEADS // 2)
            for h in range(EARLY):
                sb_z(h)
            follow(16 * IN_GROUPS)
            pe.wait_ge(s("scaled"), 4 * IN_GROUPS)
            for h in range(EARLY, BH):
                sb_z(h)
            pe.wait_ge(s("tri_ready"), 2)
            for h in range(BH):
                sb_v(h)
            for h in range(BH):
                sb_c(h)
            for h in range(BH):
                sb_z(BH + h)
            for h in range(BH):
                sb_av(h)
                sb_v(BH + h)
            for h in range(BH, HEADS):
                sb_c(h)
            for h in range(BH):
                sb_sum(h)
            for h in range(BH, HEADS):
                sb_av(h)
                if h > BH:
                    sb_sum(h - 1)
            sb_sum(HEADS - 1)
            pe.wait_ge(s("att_exp"), HEADS)
            pe.wait_ge(s("so_sb"), HEADS)
            pe.wait_ge(s("son_inv"), 1)
            pe.wait_ge(s("mix_lo"), 1)
            for r in range(2):
                tile_piece(IN_GROUPS, r)
            for i in range(HEADS // 2):
                pe.wait_ge(s("son_rstd"), 1)
                for a in range(2):
                    last = M(ps[4 + i][:, a * T:(a + 1) * T], sel[:, 2 * i + a, :], nrow, start=True, stop=True)
                last.then_inc(s("son_bc"), 1)

            for r in range(2, 16):
                if r >= 8 and r % 4 == 0:
                    pe.wait_ge(s("mix_lo"), 1 + 2 * (r // 4 - 1))
                tile_piece(IN_GROUPS, r)
            with pe.Fori(IN_GROUPS + 1, IN_GROUPS + OUT_GROUPS) as g:
                group(g)
            pe.wait_ge(s("m_add"), KT - 1)
            M(ps[4][:, 0:T], ones[:, :], ssum[:, :], start=True, stop=True).then_inc(s("m_sum"), 1)
            UC = IN_CHUNKS + OUT_CHUNKS
            for r in range(16):
                if r % 4 == 0:
                    pe.wait_ge(s("hn_lo"), r + 4)
                if r == 12:
                    pe.wait_ge(s("h_ss"), 1)
                    M(ps[4][:, 0:T], ones[:, :], ssum[:, :], start=True, stop=True).then_inc(s("h_sum"), 1)
                tile_piece(UC // 4, r)
            with pe.Fori(UC // 4 + 1, UC // 4 + 2 * UP_STEPS) as g:
                group(g)
            DC = UC + UP_CHUNKS
            pe.wait_ge(s("act_lo"), FT - 4 + 2)

            def down_chunk(c, k, slot, first, lastc, hf):
                for j in range(DOWN_TILES):
                    piece, part = j // 2, j % 2
                    if part == 0:
                        pe.wait_ge(lo_ready, c * 4 + (piece + 1))
                    if first and (hf or j < 4):
                        pe.wait_ge(bank_free, (DC + j + 1) if hf == 0 else (DC + j + 5))
                    for kk in range(DOWN_K):
                        w = slice((DOWN_K * part + kk) * P, (DOWN_K * part + kk + 1) * P)
                        xk = act[:, k + kk, :, :] if isinstance(k, int) else \
                            act[:, bass.ds(k + kk, 1), :, :].rearrange("p o a t -> p (o a) t")
                        M(ps[j][:, :], w_hi[:, 4 * slot + piece, w], xk.rearrange("p a t -> p (a t)"),
                          start=(first and kk == 0), stop=False, skip_group_check=True)
                        last = M(ps[j][:, 0:T], w_lo[:, 4 * slot + piece, w], xk[:, 0, :], start=False,
                                 stop=(lastc and kk == DOWN_K - 1), skip_group_check=True)
                    if part == 1:
                        last.then_inc(piece_used, 1)

            for hf in range(2):
                c = DC + hf * HALF_CHUNKS
                for k in range(2):
                    down_chunk(c + k, 2 * k, (c + k) % 2, k == 0, False, hf)
                with pe.Fori(1, HALF_CHUNKS // 2 - 1) as r:
                    for k in range(2):
                        down_chunk(r * 2 + (c + k), r * 4 + 2 * k, (c + k) % 2, False, False, hf)
                pe.wait_ge(s("act_lo"), FT + 2)
                for k in range(HALF_CHUNKS - 2, HALF_CHUNKS):
                    down_chunk(c + k, 2 * k, (c + k) % 2, False, k == HALF_CHUNKS - 1, hf)
            pe.wait_ge(s("f_add"), KT - 1)
            M(ps[0][:, 0:T], ones[:, :], ssum[:, :], start=True, stop=True).then_inc(s("f_sum"), 1)




def weight_chunks(w_in, w_out, w_up, w_down):
    def by_columns(w):
        k, n = w.shape
        return w.reshape(k // (CHUNK_K * P), CHUNK_K, P, n // 512, 4, P).transpose(3, 0, 2, 4, 1, 5
                                                                                  ).reshape(-1, P, CHUNK)

    sb3, width = 3 * HEADS * P, BH * P
    dn = w_in[:, sb3:].reshape(-1, 4, BATCHES, width).transpose(0, 2, 1, 3).reshape(w_in.shape[0], -1)
    w_in = np.concatenate([dn, w_in[:, 0:sb3]], axis=1)
    up = by_columns(w_up).reshape(2, UP_STEPS, 4, P, CHUNK).transpose(1, 0, 2, 3, 4).reshape(-1, P, CHUNK)
    dn = w_down.reshape(HALF_CHUNKS, DOWN_K, P, 2, DOWN_TILES, P).transpose(3, 0, 2, 4, 1, 5).reshape(-1, P, CHUNK)
    w_out = np.concatenate([w_out[HEADS * P:], w_out[:HEADS * P]], axis=0)
    return np.concatenate([by_columns(w_in), by_columns(w_out), up, dn], axis=0)


def kernel(**inputs):
    import numpy as _np
    import concourse.bacc as _bacc
    from concourse import mybir as _mybir
    from concourse.bass_utils import run_bass_kernel_spmd as _run

    a = {k: _np.asarray(v) for k, v in inputs.items()}
    w_in = a["w_in"][0]
    proj_cols = 7 * HEADS * P
    tiles = lambda v: v.reshape(-1, P).T
    w_ba = _np.zeros((P, KT, 40), w_in.dtype)
    ba = w_in[:, proj_cols:].reshape(KT, P, 2, 8).transpose(1, 0, 2, 3)
    w_ba[:, :, 0:8], w_ba[:, :, 32:40] = ba[:, :, 0], ba[:, :, 1]
    arrays = {
        "x": a["x"][0].reshape(T, KT, P).transpose(2, 1, 0),
        "wts": weight_chunks(w_in[:, :proj_cols], a["w_out"][0], a["w_up"][0], a["w_down"][0]),
        "w_ba": w_ba,
        "norm_gains": _np.stack([tiles(a[n][0]) for n in ("ln_mix_pre", "ln_mix_post", "ln_ffn_pre", "ln_ffn_post")],
                                axis=1),
        "head_gains": _np.stack([a["sb_out_gain"][0], a["dn_out_gain"][0]], axis=1),
        "dn_conv": a["dn_conv_w"][0].reshape(4, 24, P).transpose(2, 0, 1),
        "dn_gate": _np.stack([a["dn_a_log"][0], a["dn_dt_bias"][0]], axis=1),
        "ffn_cw": a["ffn_conv_w"][0].reshape(3, 2 * FT, P).transpose(2, 0, 1),
        "ffn_cb": tiles(a["ffn_conv_b"][0]),
    }
    nc = _bacc.Bacc("TRN2", target_bir_lowering=False, num_devices=1, dynamic_dma_scratch_size=64)
    feed, args = {}, []
    for name, v in arrays.items():
        v = _np.ascontiguousarray(v)
        feed[f"in_{name}"] = v
        args.append(nc.dram_tensor(f"in_{name}", v.shape, _mybir.dt.from_np(v.dtype), kind="ExternalInput").ap())
    out = nc.dram_tensor("out_y", (P, KT, T), _mybir.dt.float32, kind="ExternalOutput").ap()
    hybrid_block_kernel(nc, *args, out)
    r = _run(nc, [feed], core_ids=[0])
    y = r.results[0]["out_y"]
    return _np.ascontiguousarray(y.transpose(2, 1, 0).reshape(1, T, D))
```
